# Optimizing a Trainium2 kernel written in Bass

```python
import jax
import jax.numpy as jnp
from jax import lax
import numpy as np

D_MODEL = 1024
BATCH = 1
SEQ = 256
DEPTH = 1
DEC_BATCH = 8
DEC_SEQ = 4
PAST_LEN = 2048
PAGE_SIZE = 128

N_META = 16
CHUNK = 64
EPS = 1e-6
H_A = 8
DK_A = 128
DV_A = 128
CONV_W = 4
CONV_CH = 2 * H_A * DK_A + H_A * DV_A
H_B = 4
DK_B = 128
DV_B = 256
GATE_RANK = 16
GATE_TAU = 16.0
N_GROUPS = 4
EXPERTS_PER_GROUP = 8
N_EXPERTS = N_GROUPS * EXPERTS_PER_GROUP
TOP_K_FINE = 2
D_FF_E = 256
COL_SIZES = (CONV_CH, H_A * DV_A, H_A, H_A, H_B * DK_B, H_B * DK_B, H_B * DV_B, H_B * DV_B, GATE_RANK, D_MODEL, D_MODEL)
IN_COLS = sum(COL_SIZES)

kernel_name = 'hybrid_gdn_gla_hmoe_step'

F32 = jnp.float32

def rmsnorm(x, w):
    x32 = x.astype(F32)
    y = x32 * lax.rsqrt(jnp.mean(x32 * x32, axis=-1, keepdims=True) + EPS)
    return (y * w.astype(F32)).astype(x.dtype)

def l2norm(x):
    return x * lax.rsqrt(jnp.sum(x * x, axis=-1, keepdims=True) + EPS)

def split_cols(p):
    offs = []
    s = 0
    for c in COL_SIZES[:-1]:
        s += c
        offs.append(s)
    return jnp.split(p, offs, axis=-1)

def to_chunks(a, L):
    B, T = a.shape[:2]
    a = a.reshape(B, T // L, L, *a.shape[2:])
    return jnp.swapaxes(jnp.moveaxis(a, 1, 0), 2, 3)

def from_chunks(o):
    o = jnp.moveaxis(jnp.swapaxes(o, 2, 3), 0, 1)
    return o.reshape(o.shape[0], o.shape[1] * o.shape[2], *o.shape[3:])

def gdn_chunk(S, inp):
    q, k, v, g, beta = inp
    L = q.shape[-2]
    incl = jnp.tril(jnp.ones((L, L), bool))
    strict = jnp.tril(jnp.ones((L, L), bool), -1)
    G = jnp.cumsum(g, axis=-1)
    diff = G[..., :, None] - G[..., None, :]
    dec_incl = jnp.exp(jnp.where(incl, diff, -jnp.inf))
    dec_strict = jnp.where(strict, dec_incl, 0.0)
    A = beta[..., :, None] * jnp.einsum('bhtd,bhjd->bhtj', k, k) * dec_strict
    M = A + jnp.eye(L, dtype=F32)
    rhs = jnp.concatenate([beta[..., None] * v, (beta * jnp.exp(G))[..., None] * k], axis=-1)
    sol = lax.linalg.triangular_solve(M, rhs, left_side=True, lower=True, unit_diagonal=True)
    dv = v.shape[-1]
    value, kcd = sol[..., :dv], sol[..., dv:]
    v_new = value - jnp.einsum('bhld,bhdv->bhlv', kcd, S)
    qk = jnp.einsum('bhtd,bhjd->bhtj', q, k) * dec_incl
    o = jnp.einsum('bhld,bhdv->bhlv', q * jnp.exp(G)[..., None], S) + jnp.einsum('bhtj,bhjv->bhtv', qk, v_new)
    GL = G[..., -1:]
    S_new = S * jnp.exp(GL)[..., None] + jnp.einsum('bhjd,bhjv->bhdv', k * jnp.exp(GL - G)[..., None], v_new)
    return S_new, o

def gla_chunk(S, inp):
    q, k, v, lg = inp
    L = q.shape[-2]
    incl = jnp.tril(jnp.ones((L, L), bool))
    Bc = jnp.cumsum(lg, axis=-2)
    diff = Bc[..., :, None, :] - Bc[..., None, :, :]
    D = jnp.exp(jnp.where(incl[..., None], diff, -jnp.inf))
    A = jnp.einsum('bhtc,bhjc,bhtjc->bhtj', q, k, D)
    o = jnp.einsum('bhtc,bhcv->bhtv', q * jnp.exp(Bc), S) + jnp.einsum('bhtj,bhjv->bhtv', A, v)
    BL = Bc[..., -1:, :]
    S_new = S * jnp.swapaxes(jnp.exp(BL), -1, -2) + jnp.einsum('bhjc,bhjv->bhcv', k * jnp.exp(BL - Bc), v)
    return S_new, o

def run_chunked(body, S0, seqs, segments):
    S = S0
    outs = []
    for start, length, L in segments:
        parts = tuple(to_chunks(a[:, start:start + length], L) for a in seqs)
        S, o = lax.scan(body, S, parts)
        outs.append(from_chunks(o))
    return jnp.concatenate(outs, axis=1), S

def mixer(h, conv_buf, S_a, S_b, segments, w_in, conv_w, a_log, dt_bias, norm_a,
          gla_gate_up, gla_gate_bias, norm_b, w_proj_a, w_proj_b, w_out):
    B, T, _ = h.shape
    p = jnp.einsum('btd,dc->btc', h, w_in).astype(F32)
    qkv, z, b_a, a_a, q_b, k_b, v_b, r_b, lr, g_a, g_b = split_cols(p)
    xc = jnp.concatenate([conv_buf.astype(F32), qkv], axis=1)
    cw = conv_w.astype(F32)
    conv = cw[0] * xc[:, 0:T]
    for i in range(1, CONV_W):
        conv = conv + cw[i] * xc[:, i:i + T]
    new_buf = xc[:, T:]
    qkv = jax.nn.silu(conv)
    q_a, k_a, v_a = jnp.split(qkv, [H_A * DK_A, 2 * H_A * DK_A], axis=-1)
    q_a = l2norm(q_a.reshape(B, T, H_A, DK_A)) * (DK_A ** -0.5)
    k_a = l2norm(k_a.reshape(B, T, H_A, DK_A))
    v_a = v_a.reshape(B, T, H_A, DV_A)
    beta = jax.nn.sigmoid(b_a)
    g = -jnp.exp(a_log.astype(F32)) * jax.nn.softplus(a_a + dt_bias.astype(F32))
    o_a, S_a_new = run_chunked(gdn_chunk, S_a.astype(F32), (q_a, k_a, v_a, g, beta), segments)
    o_a = rmsnorm(o_a, norm_a) * jax.nn.silu(z.reshape(B, T, H_A, DV_A))
    y_a = jnp.einsum('btc,cd->btd', o_a.reshape(B, T, H_A * DV_A), w_proj_a.astype(F32))
    lg = jax.nn.log_sigmoid(jnp.einsum('btr,rc->btc', lr, gla_gate_up.astype(F32)) + gla_gate_bias.astype(F32)) / GATE_TAU
    lg = lg.reshape(B, T, H_B, DK_B)
    q_b = q_b.reshape(B, T, H_B, DK_B) * (DK_B ** -0.5)
    k_b = k_b.reshape(B, T, H_B, DK_B)
    v_b = v_b.reshape(B, T, H_B, DV_B)
    o_b, S_b_new = run_chunked(gla_chunk, S_b.astype(F32), (q_b, k_b, v_b, lg), segments)
    o_b = rmsnorm(o_b, norm_b) * jax.nn.silu(r_b.reshape(B, T, H_B, DV_B))
    y_b = jnp.einsum('btc,cd->btd', o_b.reshape(B, T, H_B * DV_B), w_proj_b.astype(F32))
    merged = jax.nn.sigmoid(g_a) * y_a + jax.nn.sigmoid(g_b) * y_b
    out = jnp.einsum('btd,de->bte', merged, w_out.astype(F32)).astype(h.dtype)
    return out, new_buf, S_a_new, S_b_new

def hier_moe(h, w_rg, b_rg, w_re, b_re, w_gate, w_up, w_down):
    B, T, D = h.shape
    x = h.reshape(B * T, D)
    lg = jnp.einsum('nd,dg->ng', x, w_rg).astype(F32) + b_rg.astype(F32)
    pg = jax.nn.softmax(lg, axis=-1)
    gsel = jnp.argmax(lg, axis=-1)
    pgsel = jnp.max(pg, axis=-1, keepdims=True)
    le = (jnp.einsum('nd,de->ne', x, w_re).astype(F32) + b_re.astype(F32)).reshape(-1, N_GROUPS, EXPERTS_PER_GROUP)
    le = jnp.einsum('ngk,ng->nk', le, jax.nn.one_hot(gsel, N_GROUPS, dtype=F32))
    pe = jax.nn.softmax(le, axis=-1)
    top_v, top_i = lax.top_k(pe, TOP_K_FINE)
    w_sel = pgsel * top_v / jnp.sum(top_v, axis=-1, keepdims=True)
    eid = gsel[:, None] * EXPERTS_PER_GROUP + top_i
    combine = jnp.sum(jax.nn.one_hot(eid, N_EXPERTS, dtype=F32) * w_sel[..., None], axis=1)
    out = jnp.zeros((B * T, D), F32)
    for gi in range(N_GROUPS):
        sl = slice(gi * EXPERTS_PER_GROUP, (gi + 1) * EXPERTS_PER_GROUP)
        a = jax.nn.silu(jnp.einsum('nd,edf->nef', x, w_gate[sl])) * jnp.einsum('nd,edf->nef', x, w_up[sl])
        a = a * combine[:, sl, None].astype(a.dtype)
        out = out + jnp.einsum('nef,efd->nd', a, w_down[sl]).astype(F32)
    return out.astype(h.dtype).reshape(B, T, D)

def trunk(x, segments, conv0, sa0, sb0, norm_mix, w_in, conv_w, a_log, dt_bias, norm_a,
          gla_gate_up, gla_gate_bias, norm_b, w_proj_a, w_proj_b, w_out, norm_ffn,
          router_group_w, router_group_b, router_expert_w, router_expert_b,
          expert_w_gate, expert_w_up, expert_w_down, norm_final):
    convs, sas, sbs = [], [], []
    for l in range(DEPTH):
        mix, c, sa, sb = mixer(rmsnorm(x, norm_mix[l]), conv0[l], sa0[l], sb0[l], segments,
                               w_in[l], conv_w[l], a_log[l], dt_bias[l], norm_a[l],
                               gla_gate_up[l], gla_gate_bias[l], norm_b[l],
                               w_proj_a[l], w_proj_b[l], w_out[l])
        x = x + mix
        x = x + hier_moe(rmsnorm(x, norm_ffn[l]), router_group_w[l], router_group_b[l],
                         router_expert_w[l], router_expert_b[l],
                         expert_w_gate[l], expert_w_up[l], expert_w_down[l])
        convs.append(c)
        sas.append(sa)
        sbs.append(sb)
    return rmsnorm(x, norm_final), jnp.stack(sas), jnp.stack(convs), jnp.stack(sbs)

def setup_inputs(seed: int = 0) -> dict:
    key = jax.random.key(seed)
    ks = jax.random.split(key, 32)

    def nrm(i, shape, scale):
        return jax.random.normal(ks[i], shape, F32) * scale

    dt = jnp.exp(jax.random.uniform(ks[10], (DEPTH, H_A), F32, minval=float(np.log(1e-3)), maxval=float(np.log(1e-1))))
    return {
        'x_prompt': nrm(0, (BATCH, SEQ, D_MODEL), 1.0),
        'x_sample': nrm(1, (DEC_BATCH, DEC_SEQ, D_MODEL), 1.0),
        'state_delta': nrm(2, (DEPTH, DEC_BATCH, H_A, DK_A, DV_A), 0.1),
        'state_conv': nrm(3, (DEPTH, DEC_BATCH, CONV_W - 1, CONV_CH), 1.0),
        'state_gla': nrm(4, (DEPTH, DEC_BATCH, H_B, DK_B, DV_B), 0.5),
        'meta_tokens': nrm(5, (N_META, D_MODEL), 1.0),
        'norm_mix': 1.0 + nrm(6, (DEPTH, D_MODEL), 0.02),
        'w_in': nrm(7, (DEPTH, D_MODEL, IN_COLS), D_MODEL ** -0.5),
        'conv_w': nrm(8, (DEPTH, CONV_W, CONV_CH), CONV_W ** -0.5),
        'a_log': jnp.log(jax.random.uniform(ks[9], (DEPTH, H_A), F32, minval=1.0, maxval=16.0)),
        'dt_bias': dt + jnp.log(-jnp.expm1(-dt)),
        'norm_a': 1.0 + nrm(11, (DEPTH, DV_A), 0.02),
        'gla_gate_up': nrm(12, (DEPTH, GATE_RANK, H_B * DK_B), GATE_RANK ** -0.5),
        'gla_gate_bias': nrm(13, (DEPTH, H_B * DK_B), 0.1),
        'norm_b': 1.0 + nrm(14, (DEPTH, DV_B), 0.02),
        'w_proj_a': nrm(15, (DEPTH, H_A * DV_A, D_MODEL), (H_A * DV_A) ** -0.5),
        'w_proj_b': nrm(16, (DEPTH, H_B * DV_B, D_MODEL), (H_B * DV_B) ** -0.5),
        'w_out': nrm(17, (DEPTH, D_MODEL, D_MODEL), D_MODEL ** -0.5),
        'norm_ffn': 1.0 + nrm(18, (DEPTH, D_MODEL), 0.02),
        'router_group_w': nrm(19, (DEPTH, D_MODEL, N_GROUPS), D_MODEL ** -0.5),
        'router_group_b': nrm(20, (DEPTH, N_GROUPS), 0.01),
        'router_expert_w': nrm(21, (DEPTH, D_MODEL, N_EXPERTS), D_MODEL ** -0.5),
        'router_expert_b': nrm(22, (DEPTH, N_EXPERTS), 0.01),
        'expert_w_gate': nrm(23, (DEPTH, N_EXPERTS, D_MODEL, D_FF_E), D_MODEL ** -0.5),
        'expert_w_up': nrm(24, (DEPTH, N_EXPERTS, D_MODEL, D_FF_E), D_MODEL ** -0.5),
        'expert_w_down': nrm(25, (DEPTH, N_EXPERTS, D_FF_E, D_MODEL), D_FF_E ** -0.5),
        'norm_final': 1.0 + nrm(26, (D_MODEL,), 0.02),
    }

def reference(x_prompt, x_sample, state_delta, state_conv, state_gla, meta_tokens, norm_mix, w_in,
              conv_w, a_log, dt_bias, norm_a, gla_gate_up, gla_gate_bias, norm_b, w_proj_a, w_proj_b,
              w_out, norm_ffn, router_group_w, router_group_b, router_expert_w, router_expert_b,
              expert_w_gate, expert_w_up, expert_w_down, norm_final):
    Bp, Tp, D = x_prompt.shape
    meta = jnp.broadcast_to(meta_tokens.astype(x_prompt.dtype)[None], (Bp, N_META, D))
    xp = jnp.concatenate([meta, x_prompt], axis=1)
    segs_p = [(0, N_META, N_META), (N_META, Tp, CHUNK)]
    conv0 = jnp.zeros((DEPTH, Bp, CONV_W - 1, CONV_CH), F32)
    sa0 = jnp.zeros((DEPTH, Bp, H_A, DK_A, DV_A), F32)
    sb0 = jnp.zeros((DEPTH, Bp, H_B, DK_B, DV_B), F32)
    yp, sa_p, conv_p, sb_p = trunk(xp, segs_p, conv0, sa0, sb0, norm_mix, w_in, conv_w, a_log, dt_bias,
                                   norm_a, gla_gate_up, gla_gate_bias, norm_b, w_proj_a, w_proj_b, w_out,
                                   norm_ffn, router_group_w, router_group_b, router_expert_w,
                                   router_expert_b, expert_w_gate, expert_w_up, expert_w_down, norm_final)
    y_prompt = yp[:, N_META:]
    Ts = x_sample.shape[1]
    segs_s = [(0, Ts, Ts)]
    y_sample, sa_s, conv_s, sb_s = trunk(x_sample, segs_s, state_conv, state_delta, state_gla, norm_mix, w_in,
                                         conv_w, a_log, dt_bias, norm_a, gla_gate_up, gla_gate_bias, norm_b,
                                         w_proj_a, w_proj_b, w_out, norm_ffn, router_group_w, router_group_b,
                                         router_expert_w, router_expert_b, expert_w_gate, expert_w_up,
                                         expert_w_down, norm_final)
    pdt = x_prompt.dtype
    return (y_prompt, y_sample,
            sa_p.astype(pdt), conv_p.astype(pdt), sb_p.astype(pdt),
            sa_s.astype(state_delta.dtype), conv_s.astype(state_conv.dtype), sb_s.astype(state_gla.dtype))


_drawn_inputs = setup_inputs


def setup_inputs(seed=0):
    import zlib

    import numpy as np

    out = dict(_drawn_inputs(seed))
    spreads = {}
    factors = {'norm_a': 14.441,
     'norm_b': 10.637,
     'router_group_b': 8.0,
     'router_expert_b': 12.597,
     'norm_final': 7.806,
     'norm_ffn': 5.454}
    for name, (base, spread) in spreads.items():
        noise = np.random.default_rng([zlib.crc32(name.encode()), seed]).standard_normal(out[name].shape)
        drawn = base * np.exp(spread * noise) if base else spread * noise
        out[name] = jnp.asarray(drawn.astype(out[name].dtype))
    for name, factor in factors.items():
        out[name] = (out[name] * factor).astype(out[name].dtype)
    return out
```

```python
from contextlib import ExitStack

import concourse.bass as bass
from concourse import mybir

F32 = mybir.dt.float32
I32 = mybir.dt.int32
ALU = mybir.AluOpType
ACT = mybir.ActivationFunctionType
AX = mybir.AxisListType

D = 1024
KB = D // 128
META, SEQ = 16, 256
TP = META + SEQ
NB, TS = 8, 4
NT = TP + NB * TS
L = (128, 128, NT - 256)
T0 = (0, 128, 256)
TAIL = TP - 256
HA, HB = 8, 4
CONV = 3 * D
NCB = CONV // 128
CW = 4
XW = TP + CW - 1 + NB * (TS + CW - 1)
XS = TP + CW - 1
NG, EPG = 4, 8
FF = 256
CAP = 128
SLOTS = 8
SW = 2048
EPS = 1e-6
TAU = 16.0
C_QKV, C_Z, C_BA, C_QB, C_KB, C_VB, C_RB, C_LR, C_GA, C_GB = 0, 3072, 4096, 4112, 4624, 5136, 6160, 7184, 7200, 8224
WIN = ([C_QKV + 256 * i for i in range(12)] + [C_QB, C_QB + 256, C_KB, C_KB + 256] + [C_VB + 256 * i for i in range(4)]
       + [C_Z + 256 * i for i in range(4)] + [C_RB + 256 * i for i in range(4)]
       + [C_GA + 256 * i for i in range(4)] + [C_GB + 256 * i for i in range(4)])
N_QB, N_VB, N_Z, N_PA = 12, 16, 20, len(WIN)
N_WO = N_PA + 8
N_PRE = N_WO + 4
PER_GROUP = 3 * EPG


def units(n):
    return sum(3 if N_VB <= k < N_Z or k >= N_WO else 2 for k in range(n))


def named(nc, stage, names):
    return {n: nc.alloc_semaphore(f"{stage}_{n}") for n in names.split()}


class Chain:
    def __init__(self, eng, sem):
        self.eng, self.sem, self.n = eng, sem, 0

    def __call__(self, ins):
        self.n += 1
        ins.then_inc(self.sem, 1)
        self.eng.wait_ge(self.sem, self.n)


def bc_mid(ap2, n):
    return ap2.unsqueeze(1).to_broadcast([ap2.shape[0], n, ap2.shape[1]])


def bc_last(ap, n):
    k = len(ap.shape)
    return ap.unsqueeze(k).to_broadcast([*ap.shape, n])


class Core:

    def __init__(self, nc, ctx, i_, o_):
        self.nc, self.ctx, self.i_, self.o_ = nc, ctx, i_, o_

        def sb(name, shape, dt=F32):
            return ctx.enter_context(nc.sbuf_tensor(name, shape, dt))
        self.ring = sb("ring", [128, SLOTS, SW])
        self.hT = sb("hT", [128, KB, NT])
        self.oaT = sb("oaT", [128, HA, NT])
        m = self.masks = sb("masks", [128, 21, 128])
        self.ident, self.U, self.SL, self.SU, self.BLK = (m[:, k, :] for k in range(5))
        self.PAIR = [m[:, k, :] for k in range(5, 8)]
        self.GR = m[:, 8:13, :]
        self.GM = m[:, 13:17, :]
        self.U3, self.SL3, self.SU3, self.R03 = (m[:, k, :] for k in range(17, 21))
        self.ones = sb("ones", [128, 128])
        self.seg = sb("seg", [128, 9])
        self.lrT = sb("lrT", [16, NT])
        self.small = sb("small", [128, 1300])
        self.at = 0
        self.cnti = sb("cnti", [128, 1], I32)
        self.AR = 26000
        self.arena = sb("arena", [128, self.AR])
        P = self.piece
        self.epsc = P(1)
        self.ss, self.rstd = P(3), P(3)
        self.nm, self.nf = P(8), P(8)
        self.cw = P(CW * NCB, CW, NCB)
        self.na, self.nb = P(1), P(2)
        self.sm = P(48, 3, 16)
        self.t1, self.t2 = P(24, 3, 8), P(24, 3, 8)
        self.beta = P(24, 3, 8)
        self.nbeg = P(24, 3, 8)
        self.gg = P(24, 3, 8)
        self.kw = P(24, 3, 8)
        self.egl = P(16, 2, 8)
        self.egl3, self.gm3 = P(72, 9, 8), P(72, 9, 8)
        self.hrow, self.hbc = P(16), P(16)
        self.rbias = P(36)
        self.psum = [ctx.enter_context(nc.psum_tensor(f"ps{k}", [128, 512], F32)) for k in range(8)]
        self.ring_in = [ctx.enter_context(nc.semaphore(f"ring_in{s}")) for s in range(SLOTS)]
        self.unit_done = ctx.enter_context(nc.semaphore("unit_done"))
        self.w_in = i_["w_in"][0].rearrange("(p j) c -> p j c", j=KB)

    @staticmethod
    def shaped(v, dims):
        if len(dims) == 2:
            return v.rearrange("p (a b) -> p a b", b=dims[1])
        if len(dims) == 3:
            return v.rearrange("p (a b c) -> p a b c", b=dims[1], c=dims[2])
        return v

    def piece(self, n, *dims):
        v = self.small[:, self.at:self.at + n]
        self.at += n
        assert self.at <= 1300
        return self.shaped(v, dims)

    def carve(self, off, n, *dims):
        assert off + n <= self.AR, (off, n)
        return self.shaped(self.arena[:, off:off + n], dims)

    def slot8(self, n):
        return self.ring[:, n % SLOTS, :].rearrange("p (j c) -> p j c", j=KB)

    def bank4(self, b, l=128):
        return self.psum[b][:, :].rearrange("p (h t) -> p h t", h=4)[:, :, 0:l]

    def load_w(self, sp, n):
        if n >= SLOTS:
            sp.wait_ge(self.unit_done, units(n - SLOTS + 1))
        if n < N_PA:
            src = self.w_in[:, :, WIN[n]:WIN[n] + 256]
        else:
            m, q = divmod(n - N_PA, 4)
            w = self.i_[("w_proj_a", "w_proj_b", "w_out")[m]][0]
            src = w.rearrange("(j p) c -> p j c", p=128)[:, :, 256 * q:256 * q + 256]
        sp.dma_start(self.slot8(n), src).then_inc(self.ring_in[n % SLOTS], 16)

    def load_x(self, sp, X, signal):
        xp = self.i_["x_prompt"]
        sp.dma_start(X[0:META, 0, :], self.i_["meta_tokens"][:, :]).then_inc(signal, 16)
        sp.dma_start(X[META:128, 0, :], xp[0, 0:112, :]).then_inc(signal, 16)
        sp.dma_start(X[:, 1, :], xp[0, 112:240, :]).then_inc(signal, 16)
        sp.dma_start(X[0:TAIL, 2, :], xp[0, 240:256, :]).then_inc(signal, 16)
        sp.dma_start(X[TAIL:L[2], 2, :], self.i_["x_sample"].rearrange("b t d -> (b t) d")).then_inc(signal, 16)

    def arrived(self, pe, n):
        pe.wait_ge(self.ring_in[n % SLOTS], 16 * (n // SLOTS + 1))

    def block_of_slot(self, pe, n, q, b, moving=None):
        self.arrived(pe, n)
        for j in range(KB):
            ins = self.nc.tensor.matmul(self.psum[b][:, 0:NT], self.slot8(n)[:, j, 128 * q:128 * q + 128],
                                        self.hT[:, j, :] if moving is None else moving(j), start=(j == 0), stop=(j == KB - 1))
        ins.then_inc(self.unit_done, 1)


A1 = 8576


def front(k):
    nc, i_, o_ = k.nc, k.i_, k.o_
    ident, U, SL, SU, BLK, PAIR, GR, GM = k.ident, k.U, k.SL, k.SU, k.BLK, k.PAIR, k.GR, k.GM
    U3, SL3, SU3, R03, ones, seg, masks = k.U3, k.SL3, k.SU3, k.R03, k.ones, k.seg, k.masks
    hT, oaT, psum, unit_done, w_in, lrT = k.hT, k.oaT, k.psum, k.unit_done, k.w_in, k.lrT
    epsc, ss, rstd, nm, nf, cw, na, nb, sm, t1, t2 = k.epsc, k.ss, k.rstd, k.nm, k.nf, k.cw, k.na, k.nb, k.sm, k.t1, k.t2
    beta, nbeg, gg, kw, egl, egl3, gm3, hrow, hbc, rbias = k.beta, k.nbeg, k.gg, k.kw, k.egl, k.egl3, k.gm3, k.hrow, k.hbc, k.rbias
    KT = k.carve(0, HA * NT, HA, NT)
    Kd = k.carve(2432, 3072, 3, 8, 128)
    V = k.carve(5504, 3072, 3, 8, 128)
    X = k.carve(A1, 3072, 3, D)
    XN = k.carve(A1 + 3072, 3072, 3, D)
    SC = k.carve(A1 + 6144, CONV)
    SCO = k.carve(A1 + 9216, CONV)
    CWR = k.carve(A1 + 12288, 128)
    wsm = k.carve(A1 + 12416, KB * 32, KB, 32)
    XC = k.carve(A1, 3 * XW, 3, XW)
    CV = k.carve(A1 + 3 * XW, 2 * XW, 2, XW)
    VT = k.carve(A1 + 5 * XW, 2 * NT, 2, NT)
    LAST = k.carve(A1 + 5 * XW + 2 * NT, NCB * 27, NCB, 27)
    SQ = k.carve(A1 + 3 * XW, 2 * NT, 2, NT)
    RS = k.carve(A1 + 3 * XW + 2 * NT, 2 * NT, 2, NT)
    s = named(nc, "front", """x_in par_in late_in sc_in mask_ready rstd_ready xn_ready xT_done xT_evac small_done small_ready
        hist_done hist_ready conv_ready conv_silu last_ready last_done last_evac sq_ready ssum_done rs_ready
        qk_ready vT_done vT_evac kT_done kT_evac par_done par_ready g_ready gsum_done gsum_ready lr_done lr_ready
        sc_out act_c dve_c pool_c""")
    ctx = ExitStack()
    block = ctx.enter_context(nc.Block())

    @block.sync
    def _(sp):
        k.load_x(sp, X, s["x_in"])
        sp.dma_start(nm, i_["norm_mix"][0].rearrange("(p j) -> p j", j=KB)).then_inc(s["par_in"], 16)
        sp.dma_start(wsm[:, :, 0:16], w_in[:, :, C_BA:C_BA + 16]).then_inc(s["par_in"], 16)
        sp.dma_start(wsm[:, :, 16:32], w_in[:, :, C_LR:C_LR + 16]).then_inc(s["par_in"], 16)
        sp.dma_start(CWR[0:CW * NCB, :], i_["conv_w"][0].rearrange("i (b c) -> (i b) c", c=128)).then_inc(s["par_in"], 16)
        sp.dma_start(hrow[0:1, 0:8], i_["a_log"]).then_inc(s["par_in"], 16)
        sp.dma_start(hrow[0:1, 8:16], i_["dt_bias"]).then_inc(s["par_in"], 16)
        sp.dma_start(SC[0:24, :], i_["state_conv"][0].rearrange("b r c -> (b r) c")).then_inc(s["sc_in"], 16)
        for n in range(N_Z):
            k.load_w(sp, n)
        sp.dma_start(na, i_["norm_a"][0].rearrange("(p a) -> p a", a=1)).then_inc(s["late_in"], 16)
        for a in range(2):
            sp.dma_start(nb[:, a:a + 1], i_["norm_b"][0, 128 * a:128 * a + 128].rearrange("(p a) -> p a", a=1)).then_inc(s["late_in"], 16)
        sp.dma_start(nf, i_["norm_ffn"][0].rearrange("(p j) -> p j", j=KB)).then_inc(s["late_in"], 16)
        sp.dma_start(rbias[0:1, 0:4], i_["router_group_b"]).then_inc(s["late_in"], 16)
        sp.dma_start(rbias[0:1, 4:36], i_["router_expert_b"]).then_inc(s["late_in"], 16)
        sp.wait_ge(s["last_evac"], 6)
        sp.dma_start(o_["conv_p"][0, 0], SCO[0:3, :]).then_inc(s["sc_out"], 16)
        sp.dma_start(o_["conv_s"][0].rearrange("b r c -> (b r) c"), SCO[3:27, :]).then_inc(s["sc_out"], 16)
        sp.wait_ge(s["sc_out"], 32)
        sp.wait_ge(s["late_in"], 96)


    @block.gpsimd
    def _(pl):
        link = Chain(pl, s["pool_c"])

        def keep(ap, pattern, base, cm):
            link(nc.gpsimd.affine_select(out=ap, in_=ap, compare_op=ALU.is_ge, fill=0.0, base=base,
                                   pattern=pattern, channel_multiplier=cm))

        def blocks(ap, m):
            v = ap.rearrange("p (a b) -> p a b", b=m)
            n = ap.shape[1] // m
            keep(v, [[-m, n], [0, m]], 0, 1)
            keep(v, [[m, n], [0, m]], m - 1, -1)
        link(nc.gpsimd.memset(ones[:, :], 1.0))
        link(nc.gpsimd.memset(masks[:, :, :], 1.0))
        link(nc.gpsimd.memset(epsc, EPS))
        link(nc.gpsimd.memset(seg[:, :], 1.0))
        keep(ident, [[1, 128]], 0, -1)
        keep(ident, [[-1, 128]], 0, 1)
        keep(U, [[1, 128]], 0, -1)
        keep(SL, [[-1, 128]], -1, 1)
        keep(SU, [[1, 128]], -1, -1)
        blocks(BLK, 16)
        for M, m in zip(PAIR, (16, 32, 64)):
            v = M.rearrange("p (a h b) -> p a h b", h=2, b=m)
            n = 128 // (2 * m)
            keep(v, [[-2 * m, n], [-1000, 2], [0, m]], -m, 1)
            keep(v, [[2 * m, n], [0, 2], [0, m]], 2 * m - 1, -1)
        link(nc.gpsimd.tensor_copy(GR[:, 0, :], U))
        for r, m in ((1, 8), (2, 64), (3, 32), (4, 16)):
            v = GR[:, r, :].rearrange("p (a h b) -> p a h b", h=2, b=m)
            for h, src in ((0, SL), (1, U)):
                half = src.rearrange("p (a h b) -> p a h b", h=2, b=m)
                if r == 1 and h == 0:
                    link(nc.gpsimd.tensor_scalar(v[:, :, h, :], half[:, :, h, :], -1.0, None, ALU.mult))
                else:
                    link(nc.gpsimd.tensor_copy(v[:, :, h, :], half[:, :, h, :]))
            blocks(GR[:, r, :], m)
        link(nc.gpsimd.tensor_tensor(GM[:, 0, :], U, BLK, ALU.mult))
        for r, m in ((1, 64), (2, 32), (3, 16)):
            v = GM[:, r, :].rearrange("p (a h b) -> p a h b", h=2, b=m)
            n = 128 // (2 * m)
            keep(v, [[-2 * m, n], [0, 2], [0, m]], 0, 1)
            keep(v, [[2 * m, n], [1000, 2], [0, m]], m - 1 - 1000, -1)
        for M, src in ((U3, U), (SL3, SL), (SU3, SU)):
            link(nc.gpsimd.tensor_copy(M, src))
            keep(M[:, 0:TAIL], [[0, TAIL]], TAIL - 1, -1)
            v = M[:, TAIL:L[2]].rearrange("p (a b) -> p a b", b=TS)
            keep(v, [[-TS, NB], [0, TS]], -TAIL, 1)
            keep(v, [[TS, NB], [0, TS]], TAIL + TS - 1, -1)
        link(nc.gpsimd.tensor_copy(R03[:, 0:TAIL], GR[:, 1, 0:TAIL]))
        link(nc.gpsimd.tensor_copy(R03[:, TAIL:L[2]], U3[:, TAIL:L[2]]))
        keep(seg[:, 0:1], [[0, 1]], TAIL - 1, -1)
        keep(seg[:, 1:9], [[-TS, NB]], -TAIL, 1)
        keep(seg[:, 1:9], [[TS, NB]], TAIL + TS - 1, -1)
        pl.drain().then_inc(s["mask_ready"], 1)

        for b in range(NCB):
            pl.wait_ge(s["hist_ready"], b + 1)
            x = XC[:, b % 3, :]
            nc.gpsimd.tensor_copy(LAST[:, b, 0:3], x[:, TP:TP + 3])
            nc.gpsimd.tensor_copy(LAST[:, b, 3:27].rearrange("p (a r) -> p a r", r=3),
                            x[:, XS:].rearrange("p (a r) -> p a r", r=TS + 3)[:, :, TS:]).then_inc(s["last_ready"], 1)
        pl.wait_ge(s["conv_silu"], NCB)
        for b in range(16):
            if b >= 2:
                pl.wait_ge(s["ssum_done"], b - 1)
            src = (oaT if b < 8 else KT)[:, b % 8, :]
            nc.gpsimd.tensor_tensor(SQ[:, b % 2, :], src, src, ALU.mult).then_inc(s["sq_ready"], 1)


    @block.scalar
    def _(act):
        link = Chain(act, s["act_c"])
        act.wait_ge(s["x_in"], 80)
        act.wait_ge(s["mask_ready"], 1)
        for c in range(3):
            l = L[c]
            link(nc.scalar.activation(XN[0:l, c, :], X[0:l, c, :], ACT.Square, accum_out=ss[0:l, c:c + 1]))
            link(nc.scalar.activation(ss[0:l, c:c + 1], ss[0:l, c:c + 1], ACT.Ln, scale=1.0 / D, bias=epsc[0:l, :]))
            nc.scalar.activation(rstd[0:l, c:c + 1], ss[0:l, c:c + 1], ACT.Exp, scale=-0.5).then_inc(s["rstd_ready"], 1)
        act.wait_ge(s["par_done"], 2)
        link(nc.scalar.activation(hbc, psum[5][:, 0:16], ACT.Copy))
        link(nc.scalar.activation(hbc[:, 0:8], hbc[:, 0:8], ACT.Exp))
        nc.scalar.activation(cw.rearrange("p i b -> p (i b)"), psum[4][:, 0:CW * NCB], ACT.Copy).then_inc(s["par_ready"], 1)
        act.wait_ge(s["small_done"], 3)
        for c in range(3):
            nc.scalar.activation(sm[0:L[c], c, :], psum[6][0:L[c], 16 * c:16 * c + 16], ACT.Copy).then_inc(s["small_ready"], 1)
        act.wait_ge(s["lr_done"], 1)
        nc.scalar.activation(lrT[:, :], psum[7][0:16, 200:200 + NT], ACT.Copy).then_inc(s["lr_ready"], 1)
        act.wait_ge(s["small_ready"], 3)
        act.wait_ge(s["g_ready"], 1)
        for c in range(3):
            l = L[c]
            link(nc.scalar.activation(beta[0:l, c, :], sm[0:l, c, 0:8], ACT.Exp, scale=-1.0))
            link(nc.scalar.activation(t1[0:l, c, :], t1[0:l, c, :], ACT.Exp, scale=-1.0))
            nc.scalar.activation(t1[0:l, c, :], t1[0:l, c, :], ACT.Ln, bias=1.0).then_inc(s["g_ready"], 1)
        act.wait_ge(s["xT_evac"], 8)
        for r in range(3):
            nc.scalar.activation(XC[:, r, 0:3], ones[:, 0:3], ACT.Copy, scale=0.0)

        def decays():
            act.wait_ge(s["gsum_done"], 3)
            for c in range(3):
                l = L[c]
                p = psum[7][:, 32 * c:32 * c + 32]
                link(nc.scalar.activation(nbeg[0:l, c, :], p[0:l, 0:8], ACT.Exp))
                nc.scalar.activation(kw[0:l, c, :], p[0:l, 8:16], ACT.Exp)
                if c < 2:
                    nc.scalar.activation(egl[:, c, :], p[:, 16:24], ACT.Exp)
                else:
                    nc.scalar.activation(egl3.rearrange("p a b -> p (a b)"), psum[7][:, 96:168], ACT.Exp)
                link(nc.scalar.activation(nbeg[0:l, c, :], nbeg[0:l, c, :], ACT.Copy, scale=-1.0))
                act.drain().then_inc(s["gsum_ready"], 1)

        def silu(b):
            act.wait_ge(s["conv_ready"], b + 1)
            src = CV[:, b % 2, :]
            if b < 16:
                dst = (oaT if b < 8 else KT)[:, b % 8, :]
            else:
                if b >= 18:
                    act.wait_ge(s["vT_done"], b - 17)
                dst = VT[:, b % 2, :]
            nc.scalar.activation(dst[:, 0:TP], src[:, 0:TP], ACT.Silu)
            nc.scalar.activation(dst[:, TP:].rearrange("p (a r) -> p a r", r=TS),
                         src[:, XS:XS + 56].rearrange("p (a r) -> p a r", r=TS + 3)[:, :, 0:TS], ACT.Silu).then_inc(s["conv_silu"], 1)
        for b in range(NCB):
            if b == 3:
                decays()
            act.wait_ge(s["hist_done"], b + 1)
            act.wait_ge(unit_done, b + 1)
            if b >= 3:
                act.wait_ge(s["conv_ready"], b - 2)
                act.wait_ge(s["last_ready"], b - 2)
            x = XC[:, b % 3, :]
            xs = x[:, XS:].rearrange("p (a r) -> p a r", r=TS + 3)
            nc.scalar.activation(xs[:, :, 0:3], psum[4 + b % 2][:, 0:24].rearrange("p (a r) -> p a r", r=3), ACT.Copy)
            nc.scalar.activation(x[:, 3:XS], psum[b % 4][:, 0:TP], ACT.Copy)
            nc.scalar.activation(xs[:, :, 3:], psum[b % 4][:, TP:NT].rearrange("p (a r) -> p a r", r=TS), ACT.Copy)
            act.drain().then_inc(s["hist_ready"], 1)
            if b >= 2:
                silu(b - 2)
        silu(NCB - 2)
        silu(NCB - 1)
        for b in range(16):
            act.wait_ge(s["ssum_done"], b + 1)
            if b >= 2:
                act.wait_ge(s["qk_ready"], b - 1)
            link(nc.scalar.activation(RS[:, b % 2, :], psum[b % 4][:, 0:NT], ACT.Ln, bias=epsc))
            nc.scalar.activation(RS[:, b % 2, :], RS[:, b % 2, :], ACT.Exp, scale=-0.5).then_inc(s["rs_ready"], 1)
        for q in range(6):
            act.wait_ge(s["last_done"], q + 1)
            nc.scalar.activation(SCO[0:27, 512 * q:512 * q + 512], psum[4 + q % 2][0:27, :], ACT.Copy).then_inc(s["last_evac"], 1)


    @block.vector
    def _(dve):
        link = Chain(dve, s["dve_c"])
        for c in range(3):
            l = L[c]
            dve.wait_ge(s["rstd_ready"], c + 1)
            nc.vector.tensor_scalar(XN[0:l, c, :], X[0:l, c, :], rstd[0:l, c:c + 1], None, ALU.mult).then_inc(s["xn_ready"], 1)
        dve.wait_ge(s["par_in"], 96)
        for j in range(KB):
            dve.wait_ge(s["xT_done"], j + 1)
            nc.vector.tensor_scalar(hT[:, j, :], psum[j % 4][:, 0:NT], nm[:, j:j + 1], None, ALU.mult).then_inc(s["xT_evac"], 1)
        dve.wait_ge(s["par_ready"], 1)
        dve.wait_ge(s["small_ready"], 3)
        for c in range(3):
            l = L[c]
            link(nc.vector.tensor_tensor(sm[0:l, c, 8:16], sm[0:l, c, 8:16], hbc[0:l, 8:16], ALU.add))
            link(nc.vector.tensor_scalar(t2[0:l, c, :], sm[0:l, c, 8:16], 0.0, None, ALU.max))
            link(nc.vector.scalar_tensor_tensor(t1[0:l, c, :], t2[0:l, c, :], 2.0, sm[0:l, c, 8:16], ALU.mult, ALU.subtract))
        dve.drain().then_inc(s["g_ready"], 1)
        dve.wait_ge(s["g_ready"], 4)
        for c in range(3):
            l = L[c]
            link(nc.vector.tensor_tensor(t2[0:l, c, :], t2[0:l, c, :], t1[0:l, c, :], ALU.add))
            link(nc.vector.scalar_tensor_tensor(gg[0:l, c, :], t2[0:l, c, :], -1.0, hbc[0:l, 0:8], ALU.mult, ALU.mult))
            link(nc.vector.tensor_scalar(beta[0:l, c, :], beta[0:l, c, :], 1.0, None, ALU.add))
            link(nc.vector.reciprocal(beta[0:l, c, :], beta[0:l, c, :]))
        link(nc.vector.tensor_tensor(gm3[0:48, :, :], bc_mid(gg[0:48, 2, :], 9), bc_last(seg[0:48, :], 8), ALU.mult))
        dve.drain().then_inc(s["g_ready"], 1)
        def vturn(h):
            dve.wait_ge(s["vT_done"], h + 1)
            for c in range(3):
                ins = nc.vector.tensor_copy(V[0:L[c], c, h, :], psum[6 + h % 2][0:L[c], 128 * c:128 * c + 128])
            ins.then_inc(s["vT_evac"], 1)

        for b in range(NCB):
            dve.wait_ge(s["hist_ready"], b + 1)
            if b >= 2:
                dve.wait_ge(s["conv_silu"], b - 1)
            x, o = XC[:, b % 3, :], CV[:, b % 2, 0:XW - 3]
            link(nc.vector.tensor_scalar(o, x[:, 0:XW - 3], cw[:, 0, b:b + 1], None, ALU.mult))
            for r in range(1, CW):
                ins = nc.vector.scalar_tensor_tensor(o, x[:, r:XW - 3 + r], cw[:, r, b:b + 1], o, ALU.mult, ALU.add)
                if r < 3:
                    link(ins)
            ins.then_inc(s["conv_ready"], 1)
            if b >= 19:
                vturn(b - 19)
        for h in range(NCB - 19, 8):
            vturn(h)
        for b in range(16):
            dve.wait_ge(s["rs_ready"], b + 1)
            t = (oaT if b < 8 else KT)[:, b % 8, :]
            nc.vector.scalar_tensor_tensor(t, t, 128 ** -0.5 if b < 8 else 1.0, RS[:, b % 2, :], ALU.mult, ALU.mult).then_inc(s["qk_ready"], 1)
        dve.wait_ge(s["gsum_ready"], 3)
        for h in range(8):
            dve.wait_ge(s["kT_done"], h + 1)
            for c in range(3):
                ins = nc.vector.tensor_scalar(Kd[0:L[c], c, h, :], psum[6 + h % 2][0:L[c], 128 * c:128 * c + 128], kw[0:L[c], c, h:h + 1], None, ALU.mult)
            ins.then_inc(s["kT_evac"], 1)


    @block.tensor
    def _(pe):
        mm = nc.tensor.matmul

        def tr(out, in_, n):
            return nc.tensor.transpose(out, in_, ident[0:n, 0:n])

        pe.wait_ge(s["mask_ready"], 1)
        for j in range(KB):
            if j >= 4:
                pe.wait_ge(s["xT_evac"], j - 3)
            for c in range(3):
                if j == 0:
                    pe.wait_ge(s["xn_ready"], c + 1)
                ins = tr(psum[j % 4][:, T0[c]:T0[c] + L[c]], XN[0:L[c], c, j::KB], L[c])
            ins.then_inc(s["xT_done"], 1)
        pe.wait_ge(s["par_in"], 96)
        tr(psum[4][:, 0:CW * NCB], CWR[0:CW * NCB, :], CW * NCB).then_inc(s["par_done"], 1)
        mm(psum[5][:, 0:16], ones[0:1, :], hrow[0:1, :], start=True, stop=True).then_inc(s["par_done"], 1)
        pe.wait_ge(s["xT_evac"], 8)
        for c in range(3):
            for j in range(KB):
                ins = mm(psum[6][0:L[c], 16 * c:16 * c + 16], hT[:, j, T0[c]:T0[c] + L[c]], wsm[:, j, 0:16], start=(j == 0), stop=(j == KB - 1))
            ins.then_inc(s["small_done"], 1)
        for j in range(KB):
            ins = mm(psum[7][0:16, 200:200 + NT], wsm[:, j, 16:32], hT[:, j, :], start=(j == 0), stop=(j == KB - 1))
        ins.then_inc(s["lr_done"], 1)

        def turn_v(h):
            pe.wait_ge(s["conv_silu"], 17 + h)
            if h >= 2:
                pe.wait_ge(s["vT_evac"], h - 1)
            for c in range(3):
                ins = tr(psum[6 + h % 2][0:L[c], 128 * c:128 * c + 128], VT[:, h % 2, T0[c]:T0[c] + L[c]], 128)
            ins.then_inc(s["vT_done"], 1)
        pe.wait_ge(s["sc_in"], 16)
        for b in range(NCB):
            if b >= 2:
                pe.wait_ge(s["hist_ready"], b - 1)
            if b < 2:
                pe.wait_ge(s["par_ready"], 1)
                pe.wait_ge(s["small_ready"], 3)
            tr(psum[4 + b % 2][:, 0:24], SC[0:24, 128 * b:128 * b + 128], 24).then_inc(s["hist_done"], 1)
            if b >= 4:
                pe.wait_ge(s["hist_ready"], b - 3)
            k.block_of_slot(pe, b // 2, b % 2, b % 4)
            if b == 2:
                pe.wait_ge(s["g_ready"], 5)
                pe.wait_ge(s["lr_ready"], 1)
                for c in range(3):
                    l = L[c]
                    p = psum[7][:, 32 * c:32 * c + 32]
                    mm(p[0:l, 0:8], (U if c < 2 else U3)[0:l, 0:l], gg[0:l, c, :], start=True, stop=True)
                    ins = mm(p[0:l, 8:16], (SL if c < 2 else SL3)[0:l, 0:l], gg[0:l, c, :], start=True, stop=True)
                    if c < 2:
                        ins = mm(p[:, 16:24], ones[:, :], gg[:, c, :], start=True, stop=True)
                    else:
                        ins = mm(psum[7][:, 96:168], ones[0:l, :], gm3[0:l, :, :].rearrange("p a b -> p (a b)"), start=True, stop=True)
                    ins.then_inc(s["gsum_done"], 1)
            if b >= 19:
                if b == 19:
                    pe.wait_ge(s["gsum_ready"], 3)
                turn_v(b - 19)
        for h in range(NCB - 19, 8):
            turn_v(h)
        for b in range(16):
            pe.wait_ge(s["sq_ready"], b + 1)
            if b >= 4:
                pe.wait_ge(s["rs_ready"], b - 3)
            mm(psum[b % 4][:, 0:NT], ones[:, :], SQ[:, b % 2, :], start=True, stop=True).then_inc(s["ssum_done"], 1)
        for h in range(8):
            pe.wait_ge(s["qk_ready"], 9 + h)
            pe.wait_ge(s["vT_evac"], 8)
            if h >= 2:
                pe.wait_ge(s["kT_evac"], h - 1)
            for c in range(3):
                ins = tr(psum[6 + h % 2][0:L[c], 128 * c:128 * c + 128], KT[:, h, T0[c]:T0[c] + L[c]], 128)
            ins.then_inc(s["kT_done"], 1)
        pe.wait_ge(s["last_ready"], NCB)
        for q in range(6):
            if q >= 2:
                pe.wait_ge(s["last_evac"], q - 1)
            for r in range(4):
                ins = tr(psum[4 + q % 2][0:27, 128 * r:128 * r + 128], LAST[:, 4 * q + r, :], 128)
            ins.then_inc(s["last_done"], 1)

    ctx.close()
    nc.clear_and_free_semaphores(list(s.values()))
    nc.all_engine_barrier()


def delta(k):
    nc, i_, o_ = k.nc, k.i_, k.o_
    ident, U, SL, SU, BLK, PAIR = k.ident, k.U, k.SL, k.SU, k.BLK, k.PAIR
    U3, SL3, SU3, ones, seg = k.U3, k.SL3, k.SU3, k.ones, k.seg
    oaT, bank4, beta, nbeg, gg, egl, egl3 = k.oaT, k.bank4, k.beta, k.nbeg, k.gg, k.egl, k.egl3
    KT = k.carve(0, HA * NT, HA, NT)
    Kd = k.carve(2432, 3072, 3, 8, 128)
    V = k.carve(5504, 3072, 3, 8, 128)
    MB = [A1 + 5632 * hh for hh in range(2)]
    buf = [[k.carve(MB[hh] + 512 * x, 512, 4, 128) for x in range(11)] for hh in range(2)]
    (bDT, bB, bD0, bB0, bD2, bB2, bD, bE, bY, bAT, bEG) = range(11)
    KDM = [[k.carve(MB[hh] + 512 * (2 + 3 * x), 9 * 128, 9, 128) for x in range(2)] for hh in range(2)]
    SA = k.carve(A1 + 11264, 4096, 4, 8, 128)
    S = k.carve(A1 + 15360, 1024, 8, 128)
    s = named(nc, "delta", """xg_ready sb_ready diff_done kk_done eg_done dt_ready eg_ready b_ready at1_ready at_ready qe_ready
        dT_done d0_ready d_ready b0_ready y1_ready e_ready sq2_done d2_ready b2_ready p4_done y2_ready d4_ready
        b4_ready p8_done y3_ready d8_ready p9_done y4_ready lz_done z_ready x_ready lw_done y_ready ks_done
        kst_ready kst_done r_ready vn_done vn_ready o_done oT_ready ds_done s_ready kdm_ready su_done su_ready
        sscale_ready sa_in sa_out sp_out dve_c""")
    ctx = ExitStack()
    block = ctx.enter_context(nc.Block())

    @block.sync
    def _(sp):
        for hh in range(2):
            if hh:
                sp.wait_ge(s["sa_out"], 16 * 4)
            for b in range(4):
                sp.dma_start(SA[:, b, :, :], i_["state_delta"][0, :, 4 * hh + b].rearrange("b k v -> k b v")).then_inc(s["sa_in"], 16)
            sp.wait_ge(s["su_ready"], 4 * hh + 4)
            for b in range(4):
                sp.dma_start(o_["sd_s"][0, :, 4 * hh + b].rearrange("b k v -> k b v"), SA[:, b, :, :]).then_inc(s["sa_out"], 16)
        sp.wait_ge(s["s_ready"], 6)
        sp.dma_start(o_["sd_p"][0, 0].rearrange("h k v -> k h v"), S[:, :, :]).then_inc(s["sp_out"], 16)
        sp.wait_ge(s["sa_out"], 16 * 8)
        sp.wait_ge(s["sp_out"], 16)


    @block.gpsimd
    def _(pl):
        for c in range(3):
            l = L[c]
            mU, mSL, mSU = (U, SL, SU) if c < 2 else (U3, SL3, SU3)
            for hh in range(2):
                i = 2 * c + hh
                w = buf[hh]
                hs = slice(4 * hh, 4 * hh + 4)
                if c:
                    pl.wait_ge(s["s_ready"], i - 1)
                nc.gpsimd.tensor_tensor(w[bD2][0:l, :, 0:l], bc_mid(mSL[0:l, 0:l], 4), bc_last(gg[0:l, c, hs], l), ALU.mult)
                nc.gpsimd.tensor_tensor(w[bB2][0:l, :, :], bc_mid(ones[0:l, :], 4), bc_last(gg[0:l, c, hs], 128),
                                  ALU.mult).then_inc(s["xg_ready"], 1)
                nc.gpsimd.tensor_tensor(w[bE][0:l, :, 0:l], bc_mid(mSU[0:l, 0:l], 4), bc_last(beta[0:l, c, hs], l),
                                  ALU.mult).then_inc(s["sb_ready"], 1)
            for hh in range(2):
                i = 2 * c + hh
                w = buf[hh]
                hs = slice(4 * hh, 4 * hh + 4)
                tk = slice(T0[c], T0[c] + l)
                pl.wait_ge(s["b_ready"], i + 1)
                nc.gpsimd.tensor_tensor(w[bB0][0:l, :, 0:l], w[bB][0:l, :, 0:l], bc_mid(BLK[0:l, 0:l], 4),
                                  ALU.mult).then_inc(s["b0_ready"], 1)
                pl.wait_ge(s["b0_ready"], i + 1)
                nc.gpsimd.tensor_tensor(w[bY][0:l, :, 0:l], bc_mid(ident[0:l, 0:l], 4), w[bB0][0:l, :, 0:l],
                                  ALU.subtract).then_inc(s["y1_ready"], 1)
                pl.wait_ge(s["at1_ready"], i + 1)
                nc.gpsimd.tensor_tensor(w[bAT][0:l, :, 0:l], w[bAT][0:l, :, 0:l], bc_mid(mU[0:l, 0:l], 4),
                                  ALU.mult).then_inc(s["at_ready"], 1)
                pl.wait_ge(s["eg_ready"], i + 1)
                nc.gpsimd.tensor_tensor(w[bEG][:, :, 0:l], w[bEG][:, :, 0:l], oaT[:, hs, tk], ALU.mult).then_inc(s["qe_ready"], 1)
            if c < 2:
                for r, M in enumerate(PAIR):
                    for hh in range(2):
                        w = buf[hh]
                        pl.wait_ge(s["d_ready"], 2 * c + hh + 1)
                        if r:
                            pl.wait_ge(s["lz_done"], 6 * c + 2 * (r - 1) + hh + 1)
                        nc.gpsimd.tensor_tensor(w[bE][:, :, :], w[bD][:, :, :], bc_mid(M, 4), ALU.mult).then_inc(s["e_ready"], 1)
            else:
                for h in range(8):
                    hh = h // 4
                    pl.wait_ge(s["vn_ready"], 5 + hh)
                    if h % 4 >= 2:
                        pl.wait_ge(s["su_done"], h - 1)
                    nc.gpsimd.tensor_tensor(KDM[hh][h % 2][0:l, :, :], bc_mid(Kd[0:l, 2, h, :], 9), bc_last(seg[0:l, :], 128),
                                      ALU.mult).then_inc(s["kdm_ready"], 1)
                    pl.wait_ge(s["o_done"], 5 + hh)
                    nc.gpsimd.tensor_tensor(SA[:, h % 4, :, :], SA[:, h % 4, :, :], bc_last(egl3[:, 1:9, h], 128),
                                      ALU.mult).then_inc(s["sscale_ready"], 1)


    @block.scalar
    def _(act):
        for c in range(3):
            l = L[c]
            for hh in range(2):
                i, w, b0 = 2 * c + hh, buf[hh], 4 * hh
                act.wait_ge(s["diff_done"], i + 1)
                nc.scalar.activation(w[bDT][0:l, :, 0:l], bank4(b0, l)[0:l], ACT.Exp).then_inc(s["dt_ready"], 1)
                act.wait_ge(s["eg_done"], i + 1)
                nc.scalar.activation(w[bEG][:, :, 0:l], bank4(b0 + 3, l), ACT.Exp).then_inc(s["eg_ready"], 1)
            for hh in range(2):
                i, w, b0 = 2 * c + hh, buf[hh], 4 * hh
                act.wait_ge(s["d0_ready"], i + 1)
                nc.scalar.activation(w[bD][0:l, :, 0:l], bank4(b0, l)[0:l], ACT.Copy).then_inc(s["d_ready"], 1)
            for hh in range(2):
                i, w, b0 = 2 * c + hh, buf[hh], 4 * hh
                act.wait_ge(s["sq2_done"], i + 1)
                nc.scalar.activation(w[bD2][0:l, :, 0:l], bank4(b0 + 1, l)[0:l], ACT.Copy).then_inc(s["d2_ready"], 1)
            for hh in range(2):
                i, w, b0 = 2 * c + hh, buf[hh], 4 * hh
                act.wait_ge(s["p4_done"], i + 1)
                nc.scalar.activation(w[bD0][0:l, :, 0:l], bank4(b0, l)[0:l], ACT.Copy).then_inc(s["d4_ready"], 1)
                nc.scalar.activation(w[bB0][0:l, :, 0:l], bank4(b0 + 1, l)[0:l], ACT.Copy).then_inc(s["b4_ready"], 1)
            for hh in range(2):
                i, w, b0 = 2 * c + hh, buf[hh], 4 * hh
                act.wait_ge(s["p8_done"], i + 1)
                nc.scalar.activation(w[bD2][0:l, :, 0:l], bank4(b0 + 3, l)[0:l], ACT.Copy).then_inc(s["d8_ready"], 1)
            if c < 2:
                for k in range(3):
                    for hh in range(2):
                        w, b0 = buf[hh], 4 * hh
                        act.wait_ge(s["lz_done"], 6 * c + 2 * k + hh + 1)
                        nc.scalar.activation(w[bD0], bank4(b0 + 2, l), ACT.Copy).then_inc(s["x_ready"], 1)
            for hh in range(2):
                i, w, b0 = 2 * c + hh, buf[hh], 4 * hh
                hs = slice(4 * hh, 4 * hh + 4)
                if c == 2:
                    act.wait_ge(s["ks_done"], 3 + hh)
                    nc.scalar.activation(w[bD][:, :, 0:l], bank4(b0, l), ACT.Copy).then_inc(s["kst_ready"], 1)
                act.wait_ge(s["o_done"], i + 1)
                nc.scalar.activation(oaT[:, hs, T0[c]:T0[c] + l], bank4(b0 + 2, l), ACT.Copy).then_inc(s["oT_ready"], 1)


    @block.vector
    def _(dve):
        link = Chain(dve, s["dve_c"])
        for c in range(3):
            l = L[c]
            for hh in range(2):
                i, w, b0 = 2 * c + hh, buf[hh], 4 * hh

                def m(x):
                    return w[x][0:l, :, 0:l]
                dve.wait_ge(s["kk_done"], i + 1)
                dve.wait_ge(s["dt_ready"], i + 1)
                link(nc.vector.tensor_tensor(m(bB), bank4(b0 + 1, l)[0:l], m(bDT), ALU.mult))
                dve.wait_ge(s["sb_ready"], i + 1)
                nc.vector.tensor_tensor(m(bB), m(bB), m(bE), ALU.mult).then_inc(s["b_ready"], 1)
                nc.vector.tensor_tensor(m(bAT), bank4(b0 + 2, l)[0:l], m(bDT), ALU.mult).then_inc(s["at1_ready"], 1)
            for hh in range(2):
                i, w, b0 = 2 * c + hh, buf[hh], 4 * hh
                dve.wait_ge(s["dT_done"], i + 1)
                nc.vector.tensor_tensor(w[bD0][0:l, :, 0:l], bank4(b0, l)[0:l], bc_mid(BLK[0:l, 0:l], 4), ALU.mult).then_inc(s["d0_ready"], 1)
            for hh in range(2):
                i, w, b0 = 2 * c + hh, buf[hh], 4 * hh
                dve.wait_ge(s["sq2_done"], i + 1)
                nc.vector.tensor_copy(w[bB2][0:l, :, 0:l], bank4(b0 + 2, l)[0:l]).then_inc(s["b2_ready"], 1)
            for done, ready, bk in ((s["p4_done"], s["y2_ready"], 3), (s["p8_done"], s["y3_ready"], 2), (s["p9_done"], s["y4_ready"], 0)):
                for hh in range(2):
                    i, w, b0 = 2 * c + hh, buf[hh], 4 * hh
                    dve.wait_ge(done, i + 1)
                    nc.vector.tensor_tensor(w[bY][0:l, :, 0:l], w[bY][0:l, :, 0:l], bank4(b0 + bk, l)[0:l], ALU.add).then_inc(ready, 1)
            if c < 2:
                for k in range(3):
                    for hh in range(2):
                        w, b0 = buf[hh], 4 * hh
                        n = 6 * c + 2 * k + hh + 1
                        dve.wait_ge(s["lz_done"], n)
                        nc.vector.tensor_copy(w[bB2], bank4(b0 + 1, l)).then_inc(s["z_ready"], 1)
                    for hh in range(2):
                        w, b0 = buf[hh], 4 * hh
                        n = 6 * c + 2 * k + hh + 1
                        dve.wait_ge(s["lw_done"], n)
                        nc.vector.tensor_tensor(w[bY], w[bY], bank4(b0 + 3, l), ALU.subtract).then_inc(s["y_ready"], 1)
            for hh in range(2):
                i, w, b0 = 2 * c + hh, buf[hh], 4 * hh
                hs = slice(4 * hh, 4 * hh + 4)
                if c:
                    if c == 1:
                        dve.wait_ge(s["ks_done"], 1 + hh)
                        ks = bank4(b0, 128)
                    else:
                        dve.wait_ge(s["kst_done"], 1 + hh)
                        ks = bank4(b0 + 1, 128)[0:l]
                    r = w[bE][0:l, :, :]
                    link(nc.vector.tensor_tensor(r, ks, bc_last(nbeg[0:l, c, hs], 128), ALU.mult))
                    nc.vector.tensor_tensor(r, r, V[0:l, c, hs, :], ALU.add).then_inc(s["r_ready"], 1)
                dve.wait_ge(s["vn_done"], i + 1)
                nc.vector.tensor_tensor(w[bDT][0:l, :, :], bank4(b0 + 1, 128)[0:l], bc_last(beta[0:l, c, hs], 128), ALU.mult).then_inc(s["vn_ready"], 1)
                if c == 2:
                    for h in range(4 * hh, 4 * hh + 4):
                        dve.wait_ge(s["sscale_ready"], h + 1)
                        dve.wait_ge(s["su_done"], h + 1)
                        for q in range(2):
                            st = SA[:, h % 4, 4 * q:4 * q + 4, :]
                            ins = nc.vector.tensor_tensor(st, st, bank4(4 * (h % 2) + q, 128), ALU.add)
                        ins.then_inc(s["su_ready"], 1)
                dve.wait_ge(s["ds_done"], i + 1)
                if c == 0:
                    nc.vector.tensor_copy(S[:, hs, :], bank4(b0 + 3, 128)).then_inc(s["s_ready"], 1)
                else:
                    e = egl[:, 1, hs] if c == 1 else egl3[:, 0, hs]
                    link(nc.vector.tensor_tensor(S[:, hs, :], S[:, hs, :], bc_last(e, 128), ALU.mult))
                    nc.vector.tensor_tensor(S[:, hs, :], S[:, hs, :], bank4(b0 + 3, 128), ALU.add).then_inc(s["s_ready"], 1)


    @block.tensor
    def _(pe):
        mm = nc.tensor.matmul

        def tr(out, in_, n):
            return nc.tensor.transpose(out, in_, ident[0:n, 0:n])

        for c in range(3):
            l = L[c]
            tk = slice(T0[c], T0[c] + l)
            mU = U if c < 2 else U3

            def four(b, lhs, rhs, hh, start=True):
                for h in range(4):
                    ins = mm(bank4(b, l)[0:l, h, :], lhs[0:l, h, 0:l], rhs[0:l, h, 0:l], start=True, stop=True)
                return ins
            for hh in range(2):
                i, w, b0 = 2 * c + hh, buf[hh], 4 * hh
                if c:
                    pe.wait_ge(s["s_ready"], i - 1)
                    pe.wait_ge(s["oT_ready"], i - 1)
                for h in range(4):
                    ins = mm(bank4(b0 + 1, l)[0:l, h, :], KT[:, 4 * hh + h, tk], KT[:, 4 * hh + h, tk], start=True, stop=True)
                for h in range(4):
                    ins = mm(bank4(b0 + 2, l)[0:l, h, :], KT[:, 4 * hh + h, tk], oaT[:, 4 * hh + h, tk], start=True, stop=True)
                ins.then_inc(s["kk_done"], 1)
                pe.wait_ge(s["xg_ready"], i + 1)
                for h in range(4):
                    ins = mm(bank4(b0, l)[0:l, h, :], w[bD2][0:l, h, 0:l], mU[0:l, 0:l], start=True, stop=True)
                ins.then_inc(s["diff_done"], 1)
                for h in range(4):
                    ins = mm(bank4(b0 + 3, l)[:, h, :], w[bB2][0:l, h, :], mU[0:l, 0:l], start=True, stop=True)
                ins.then_inc(s["eg_done"], 1)
            for hh in range(2):
                i, w, b0 = 2 * c + hh, buf[hh], 4 * hh
                pe.wait_ge(s["b_ready"], i + 1)
                for h in range(4):
                    ins = tr(bank4(b0, l)[0:l, h, :], w[bB][0:l, h, 0:l], l)
                ins.then_inc(s["dT_done"], 1)
            for hh in range(2):
                i, w, b0 = 2 * c + hh, buf[hh], 4 * hh
                pe.wait_ge(s["d0_ready"], i + 1)
                pe.wait_ge(s["b0_ready"], i + 1)
                pe.wait_ge(s["at1_ready"], i + 1)
                four(b0 + 1, w[bB0], w[bD0], hh)
                four(b0 + 2, w[bD0], w[bB0], hh).then_inc(s["sq2_done"], 1)
            for hh in range(2):
                i, w, b0 = 2 * c + hh, buf[hh], 4 * hh
                pe.wait_ge(s["d2_ready"], i + 1)
                pe.wait_ge(s["b2_ready"], i + 1)
                pe.wait_ge(s["y1_ready"], i + 1)
                pe.wait_ge(s["eg_ready"], i + 1)
                pe.wait_ge(s["d_ready"], i + 1)
                four(b0 + 3, w[bD2], w[bY], hh)
                four(b0, w[bB2], w[bD2], hh)
                four(b0 + 1, w[bD2], w[bB2], hh).then_inc(s["p4_done"], 1)
            for hh in range(2):
                i, w, b0 = 2 * c + hh, buf[hh], 4 * hh
                pe.wait_ge(s["d4_ready"], i + 1)
                pe.wait_ge(s["y2_ready"], i + 1)
                four(b0 + 2, w[bD0], w[bY], hh)
                pe.wait_ge(s["b4_ready"], i + 1)
                four(b0 + 3, w[bB0], w[bD0], hh).then_inc(s["p8_done"], 1)
            for hh in range(2):
                i, w, b0 = 2 * c + hh, buf[hh], 4 * hh
                pe.wait_ge(s["d8_ready"], i + 1)
                pe.wait_ge(s["y3_ready"], i + 1)
                four(b0, w[bD2], w[bY], hh).then_inc(s["p9_done"], 1)
            if c < 2:
                for k in range(3):
                    for hh in range(2):
                        w, b0 = buf[hh], 4 * hh
                        n = 6 * c + 2 * k + hh + 1
                        if k == 0:
                            pe.wait_ge(s["y4_ready"], 2 * c + hh + 1)
                        else:
                            pe.wait_ge(s["y_ready"], n - 2)
                        pe.wait_ge(s["e_ready"], n)
                        four(b0 + 1, w[bE], w[bY], hh)
                        for h in range(4):
                            ins = tr(bank4(b0 + 2, l)[:, h, :], w[bY][:, h, :], l)
                        ins.then_inc(s["lz_done"], 1)
                    for hh in range(2):
                        w, b0 = buf[hh], 4 * hh
                        n = 6 * c + 2 * k + hh + 1
                        pe.wait_ge(s["z_ready"], n)
                        pe.wait_ge(s["x_ready"], n)
                        four(b0 + 3, w[bD0], w[bB2], hh).then_inc(s["lw_done"], 1)
            for hh in range(2):
                i, w, b0 = 2 * c + hh, buf[hh], 4 * hh
                if c < 2:
                    pe.wait_ge(s["y_ready"], 6 * c + 4 + hh + 1)
                else:
                    pe.wait_ge(s["y4_ready"], i + 1)
                if c == 1:
                    for h in range(4):
                        ins = mm(bank4(b0, 128)[:, h, :], KT[:, 4 * hh + h, tk], S[:, 4 * hh + h, :], start=True, stop=True)
                    ins.then_inc(s["ks_done"], 1)
                if c == 2:
                    pe.wait_ge(s["sa_in"], 64 * (hh + 1))
                    if hh:
                        pe.wait_ge(s["su_ready"], 4)

                    def states(dst, src, k0, first):
                        for h in range(4):
                            for b in range(9):
                                a, e = (0, TAIL) if b == 0 else (TAIL + TS * (b - 1), TAIL + TS * b)
                                st = S[:, 4 * hh + h, :] if b == 0 else SA[:, h, b - 1, :]
                                ins = mm(dst[:, h, a:e], st, src(h)[:, a:e], start=(h == 0 and b == 0), stop=(b == 8 and h == 3 and first), skip_group_check=True)
                        return ins
                    states(bank4(b0, l), lambda h: KT[:, 4 * hh + h, tk], 0, True).then_inc(s["ks_done"], 1)
                    pe.wait_ge(s["kst_ready"], hh + 1)
                    for h in range(4):
                        ins = tr(bank4(b0 + 1, 128)[0:l, h, :], w[bD][:, h, 0:l], 128)
                    ins.then_inc(s["kst_done"], 1)
                if c:
                    pe.wait_ge(s["r_ready"], i - 1)
                for h in range(4):
                    rhs = w[bE][0:l, h, :] if c else V[0:l, 0, 4 * hh + h, :]
                    ins = mm(bank4(b0 + 1, 128)[0:l, h, :], w[bY][0:l, h, 0:l], rhs, start=True, stop=True)
                ins.then_inc(s["vn_done"], 1)
                pe.wait_ge(s["vn_ready"], i + 1)
                pe.wait_ge(s["at_ready"], i + 1)
                pe.wait_ge(s["qe_ready"], i + 1)
                o = bank4(b0 + 2, l)
                if c == 2:
                    states(o, lambda h: w[bEG][:, h, 0:l], 0, False)
                for h in range(4):
                    if c == 1:
                        mm(o[:, h, :], S[:, 4 * hh + h, :], w[bEG][:, h, 0:l], start=True, stop=False)
                    ins = mm(o[:, h, :], w[bDT][0:l, h, :], w[bAT][0:l, h, 0:l], start=(c == 0), stop=True, skip_group_check=(c == 2))
                ins.then_inc(s["o_done"], 1)
                for h in range(4):
                    if c < 2:
                        lhs = Kd[0:l, c, 4 * hh + h, :]
                    else:
                        pe.wait_ge(s["kdm_ready"], 4 * hh + h + 1)
                        lhs = KDM[hh][h % 2][0:l, 0, :]
                        if h == 0:
                            pe.wait_ge(s["oT_ready"], i + 1)
                    ins = mm(bank4(b0 + 3, 128)[:, h, :], lhs, w[bDT][0:l, h, :], start=True, stop=True)
                    if h == 3:
                        ins.then_inc(s["ds_done"], 1)
                    if c == 2:
                        hd = 4 * hh + h
                        if hd >= 2:
                            pe.wait_ge(s["su_ready"], hd - 1)
                        else:
                            pe.wait_ge(s["y4_ready"], 6)
                        for b in range(8):
                            ins = mm(bank4(4 * (hd % 2) + b // 4, 128)[:, b % 4, :], KDM[hh][h % 2][0:l, 1 + b, :], w[bDT][0:l, h, :], start=True, stop=True)
                        ins.then_inc(s["su_done"], 1)

    ctx.close()


def gla(k):
    nc, i_, o_ = k.nc, k.i_, k.o_
    ident, SL, SL3, U3, R03, GR, GM, ones, seg = k.ident, k.SL, k.SL3, k.U3, k.R03, k.GR, k.GM, k.ones, k.seg
    hT, psum, bank4, unit_done, lrT = k.hT, k.psum, k.bank4, k.unit_done, k.lrT
    QK = k.carve(0, 8 * NT, 8, NT)
    V = k.carve(2432, 3072, 3, D)
    Kd = k.carve(5504, 1536, 3, 512)
    LG = k.carve(7040, 1536, 3, 512)
    EX = [k.carve(8576 + 768 * p, 768, 6, 128) for p in range(2)]
    QP = [k.carve(10112 + 640 * p, 640, 5, 128) for p in range(2)]
    KP = [k.carve(11392 + 512 * p, 512, 4, 128) for p in range(2)]
    AM = [k.carve(12416 + 512 * p, 512, 4, 128) for p in range(2)]
    AT = [k.carve(13440 + 128 * p, 128) for p in range(2)]
    S = k.carve(13696, 1024, HB, 256)
    SS = [k.carve(14720 + 2048 * p, 2048, 8, 256) for p in range(2)]
    KM = [k.carve(18816 + 1152 * p, 1152, 9, 128) for p in range(2)]
    UP = k.carve(21120, 512)
    GB = k.carve(21632, 512)
    TL = [k.carve(22144 + 512 * p, 512) for p in range(2)]
    s = named(nc, "gla", """up_in qk_ready v_ready lg_done abs_ready soft_ready lg_ready kb_done kd_done kdec_ready kd_ready
        ex_done ex_ready q_ready kp_ready pair_done am_ready at_ready o_done oT_ready ds_done s_ready
        ss_in0 ss_in1 ss_out sp_out km_ready su_done su_ready act_c dve_c""")
    ctx = ExitStack()
    block = ctx.enter_context(nc.Block())
    ss_in = (s["ss_in0"], s["ss_in1"])
    SC3 = 3 * HB

    @block.sync
    def _(sp):
        sp.dma_start(UP[0:16, :], i_["gla_gate_up"][0]).then_inc(s["up_in"], 16)
        sp.dma_start(GB[0:1, :], i_["gla_gate_bias"]).then_inc(s["up_in"], 16)
        for h in range(2):
            sp.dma_start(SS[h][:, :, :], i_["state_gla"][0, :, h].rearrange("b k v -> k b v")).then_inc(ss_in[h], 16)
        for n in range(N_Z, N_Z + 8):
            k.load_w(sp, n)
        for h in range(HB):
            sp.wait_ge(s["su_ready"], 8 * h + 8)
            sp.dma_start(o_["sg_s"][0, :, h].rearrange("b k v -> k b v"), SS[h % 2][:, :, :]).then_inc(s["ss_out"], 16)
            if h < 2:
                sp.wait_ge(s["ss_out"], 16 * (h + 1))
                sp.dma_start(SS[h][:, :, :], i_["state_gla"][0, :, h + 2].rearrange("b k v -> k b v")).then_inc(ss_in[h], 16)
        sp.wait_ge(s["s_ready"], SC3)
        sp.dma_start(o_["sg_p"][0, 0].rearrange("h k v -> k h v"), S[:, :, :]).then_inc(s["sp_out"], 16)
        sp.wait_ge(s["ss_out"], 16 * HB)
        sp.wait_ge(s["sp_out"], 16)

    @block.gpsimd
    def _(pl):
        for c in range(3):
            l = L[c]
            for h in range(HB):
                i = HB * c + h
                p = i % 2
                pl.wait_ge(s["ex_ready"], i + 1)
                if i >= 2:
                    pl.wait_ge(s["pair_done"], i - 1)
                kk = QK[:, 4 + h, T0[c]:T0[c] + l]
                if c < 2:
                    nc.gpsimd.tensor_tensor(KP[p][:, :, :], bc_mid(kk, 4), EX[p][:, 2:6, :], ALU.mult).then_inc(s["kp_ready"], 1)
                else:
                    nc.gpsimd.tensor_tensor(KP[p][:, 3, 0:l], kk, EX[p][:, 5, 0:l], ALU.mult).then_inc(s["kp_ready"], 1)
                    pl.wait_ge(s["kd_ready"], 3)
                    if h >= 2:
                        pl.wait_ge(s["su_done"], 8 * (h - 1))
                    nc.gpsimd.tensor_tensor(KM[p][0:l, :, :], bc_mid(Kd[0:l, 2, 128 * h:128 * h + 128], 9), bc_last(seg[0:l, :], 128),
                                            ALU.mult).then_inc(s["km_ready"], 1)

    def out(act, i):
        c, h = divmod(i, HB)
        act.wait_ge(s["o_done"], i + 1)
        nc.scalar.activation(QK[:, h::4, T0[c]:T0[c] + L[c]], bank4(4 * (i % 2) + 3)[:, 0:2, 0:L[c]], ACT.Copy).then_inc(s["oT_ready"], 1)

    @block.scalar
    def _(act):
        link = Chain(act, s["act_c"])
        base = units(N_QB)
        for b in range(8):
            act.wait_ge(unit_done, base + b + 1)
            nc.scalar.activation(QK[:, b, :], psum[b % 4][:, 0:NT], ACT.Copy, scale=128 ** -0.5 if b < 4 else 1.0).then_inc(s["qk_ready"], 1)
        for c in range(3):
            l = L[c]
            act.wait_ge(s["lg_done"], c + 1)
            t = TL[c % 2][0:l, :]
            if c == 2:
                act.wait_ge(s["lg_ready"], 1)
            link(nc.scalar.activation(t, psum[4 + c][0:l, :], ACT.Abs))
            link(nc.scalar.activation(t, t, ACT.Exp, scale=-1.0))
            nc.scalar.activation(t, t, ACT.Ln, bias=1.0).then_inc(s["soft_ready"], 1)
        for u in range(12):
            q, c = divmod(u, 3)
            act.wait_ge(unit_done, base + 8 + u + 1)
            nc.scalar.activation(V[0:L[c], c, 256 * q:256 * q + 256], psum[u % 4][0:L[c], 0:256], ACT.Copy).then_inc(s["v_ready"], 1)
        for c in range(3):
            l = L[c]
            act.wait_ge(s["kd_done"], c + 1)
            if c == 2:
                act.wait_ge(s["kd_ready"], 1)
            nc.scalar.activation(TL[c % 2][0:l, :], psum[4 + c % 2][0:l, :], ACT.Exp, scale=1 / TAU).then_inc(s["kdec_ready"], 1)
        for c in range(3):
            l = L[c]
            for h in range(HB):
                i = HB * c + h
                p = i % 2
                act.wait_ge(s["ex_done"], i + 1)
                if i >= 2:
                    act.wait_ge(s["q_ready"], i - 1)
                    act.wait_ge(s["kp_ready"], i - 1)
                    act.wait_ge(s["s_ready"], i - 1)
                if c == 2 and h >= 2:
                    act.wait_ge(s["su_ready"], 8 * (h - 1))
                a, b = bank4(4 * p), bank4(4 * p + 1)
                if c < 2:
                    nc.scalar.activation(EX[p][:, 0:4, :], a, ACT.Exp, scale=1 / TAU)
                    nc.scalar.activation(EX[p][:, 4, :], b[:, 0, :], ACT.Exp, scale=1 / TAU)
                    nc.scalar.activation(EX[p][:, 5, :], a[:, 1, :], ACT.Exp, scale=-1 / TAU).then_inc(s["ex_ready"], 1)
                else:
                    nc.scalar.activation(EX[p][:, 0:2, 0:l], a[:, 0:2, 0:l], ACT.Exp, scale=1 / TAU)
                    nc.scalar.activation(EX[p][:, 5, 0:l], a[:, 1, 0:l], ACT.Exp, scale=-1 / TAU).then_inc(s["ex_ready"], 1)
                if i:
                    out(act, i - 1)
        out(act, SC3 - 1)

    @block.vector
    def _(dve):
        link = Chain(dve, s["dve_c"])
        for c in range(3):
            l = L[c]
            dve.wait_ge(s["soft_ready"], c + 1)
            nc.vector.scalar_tensor_tensor(LG[0:l, c, :], psum[4 + c][0:l, :], 0.0, TL[c % 2][0:l, :], ALU.min, ALU.subtract).then_inc(s["lg_ready"], 1)
        for c in range(3):
            l = L[c]
            dve.wait_ge(s["kb_done"], c + 1)
            dve.wait_ge(s["kdec_ready"], c + 1)
            nc.vector.tensor_tensor(Kd[0:l, c, :], psum[6 + c % 2][0:l, :], TL[c % 2][0:l, :], ALU.mult).then_inc(s["kd_ready"], 1)

        def state(i):
            c, h = divmod(i, HB)
            p = i % 2
            e = EX[p][:, 0, (TAIL if c == 2 else 128) - 1:][:, 0:1]
            dve.wait_ge(s["ds_done"], i + 1)
            d = psum[4 * p + 2][:, 0:256]
            if c == 0:
                nc.vector.tensor_copy(S[:, h, :], d).then_inc(s["s_ready"], 1)
            else:
                nc.vector.scalar_tensor_tensor(S[:, h, :], S[:, h, :], e, d, ALU.mult, ALU.add).then_inc(s["s_ready"], 1)
            if c == 2:
                for b in range(8):
                    dve.wait_ge(s["su_done"], 8 * h + b + 1)
                    x = TAIL + TS * b + TS - 1
                    nc.vector.scalar_tensor_tensor(SS[h % 2][:, b, :], SS[h % 2][:, b, :], EX[p][:, 0, x:x + 1],
                                                   psum[4 * p + b % 2][:, 0:256], ALU.mult, ALU.add).then_inc(s["su_ready"], 1)
        for c in range(3):
            l = L[c]
            for h in range(HB):
                i = HB * c + h
                p = i % 2
                q = QK[:, h, T0[c]:T0[c] + l]
                dve.wait_ge(s["ex_ready"], i + 1)
                if i >= 2:
                    dve.wait_ge(s["o_done"], i - 1)
                if c < 2:
                    nc.vector.tensor_tensor(QP[p][:, :, :], bc_mid(q, 5), EX[p][:, 0:5, :], ALU.mult).then_inc(s["q_ready"], 1)
                else:
                    nc.vector.tensor_tensor(QP[p][:, 0:2, 0:l], bc_mid(q, 2), EX[p][:, 0:2, 0:l], ALU.mult).then_inc(s["q_ready"], 1)
                dve.wait_ge(s["pair_done"], i + 1)
                if c < 2:
                    link(nc.vector.tensor_tensor(AM[p][:, :, :], bank4(4 * p + 2), GM[:, :, :], ALU.mult))
                    nc.vector.tensor_reduce(AT[p][:, :], AM[p][:, :, :].rearrange("p a t -> p t a"), AX.X, ALU.add).then_inc(s["at_ready"], 1)
                else:
                    nc.vector.tensor_tensor(AT[p][0:l, 0:l], bank4(4 * p + 2)[0:l, 0, 0:l], U3[0:l, 0:l], ALU.mult).then_inc(s["at_ready"], 1)
                state(i)

    @block.tensor
    def _(pe):
        mm = nc.tensor.matmul
        for b in range(8):
            if b >= 4:
                pe.wait_ge(s["qk_ready"], b - 3)
            k.block_of_slot(pe, N_QB + b // 2, b % 2, b % 4)
        pe.wait_ge(s["up_in"], 32)
        for c in range(3):
            l = L[c]
            mm(psum[4 + c][0:l, :], lrT[:, T0[c]:T0[c] + l], UP[0:16, :], start=True, stop=False)
            mm(psum[4 + c][0:l, :], ones[0:1, 0:l], GB[0:1, :], start=False, stop=True).then_inc(s["lg_done"], 1)
        for u in range(12):
            q, c = divmod(u, 3)
            n = N_VB + q
            if u < 4:
                pe.wait_ge(s["qk_ready"], 5 + u)
            else:
                pe.wait_ge(s["v_ready"], u - 3)
            k.arrived(pe, n)
            for j in range(KB):
                ins = mm(psum[u % 4][0:L[c], 0:256], hT[:, j, T0[c]:T0[c] + L[c]], k.slot8(n)[:, j, :], start=(j == 0), stop=(j == KB - 1))
            ins.then_inc(unit_done, 1)
        pe.wait_ge(s["lg_ready"], 3)
        for c in range(3):
            l = L[c]
            if c == 2:
                pe.wait_ge(s["kd_ready"], 1)
            for h in range(HB):
                ins = nc.tensor.transpose(bank4(6 + c % 2)[0:l, h, :], QK[:, 4 + h, T0[c]:T0[c] + l], ident)
            ins.then_inc(s["kb_done"], 1)
            mm(psum[4 + c % 2][0:l, :], (SL if c < 2 else SL3)[0:l, 0:l], LG[0:l, c, :], start=True, stop=True).then_inc(s["kd_done"], 1)

        def exps(i):
            c, h = divmod(i, HB)
            l, p = L[c], i % 2
            lg = LG[0:l, c, 128 * h:128 * h + 128]
            if c < 2:
                mm(psum[4 * p][:, :], lg, GR[:, 0:4, :], start=True, stop=True)
                mm(bank4(4 * p + 1)[:, 0, :], lg, GR[:, 4, :], start=True, stop=True).then_inc(s["ex_done"], 1)
            else:
                mm(bank4(4 * p)[:, 0, 0:l], lg, U3[0:l, 0:l], start=True, stop=True)
                mm(bank4(4 * p)[:, 1, 0:l], lg, R03[0:l, 0:l], start=True, stop=True).then_inc(s["ex_done"], 1)

        pe.wait_ge(s["v_ready"], 12)
        pe.wait_ge(s["kd_ready"], 3)
        pe.wait_ge(s["kdec_ready"], 3)
        exps(0)
        for i in range(SC3):
            c, h = divmod(i, HB)
            l, p = L[c], i % 2
            tk = slice(T0[c], T0[c] + l)
            if c < 2 and i + 1 < SC3:
                if i >= 1:
                    pe.wait_ge(s["ex_ready"], i)
                exps(i + 1)
            pe.wait_ge(s["q_ready"], i + 1)
            pe.wait_ge(s["kp_ready"], i + 1)
            if i >= 2:
                pe.wait_ge(s["s_ready"], i - 1)
            if c < 2:
                for r, (kx, qx) in enumerate(((3, 1), (0, 2), (1, 3), (2, 4))):
                    ins = mm(bank4(4 * p + 2)[:, r, :], KP[p][:, kx, :], QP[p][:, qx, :], start=True, stop=True)
            else:
                ins = mm(bank4(4 * p + 2)[0:l, 0, 0:l], KP[p][:, 3, 0:l], QP[p][:, 1, 0:l], start=True, stop=True)
            ins.then_inc(s["pair_done"], 1)
            if i >= 2:
                pe.wait_ge(s["oT_ready"], i - 1)
            o = bank4(4 * p + 3)
            if c == 2:
                pe.wait_ge(ss_in[h % 2], 16 * (h // 2 + 1))
                for e in range(2):
                    for b in range(9):
                        t0, t1 = (0, TAIL) if b == 0 else (TAIL + TS * (b - 1), TAIL + TS * b)
                        st = S[:, h, :] if b == 0 else SS[h % 2][:, b - 1, :]
                        mm(o[:, e, t0:t1], st[:, 128 * e:128 * e + 128], QP[p][:, 0, t0:t1], start=(e == 0 and b == 0), stop=False, skip_group_check=True)
            pe.wait_ge(s["at_ready"], i + 1)
            for e in range(2):
                if c == 1:
                    pe.wait_ge(s["s_ready"], i - 3)
                    mm(o[:, e, 0:l], S[:, h, 128 * e:128 * e + 128], QP[p][:, 0, 0:l], start=True, stop=False)
                ins = mm(o[:, e, 0:l], V[0:l, c, 256 * h + 128 * e:256 * h + 128 * e + 128], AT[p][0:l, 0:l],
                         start=(c == 0), stop=True, skip_group_check=(c == 2))
            ins.then_inc(s["o_done"], 1)
            if c == 2:
                pe.wait_ge(s["km_ready"], h + 1)
            mm(psum[4 * p + 2][:, 0:256], KM[p][0:l, 0, :] if c == 2 else Kd[0:l, c, 128 * h:128 * h + 128],
               V[0:l, c, 256 * h:256 * h + 256], start=True, stop=True).then_inc(s["ds_done"], 1)
            if c == 2:
                pe.wait_ge(s["ex_ready"], i + 1)
                for b in range(8):
                    if b >= 2:
                        pe.wait_ge(s["su_ready"], 8 * h + b - 1)
                    mm(psum[4 * p + b % 2][:, 0:256], KM[p][0:l, 1 + b, :], V[0:l, 2, 256 * h:256 * h + 256], start=True, stop=True).then_inc(s["su_done"], 1)
                if i + 1 < SC3:
                    if h >= 1:
                        pe.wait_ge(s["su_ready"], 8 * h)
                    exps(i + 1)
    ctx.close()


X_AT = 17696


def merge(k):
    nc, i_, o_ = k.nc, k.i_, k.o_
    oaT, ones, psum, unit_done, epsc, na, nb = k.oaT, k.ones, k.psum, k.unit_done, k.epsc, k.na, k.nb
    obT = k.carve(0, 8 * NT, 8, NT)
    WN = k.carve(3072, D)
    WR = k.carve(4096, 288, KB, 36)
    GA = k.carve(8576, 8 * NT, 8, NT)
    GB = k.carve(11008, 8 * NT, 8, NT)
    MG = k.carve(13440, 8 * NT, 8, NT)
    ZT = k.carve(15872, 2 * NT, 2, NT)
    RS = k.carve(15872 + 2 * NT, 2 * NT, 2, NT)
    assert 15872 + 4 * NT <= X_AT
    X = k.carve(X_AT, 3072, 3, D)
    SQ = [k.carve(X_AT + 3072 + 2 * NT * p, 2 * NT, 2, NT) for p in range(2)]
    s = named(nc, "merge", """x_in par_in sq_ready sum_done rs_ready on_ready silu_ready gated gate_ready ya_ready yb_ready mg_ready
        wo_done x1_ready act_c""")
    ctx = ExitStack()
    block = ctx.enter_context(nc.Block())
    base = units(N_Z)

    def ob(j):
        return obT[:, j // 2 + 4 * (j % 2), :]

    @block.sync
    def _(sp):
        k.load_x(sp, X, s["x_in"])
        sp.dma_start(WN, i_["norm_final"].partition_broadcast(128)).then_inc(s["par_in"], 16)
        sp.dma_start(WR[:, :, 0:4], i_["router_group_w"][0].rearrange("(p j) g -> p j g", j=KB)).then_inc(s["par_in"], 16)
        sp.dma_start(WR[:, :, 4:36], i_["router_expert_w"][0].rearrange("(p j) e -> p j e", j=KB)).then_inc(s["par_in"], 16)
        for n in range(N_Z + 8, N_PRE):
            k.load_w(sp, n)
        sp.wait_ge(s["par_in"], 48)

    @block.gpsimd
    def _(pl):
        for h in range(12):
            if h >= 2:
                pl.wait_ge(s["sum_done"], h - 1)
            if h < 8:
                nc.gpsimd.tensor_tensor(SQ[h % 2][:, 0, :], oaT[:, h, :], oaT[:, h, :], ALU.mult).then_inc(s["sq_ready"], 1)
            else:
                v = obT[:, h - 8::4, :]
                nc.gpsimd.tensor_tensor(SQ[h % 2][:, :, :], v, v, ALU.mult).then_inc(s["sq_ready"], 1)
        for b in range(8):
            pl.wait_ge(s["yb_ready"], b + 1)
            nc.gpsimd.tensor_tensor(MG[:, b, :], MG[:, b, :], GB[:, b, :], ALU.add).then_inc(s["mg_ready"], 1)

    @block.scalar
    def _(act):
        link = Chain(act, s["act_c"])
        for h in range(12):
            act.wait_ge(s["sum_done"], h + 1)
            if h >= 2:
                act.wait_ge(s["on_ready"], h - 1 if h - 1 <= 8 else 8 + 2 * (h - 9))
            link(nc.scalar.activation(RS[:, h % 2, :], psum[4 + h % 4][:, 0:NT], ACT.Ln, scale=1 / 128 if h < 8 else 1 / 256, bias=epsc))
            nc.scalar.activation(RS[:, h % 2, :], RS[:, h % 2, :], ACT.Exp, scale=-0.5).then_inc(s["rs_ready"], 1)
        for u in range(16):
            act.wait_ge(unit_done, base + u + 1)
            if u >= 2:
                act.wait_ge(s["gated"], u - 1)
            nc.scalar.activation(ZT[:, u % 2, :], psum[u % 4][:, 0:NT], ACT.Silu).then_inc(s["silu_ready"], 1)
        for u in range(16, 32):
            act.wait_ge(unit_done, base + u + 1)
            nc.scalar.activation((GA if u < 24 else GB)[:, u % 8, :], psum[u % 4][:, 0:NT], ACT.Sigmoid).then_inc(s["gate_ready"], 1)

    @block.vector
    def _(dve):
        for h in range(12):
            dve.wait_ge(s["rs_ready"], h + 1)
            if h < 8:
                nc.vector.scalar_tensor_tensor(oaT[:, h, :], oaT[:, h, :], na, RS[:, h % 2, :], ALU.mult, ALU.mult).then_inc(s["on_ready"], 1)
            else:
                for e in range(2):
                    v = obT[:, h - 8 + 4 * e, :]
                    nc.vector.scalar_tensor_tensor(v, v, nb[:, e:e + 1], RS[:, h % 2, :], ALU.mult, ALU.mult).then_inc(s["on_ready"], 1)
        dve.wait_ge(s["on_ready"], 16)
        for u in range(16):
            dve.wait_ge(s["silu_ready"], u + 1)
            v = oaT[:, u, :] if u < 8 else ob(u - 8)
            nc.vector.tensor_tensor(v, v, ZT[:, u % 2, :], ALU.mult).then_inc(s["gated"], 1)
        for b in range(8):
            dve.wait_ge(unit_done, base + 32 + b + 1)
            dve.wait_ge(s["gate_ready"], b + 1)
            nc.vector.tensor_tensor(MG[:, b, :], psum[b % 4][:, 0:NT], GA[:, b, :], ALU.mult).then_inc(s["ya_ready"], 1)
        for b in range(8):
            dve.wait_ge(unit_done, base + 40 + b + 1)
            dve.wait_ge(s["gate_ready"], 8 + b + 1)
            dve.wait_ge(s["ya_ready"], b + 1)
            nc.vector.tensor_tensor(GB[:, b, :], psum[b % 4][:, 0:NT], GB[:, b, :], ALU.mult).then_inc(s["yb_ready"], 1)
        dve.wait_ge(s["x_in"], 80)
        for u in range(12):
            q, c = divmod(u, 3)
            dve.wait_ge(unit_done, base + 48 + u + 1)
            x = X[0:L[c], c, 256 * q:256 * q + 256]
            nc.vector.tensor_tensor(x, x, psum[4 + u % 4][0:L[c], 0:256], ALU.add).then_inc(s["x1_ready"], 1)

    @block.tensor
    def _(pe):
        mm = nc.tensor.matmul
        for h in range(12):
            pe.wait_ge(s["sq_ready"], h + 1)
            if h >= 4:
                pe.wait_ge(s["rs_ready"], h - 3)
            if h < 8:
                ins = mm(psum[4 + h % 4][:, 0:NT], ones[:, :], SQ[h % 2][:, 0, :], start=True, stop=True)
            else:
                mm(psum[4 + h % 4][:, 0:NT], ones[:, :], SQ[h % 2][:, 0, :], start=True, stop=False)
                ins = mm(psum[4 + h % 4][:, 0:NT], ones[:, :], SQ[h % 2][:, 1, :], start=False, stop=True)
            ins.then_inc(s["sum_done"], 1)
            if h in (3, 5, 7, 9):
                u = (h - 3) // 2
                k.block_of_slot(pe, N_Z + u // 2, u % 2, u)
        for u in range(4, 48):
            if u - 4 < 16:
                pe.wait_ge(s["silu_ready"], u - 3)
            elif u - 4 < 32:
                pe.wait_ge(s["gate_ready"], u - 19)
            elif u - 4 < 40:
                pe.wait_ge(s["ya_ready"], u - 35)
            else:
                pe.wait_ge(s["yb_ready"], u - 43)
            moving = None
            if u == 32:
                pe.wait_ge(s["gated"], 8)
            if u == 40:
                pe.wait_ge(s["gated"], 16)
            if 32 <= u < 40:
                moving = lambda j: oaT[:, j, :]
            elif u >= 40:
                moving = ob
            k.block_of_slot(pe, N_Z + u // 2, u % 2, u % 4, moving)
        for u in range(12):
            q, c = divmod(u, 3)
            n = N_WO + q
            k.arrived(pe, n)
            if u >= 4:
                pe.wait_ge(s["x1_ready"], u - 3)
            for j in range(KB):
                if u == 0:
                    pe.wait_ge(s["mg_ready"], j + 1)
                ins = mm(psum[4 + u % 4][0:L[c], 0:256], MG[:, j, T0[c]:T0[c] + L[c]], k.slot8(n)[:, j, :], start=(j == 0), stop=(j == KB - 1))
            ins.then_inc(unit_done, 1)
    ctx.close()


def experts(k):
    nc, i_, o_ = k.nc, k.i_, k.o_
    ident, SU, ones, hT, psum, bank4, epsc, nf, rbias = k.ident, k.SU, k.ones, k.hT, k.psum, k.bank4, k.epsc, k.nf, k.rbias
    X = k.carve(X_AT, 3072, 3, D)
    XN = k.carve(0, 3072, 3, D)
    WN = k.carve(3072, D)
    WR = k.carve(4096, 288, KB, 36)
    XG = k.carve(4384, 1024, KB, 128)
    P = k.carve(5408, 384, 3, 128)
    PT = k.carve(5792, NT)
    SIL = [k.carve(6096 + 256 * p, 256) for p in range(2)]
    H = [k.carve(6608 + 256 * p, 256) for p in range(2)]
    HX = [k.carve(7120 + 256 * p, 256, 2, 128) for p in range(2)]
    OG = k.carve(7632, 1024)
    IO = k.carve(8656, 128)
    LT = k.carve(8784, 108, 3, 36)
    TE = k.carve(8892, 96)
    WT = k.carve(8988, 1)
    DESC = k.carve(8989, 8)
    at = [9000]

    def take(n, *dims):
        at[0] += n
        return k.carve(at[0] - n, n, *dims)
    gmax, gkey, gsum, pg, a1, a2, b1, b2, w1, w2, key, ss, rstd, tcount, tmax = (take(3) for _ in range(15))
    eq4, ky4, oh4, ex4 = (take(12, 3, 4) for _ in range(4))
    le, eq8, ky8, oh1, oh2, comb = (take(24, 3, 8) for _ in range(6))
    CMB = take(8)
    IOI = k.carve(9600, 128).bitcast(I32)
    TE4 = TE.rearrange("p (c g e) -> p c g e", g=4, e=8)
    s = named(nc, "experts", """io_ready rstd_ready xn_ready xT_done xT_ready rt_done lt_ready d4_ready ex4_ready d2_ready w2_ready oh_ready
        rank_done comb_ready cnt_ready p_ready pt_done pt_ready xg_done xgT_ready gu_done sil_ready h_ready hx_done hx_ready
        dn_done og_ready sc_done y_added x2_ready r3_ready key_back fin_ready out_done act_c dve_c pool_c""")
    ctx = ExitStack()
    block = ctx.enter_context(nc.Block())
    PASSES = 3
    assert PASSES * CAP >= NT

    def expert_load(sp, v, g, p, m):
        e, kind = divmod(m, 3)
        before = m - SLOTS
        if before >= 0:
            eb, kb = divmod(before, 3)
            sp.wait_ge(s["dn_done"] if kb == 2 else s["gu_done"], v * EPG + (eb + 1))
        elif isinstance(v, int) and v == 0:
            sp.wait_ge(k.unit_done, units(N_PRE + before + 1))
        else:
            eb, kb = divmod(before + PER_GROUP, 3)
            sp.wait_ge(s["dn_done"] if kb == 2 else s["gu_done"], (v - 1) * EPG + (eb + 1))
        w = i_[("expert_w_gate", "expert_w_up", "expert_w_down")[kind]][0][g * EPG + e]
        sp.dma_start(k.ring[:, m % SLOTS, :], w.rearrange("(p j) c -> p (j c)", p=128)).then_inc(k.ring_in[m % SLOTS], 16)

    def slot_wait(pe, v, m):
        pe.wait_ge(k.ring_in[m % SLOTS], v * 48 + 16 * (N_PRE // SLOTS + 1 + m // SLOTS))

    def passes(eng, body):
        body(0)
        eng.wait_ge(s["cnt_ready"], 1)
        count = eng.value_load(k.cnti[0:1, 0:1], min_val=0, max_val=NT)
        for p in range(1, PASSES):
            with eng.If(count > CAP * p):
                body(p)

    @block.sync
    def _(sp):
        def one_pass(p):
            for m in range(SLOTS):
                expert_load(sp, NG * p, 0, p, m)
            with sp.Fori(0, NG - 1) as g:
                v = g + NG * p
                for m in range(SLOTS, PER_GROUP):
                    expert_load(sp, v, g, p, m)
                for m in range(SLOTS):
                    expert_load(sp, v + 1, g + 1, p, m)
            for m in range(SLOTS, PER_GROUP):
                expert_load(sp, NG * p + NG - 1, NG - 1, p, m)
        passes(sp, one_pass)
        yp, ys = o_["y_p"][0], o_["y_s"].rearrange("b t d -> (b t) d")
        for c in range(3):
            sp.wait_ge(s["fin_ready"], c + 1)
            if c == 0:
                sp.dma_start(yp[0:112, :], X[META:128, 0, :]).then_inc(s["out_done"], 16)
            elif c == 1:
                sp.dma_start(yp[112:240, :], X[:, 1, :]).then_inc(s["out_done"], 16)
            else:
                sp.dma_start(yp[240:256, :], X[0:TAIL, 2, :]).then_inc(s["out_done"], 16)
                sp.dma_start(ys, X[TAIL:L[2], 2, :]).then_inc(s["out_done"], 16)
        sp.wait_ge(s["out_done"], 64)

    @block.gpsimd
    def _(pl):
        link = Chain(pl, s["pool_c"])
        link(nc.gpsimd.iota(IOI, [[1, 128]], base=0, channel_multiplier=0))
        for e in range(8):
            nc.gpsimd.memset(DESC[:, e:e + 1], float(8 - e))
        nc.gpsimd.memset(LT[:, :, :], 0.0)
        link(nc.gpsimd.tensor_copy(IO, IOI))
        pl.drain().then_inc(s["io_ready"], 1)

    @block.scalar
    def _(act):
        link = Chain(act, s["act_c"])

        def inverse_rms(signal):
            for c in range(3):
                l = L[c]
                link(nc.scalar.activation(XN[0:l, c, :], X[0:l, c, :], ACT.Square, accum_out=ss[0:l, c:c + 1]))
                link(nc.scalar.activation(ss[0:l, c:c + 1], ss[0:l, c:c + 1], ACT.Ln, scale=1 / D, bias=epsc[0:l, :]))
                nc.scalar.activation(rstd[0:l, c:c + 1], ss[0:l, c:c + 1], ACT.Exp, scale=-0.5).then_inc(signal, 1)
        inverse_rms(s["rstd_ready"])
        act.wait_ge(s["d4_ready"], 1)
        nc.scalar.activation(ex4[:, :, :], ex4[:, :, :], ACT.Exp).then_inc(s["ex4_ready"], 1)
        act.wait_ge(s["d2_ready"], 1)
        nc.scalar.activation(w2[:, :], w2[:, :], ACT.Exp).then_inc(s["w2_ready"], 1)

        def one_pass(p):
            with act.Fori(0, NG) as g:
                v = g + NG * p
                act.wait_ge(s["pt_done"], v + 1)
                link_loop = None
                nc.scalar.activation(CMB[:, :], psum[3][:, 400:408], ACT.Copy)
                nc.scalar.activation(PT[:, :], psum[3][:, 0:NT], ACT.Copy).then_inc(s["pt_ready"], 1)
                for e in range(EPG + 1):
                    if e < EPG:
                        act.wait_ge(s["gu_done"], v * EPG + (e + 1))
                        if e >= 2:
                            act.wait_ge(s["h_ready"], v * EPG + (e - 1))
                        nc.scalar.activation(SIL[e % 2][:, :], psum[e % 2][:, 0:256], ACT.Silu).then_inc(s["sil_ready"], 1)
                    if e >= 1:
                        act.wait_ge(s["hx_done"], v * EPG + e)
                        if e >= 3:
                            act.wait_ge(s["dn_done"], v * EPG + (e - 2))
                        nc.scalar.activation(HX[(e - 1) % 2][:, :, :], psum[2 + (e - 1) % 2][:, 0:256].rearrange("p (j t) -> p j t", j=2),
                                             ACT.Copy).then_inc(s["hx_ready"], 1)
                act.wait_ge(s["dn_done"], v * EPG + EPG)
                nc.scalar.activation(OG[:, 0:512], psum[4][:, :], ACT.Copy)
                nc.scalar.activation(OG[:, 512:1024], psum[5][:, :], ACT.Copy).then_inc(s["og_ready"], 1)
        passes(act, one_pass)
        act.wait_ge(s["x2_ready"], 1)
        inverse_rms(s["r3_ready"])

    @block.vector
    def _(dve):
        V = nc.vector
        link = Chain(dve, s["dve_c"])
        for c in range(3):
            l = L[c]
            dve.wait_ge(s["rstd_ready"], c + 1)
            V.tensor_scalar(XN[0:l, c, :], X[0:l, c, :], rstd[0:l, c:c + 1], None, ALU.mult).then_inc(s["xn_ready"], 1)
        for j in range(KB):
            dve.wait_ge(s["xT_done"], j + 1)
            V.tensor_scalar(hT[:, j, :], psum[j % 4][:, 0:NT], nf[:, j:j + 1], None, ALU.mult).then_inc(s["xT_ready"], 1)
        dve.wait_ge(s["io_ready"], 1)
        for c in range(3):
            dve.wait_ge(s["rt_done"], c + 1)
            link(V.tensor_copy(LT[0:L[c], c, :], psum[4 + c][0:L[c], 0:36]))

        def first_of_max(v, n, out_max, eq, ky, oh, top):
            link(V.tensor_reduce(out_max, v, AX.X, ALU.max))
            link(V.tensor_tensor(eq, v, bc_last(out_max, n), ALU.is_equal))
            link(V.tensor_tensor(ky, eq, bc_mid(DESC[:, 8 - n:8], 3), ALU.mult))
            link(V.tensor_reduce(top, ky, AX.X, ALU.max))
            link(V.tensor_tensor(oh, ky, bc_last(top, n), ALU.is_equal))
        lg = LT[:, :, 0:4]
        first_of_max(lg, 4, gmax, eq4, ky4, oh4, gkey)
        dve.drain().then_inc(s["oh_ready"], 1)
        V.tensor_tensor(ex4, lg, bc_last(gmax, 4), ALU.subtract).then_inc(s["d4_ready"], 1)
        link(V.tensor_tensor(TE4, LT[:, :, 4:36].rearrange("p c (g e) -> p c g e", g=4), bc_last(oh4, 8), ALU.mult))
        link(V.tensor_reduce(le, TE4.rearrange("p c g e -> p c e g"), AX.X, ALU.add))
        first_of_max(le, 8, a1, eq8, ky8, oh1, b1)
        link(V.scalar_tensor_tensor(le, oh1, -1e30, le, ALU.mult, ALU.add))
        first_of_max(le, 8, a2, eq8, ky8, oh2, b2)
        V.tensor_tensor(w2, a2, a1, ALU.subtract).then_inc(s["d2_ready"], 1)
        dve.wait_ge(s["ex4_ready"], 1)
        link(V.tensor_reduce(gsum, ex4, AX.X, ALU.add))
        link(V.reciprocal(pg, gsum))
        dve.wait_ge(s["w2_ready"], 1)
        link(V.tensor_scalar(w1, w2, 1.0, None, ALU.add))
        link(V.reciprocal(w1, w1))
        link(V.tensor_tensor(w1, w1, pg, ALU.mult))
        link(V.tensor_tensor(w2, w2, w1, ALU.mult))
        link(V.tensor_tensor(comb, oh1, bc_last(w1, 8), ALU.mult))
        link(V.tensor_tensor(oh2, oh2, bc_last(w2, 8), ALU.mult))
        V.tensor_tensor(comb, comb, oh2, ALU.add).then_inc(s["comb_ready"], 1)
        dve.wait_ge(s["rank_done"], 4)
        link(V.tensor_scalar(tmax, gkey, -1024.0, 4096.0, ALU.mult, ALU.add))
        for c in range(3):
            l = L[c]
            link(V.tensor_tensor(ky4[0:l, c, :], psum[4 + c][0:l, 0:4], oh4[0:l, c, :], ALU.mult))
            link(V.tensor_reduce(key[0:l, c:c + 1], ky4[0:l, c, :], AX.X, ALU.add))
            link(V.tensor_tensor(key[0:l, c:c + 1], key[0:l, c:c + 1], tmax[0:l, c:c + 1], ALU.add))
        link(V.tensor_reduce(tcount[:, 0:1], psum[7][:, 0:4], AX.X, ALU.max))
        V.tensor_copy(k.cnti[:, :], tcount[:, 0:1]).then_inc(s["cnt_ready"], 1)

        def one_pass(p):
            if p:
                dve.wait_ge(s["key_back"], p)
            with dve.Fori(0, NG) as g:
                v = g + NG * p
                for c in range(3):
                    l = L[c]
                    ins = V.tensor_scalar(P[0:l, c, :], IO[0:l, :], key[0:l, c:c + 1], None, ALU.is_equal)
                ins.then_inc(s["p_ready"], 1)
                dve.wait_ge(s["p_ready"], v + 1)
                for c in range(3):
                    V.tensor_scalar(key[0:L[c], c:c + 1], key[0:L[c], c:c + 1], -1024.0, None, ALU.add)
                for q in range(2):
                    dve.wait_ge(s["xg_done"], v * 2 + (q + 1))
                    V.tensor_tensor(XG[:, 4 * q:4 * q + 4, :], bank4(6 + q), bc_last(nf[:, 4 * q:4 * q + 4], 128), ALU.mult).then_inc(s["xgT_ready"], 1)
                dve.wait_ge(s["pt_ready"], v + 1)
                for e in range(EPG):
                    dve.wait_ge(s["sil_ready"], v * EPG + (e + 1))
                    if e >= 2:
                        dve.wait_ge(s["hx_done"], v * EPG + (e - 1))
                    V.scalar_tensor_tensor(H[e % 2][:, :], SIL[e % 2][:, :], CMB[:, e:e + 1], psum[e % 2][:, 256:512],
                                           ALU.mult, ALU.mult).then_inc(s["h_ready"], 1)
                for q in range(6):
                    c, half = divmod(q, 2)
                    dve.wait_ge(s["sc_done"], v * 6 + (q + 1))
                    x = X[0:L[c], c, 512 * half:512 * half + 512]
                    V.tensor_tensor(x, x, psum[6 + q % 2][0:L[c], :], ALU.add).then_inc(s["y_added"], 1)
                dve.wait_ge(s["y_added"], v * 6 + 6)
            if p + 1 < PASSES:
                for c in range(3):
                    ins = V.tensor_scalar(key[0:L[c], c:c + 1], key[0:L[c], c:c + 1], 1024.0 * NG - CAP, None, ALU.add)
                ins.then_inc(s["key_back"], 1)
        passes(dve, one_pass)
        dve.drain().then_inc(s["x2_ready"], 1)
        for c in range(3):
            l = L[c]
            dve.wait_ge(s["r3_ready"], c + 1)
            V.scalar_tensor_tensor(X[0:l, c, :], X[0:l, c, :], rstd[0:l, c:c + 1], WN[0:l, :], ALU.mult, ALU.mult).then_inc(s["fin_ready"], 1)

    @block.tensor
    def _(pe):
        mm, tr = nc.tensor.matmul, nc.tensor.transpose
        for j in range(KB):
            if j >= 4:
                pe.wait_ge(s["xT_ready"], j - 3)
            for c in range(3):
                if j == 0:
                    pe.wait_ge(s["xn_ready"], c + 1)
                ins = tr(psum[j % 4][:, T0[c]:T0[c] + L[c]], XN[0:L[c], c, j::KB], ident[0:L[c], 0:L[c]])
            ins.then_inc(s["xT_done"], 1)
        pe.wait_ge(s["xT_ready"], KB)
        for c in range(3):
            l = L[c]
            for j in range(KB):
                mm(psum[4 + c][0:l, 0:36], hT[:, j, T0[c]:T0[c] + l], WR[:, j, :], start=(j == 0), stop=False)
            mm(psum[4 + c][0:l, 0:36], ones[0:1, 0:l], rbias[0:1, :], start=False, stop=True).then_inc(s["rt_done"], 1)
        pe.wait_ge(s["oh_ready"], 1)
        for c in range(3):
            l = L[c]
            ins = mm(psum[4 + c][0:l, 0:4], SU[0:l, 0:l], oh4[0:l, c, :], start=True, stop=(c == 0))
            for b in range(c):
                ins = mm(psum[4 + c][0:l, 0:4], ones[:, 0:l], oh4[:, b, :], start=False, stop=(b == c - 1))
            ins.then_inc(s["rank_done"], 1)
        for c in range(3):
            ins = mm(psum[7][:, 0:4], ones[0:L[c], :], oh4[0:L[c], c, :], start=(c == 0), stop=(c == 2))
        ins.then_inc(s["rank_done"], 1)
        pe.wait_ge(s["comb_ready"], 1)
        pe.wait_ge(s["cnt_ready"], 1)

        def one_pass(p):
            with pe.Fori(0, NG) as g:
                v = g + NG * p
                pe.wait_ge(s["p_ready"], v + 1)
                for q in range(2):
                    for j in range(4):
                        for c in range(3):
                            ins = mm(bank4(6 + q)[:, j, :], XN[0:L[c], c, 4 * q + j::KB], P[0:L[c], c, :], start=(c == 0), stop=(c == 2))
                    ins.then_inc(s["xg_done"], 1)
                for c in range(3):
                    tr(psum[3][:, T0[c]:T0[c] + L[c]], P[0:L[c], c, :], ident[0:L[c], 0:L[c]])
                for c in range(3):
                    ins = mm(psum[3][:, 400:408], P[0:L[c], c, :], comb[0:L[c], c, :], start=(c == 0), stop=(c == 2))
                ins.then_inc(s["pt_done"], 1)
                pe.wait_ge(s["xgT_ready"], v * 2 + 2)

                def gate_up(e):
                    if e >= 2:
                        pe.wait_ge(s["h_ready"], v * EPG + (e - 1))
                    for half in range(2):
                        slot_wait(pe, v, 3 * e + half)
                        for j in range(KB):
                            ins = mm(psum[e % 2][:, 256 * half:256 * half + 256], XG[:, j, :], k.slot8(3 * e + half)[:, j, :],
                                     start=(j == 0), stop=(j == KB - 1))
                    ins.then_inc(s["gu_done"], 1)

                def turn(e):
                    pe.wait_ge(s["h_ready"], v * EPG + (e + 1))
                    if e == 1:
                        pe.wait_ge(s["pt_ready"], v + 1)
                    if e >= 2:
                        pe.wait_ge(s["hx_ready"], v * EPG + (e - 1))
                    for j in range(2):
                        ins = tr(psum[2 + e % 2][:, 128 * j:128 * j + 128], H[e % 2][:, j::2], ident)
                    ins.then_inc(s["hx_done"], 1)

                def down(e):
                    pe.wait_ge(s["hx_ready"], v * EPG + (e + 1))
                    slot_wait(pe, v, 3 * e + 2)
                    w = k.ring[:, (3 * e + 2) % SLOTS, :].rearrange("p (j c) -> p j c", j=2)
                    for j in range(2):
                        for half in range(2):
                            ins = mm(psum[4 + half][:, :], HX[e % 2][:, j, :], w[:, j, 512 * half:512 * half + 512],
                                     start=(e == 0 and j == 0), stop=(e == EPG - 1 and j == 1))
                    ins.then_inc(s["dn_done"], 1)
                gate_up(0)
                for e in range(EPG):
                    if e + 1 < EPG:
                        gate_up(e + 1)
                    turn(e)
                    down(e)
                pe.wait_ge(s["og_ready"], v + 1)
                for q in range(6):
                    c, half = divmod(q, 2)
                    if q >= 2:
                        pe.wait_ge(s["y_added"], v * 6 + (q - 1))
                    mm(psum[6 + q % 2][0:L[c], :], PT[:, T0[c]:T0[c] + L[c]], OG[:, 512 * half:512 * half + 512],
                       start=True, stop=True).then_inc(s["sc_done"], 1)
                pe.wait_ge(s["y_added"], v * 6 + 6)
        passes(pe, one_pass)
    ctx.close()


def build(nc, i_, o_):
    with ExitStack() as ctx:
        k = Core(nc, ctx, i_, o_)
        front(k)
        delta(k)
        gla(k)
        merge(k)
        experts(k)


_INS = ['x_prompt', 'x_sample', 'state_delta', 'state_conv', 'state_gla', 'meta_tokens', 'norm_mix', 'w_in',
        'conv_w', 'a_log', 'dt_bias', 'norm_a', 'gla_gate_up', 'gla_gate_bias', 'norm_b', 'w_proj_a', 'w_proj_b',
        'w_out', 'norm_ffn', 'router_group_w', 'router_group_b', 'router_expert_w', 'router_expert_b',
        'expert_w_gate', 'expert_w_up', 'expert_w_down', 'norm_final']
_OUTS = {'y_p': (1, SEQ, D), 'y_s': (NB, TS, D), 'sd_p': (1, 1, HA, 128, 128), 'conv_p': (1, 1, CW - 1, CONV),
         'sg_p': (1, 1, HB, 128, 256), 'sd_s': (1, NB, HA, 128, 128), 'conv_s': (1, NB, CW - 1, CONV),
         'sg_s': (1, NB, HB, 128, 256)}


def kernel(**inputs):
    import numpy as _np
    import concourse.bacc as _bacc
    from concourse import mybir as _mybir
    from concourse.bass_utils import run_bass_kernel_spmd as _run

    nc = _bacc.Bacc("TRN2", target_bir_lowering=False, num_devices=1)
    arrays, ins, outs = {}, {}, {}
    for name in _INS:
        a = _np.ascontiguousarray(inputs[name])
        arrays[f"in_{name}"] = a
        ins[name] = nc.dram_tensor(f"in_{name}", a.shape, _mybir.dt.from_np(a.dtype), kind="ExternalInput").ap()
    for name, shape in _OUTS.items():
        outs[name] = nc.dram_tensor(f"out_{name}", shape, _mybir.dt.float32, kind="ExternalOutput").ap()
    build(nc, ins, outs)
    r = _run(nc, [arrays], core_ids=[0])
    return tuple(r.results[0][f"out_{name}"] for name in _OUTS)
```

```python
from contextlib import ExitStack

import numpy as np

import concourse.bass as bass
from concourse import mybir

F32 = mybir.dt.float32
F32R = mybir.dt.float32r
I32 = mybir.dt.int32
ALU = mybir.AluOpType
ACT = mybir.ActivationFunctionType
AX = mybir.AxisListType

D = 1024
KB = D // 128
META, SEQ = 16, 256
TP = META + SEQ
NB, TS = 8, 4
NT = TP + NB * TS
L = (128, 128, NT - 256)
T0 = (0, 128, 256)
TAIL = TP - 256
HA, HB = 8, 4
CONV = 3 * D
NCB = CONV // 128
CW = 4
XW = TP + CW - 1 + NB * (TS + CW - 1)
XS = TP + CW - 1
NG, EPG = 4, 8
FF = 256
CAP = 128
SLOTS = 8
SW = 2048
EPS = 1e-6
LN_EXP = "natural_log_exp_and_others"
TAU = 16.0
C_QKV, C_Z, C_BA, C_QB, C_KB, C_VB, C_RB, C_LR, C_GA, C_GB = 0, 3072, 4096, 4112, 4624, 5136, 6160, 7184, 7200, 8224
WIN = ([C_QKV + 256 * i for i in range(12)] + [C_QB, C_QB + 256, C_KB, C_KB + 256] + [C_VB + 256 * i for i in range(4)]
       + [C_Z + 256 * i for i in range(4)] + [C_RB + 256 * i for i in range(4)]
       + [C_GA + 256 * i for i in range(4)] + [C_GB + 256 * i for i in range(4)])
N_QB, N_VB, N_Z, N_PA = 12, 16, 20, len(WIN)
N_WO = N_PA + 8
N_PRE = N_WO + 4
PER_GROUP = 3 * EPG


def units(n):
    return sum(3 if N_VB <= k < N_Z or k >= N_WO else 2 for k in range(n))


def named(nc, stage, names):
    return {n: nc.alloc_semaphore(f"{stage}_{n}") for n in names.split()}


class Chain:
    def __init__(self, eng, sem):
        self.eng, self.sem, self.n = eng, sem, 0

    def __call__(self, ins):
        self.n += 1
        ins.then_inc(self.sem, 1)
        self.eng.wait_ge(self.sem, self.n)


def bc_mid(ap2, n):
    return ap2.unsqueeze(1).to_broadcast([ap2.shape[0], n, ap2.shape[1]])


def bc_last(ap, n):
    k = len(ap.shape)
    return ap.unsqueeze(k).to_broadcast([*ap.shape, n])


class Core:

    def __init__(self, nc, ctx, i_, o_):
        self.nc, self.ctx, self.i_, self.o_ = nc, ctx, i_, o_

        self.addr, self.views = {}, 0


        def sb(name, shape, dt=F32):
            v = ctx.enter_context(nc.sbuf_tensor(name, shape, dt))
            self.addr[name] = nc.sbuf_base - 4 * int(np.prod(shape[1:]))
            return v
        self.ring = sb("ring", [128, SLOTS, SW])
        self.hT = sb("hT", [128, KB, NT])
        self.hH = self.rounded("hT", 0, KB * NT, KB, NT)
        self.hL = sb("hL", [128, KB, NT], F32R)
        self.oaT = sb("oaT", [128, HA, NT])
        m = self.masks = sb("masks", [128, 21, 128])
        self.ident, self.U, self.SL, self.SU, self.BLK = (m[:, k, :] for k in range(5))
        self.PAIR = [m[:, k, :] for k in range(5, 8)]
        self.GR = m[:, 8:13, :]
        self.GM = m[:, 13:17, :]
        self.U3, self.SL3, self.SU3, self.R03 = (m[:, k, :] for k in range(17, 21))
        self.ones = sb("ones", [128, 128])
        self.seg = sb("seg", [128, 9])
        self.lrT = sb("lrT", [16, NT])
        self.small = sb("small", [128, 1300])
        self.at = 0
        self.cnti = sb("cnti", [128, 1], I32)
        self.AR = 24960
        self.arena = sb("arena", [128, self.AR])
        P = self.piece
        self.epsc = P(1)
        self.ss, self.rstd = P(3), P(3)
        self.nm, self.nf = P(8), P(8)
        self.cw = P(CW * NCB, CW, NCB)
        self.na, self.nb = P(1), P(2)
        self.sm = P(48, 3, 16)
        self.t1, self.t2 = P(24, 3, 8), P(24, 3, 8)
        self.beta = P(24, 3, 8)
        self.nbeg = P(24, 3, 8)
        self.gg = P(24, 3, 8)
        self.kw = P(24, 3, 8)
        self.egl = P(16, 2, 8)
        self.egl3, self.gm3 = P(72, 9, 8), P(72, 9, 8)
        self.hrow, self.hbc = P(16), P(16)
        self.rbias = P(36)
        self.psum = [ctx.enter_context(nc.psum_tensor(f"ps{k}", [128, 512], F32)) for k in range(8)]
        self.ring_in = [ctx.enter_context(nc.semaphore(f"ring_in{s}")) for s in range(SLOTS)]
        self.unit_done = ctx.enter_context(nc.semaphore("unit_done"))
        self.w_hi = ctx.enter_context(nc.semaphore("w_hi"))
        self.w_lo = ctx.enter_context(nc.semaphore("w_lo"))
        self.LOW = self.rounded("ring", 0, SLOTS * SW, SLOTS, SW)
        self.w_in = i_["w_in"][0].rearrange("(p j) c -> p j c", j=KB)

    @staticmethod
    def shaped(v, dims):
        if len(dims) == 2:
            return v.rearrange("p (a b) -> p a b", b=dims[1])
        if len(dims) == 3:
            return v.rearrange("p (a b c) -> p a b c", b=dims[1], c=dims[2])
        return v

    def piece(self, n, *dims):
        v = self.small[:, self.at:self.at + n]
        self.at += n
        assert self.at <= 1300
        return self.shaped(v, dims)

    def carve(self, off, n, *dims):
        assert off + n <= self.AR, (off, n)
        return self.shaped(self.arena[:, off:off + n], dims)

    def rounded(self, tensor, off, n, *dims):
        self.views += 1
        v = self.nc.alloc_sbuf_tensor_at(f"rounded{self.views}", [128, n], F32R, offset=self.addr[tensor] + 4 * off)
        return self.shaped(v[:, :], dims)

    def carve_r(self, off, n, *dims):
        assert off + n <= self.AR, (off, n)
        return self.rounded("arena", off, n, *dims)

    def slot8(self, n):
        return self.ring[:, n % SLOTS, :].rearrange("p (j c) -> p j c", j=KB)

    def bank4(self, b, l=128):
        return self.psum[b][:, :].rearrange("p (h t) -> p h t", h=4)[:, :, 0:l]

    def load_w(self, sp, n):
        if n >= SLOTS:
            sp.wait_ge(self.unit_done, units(n - SLOTS + 1))
        if n < N_PA:
            src = self.w_in[:, :, WIN[n]:WIN[n] + 256]
        else:
            m, q = divmod(n - N_PA, 4)
            w = self.i_[("w_proj_a", "w_proj_b", "w_out")[m]][0]
            src = w.rearrange("(j p) c -> p j c", p=128)[:, :, 256 * q:256 * q + 256]
        sp.dma_start(self.slot8(n), src).then_inc(self.ring_in[n % SLOTS], 16)

    def load_x(self, sp, X, signal):
        xp = self.i_["x_prompt"]
        sp.dma_start(X[0:META, 0, :], self.i_["meta_tokens"][:, :]).then_inc(signal, 16)
        sp.dma_start(X[META:128, 0, :], xp[0, 0:112, :]).then_inc(signal, 16)
        sp.dma_start(X[:, 1, :], xp[0, 112:240, :]).then_inc(signal, 16)
        sp.dma_start(X[0:TAIL, 2, :], xp[0, 240:256, :]).then_inc(signal, 16)
        sp.dma_start(X[TAIL:L[2], 2, :], self.i_["x_sample"].rearrange("b t d -> (b t) d")).then_inc(signal, 16)

    def high_part(self, act, n, HI):
        self.arrived(act, n)
        if n >= 3:
            act.wait_ge(self.unit_done, units(n - 2))
        self.nc.scalar.activation(HI[n % 3], self.ring[:, n % SLOTS, :], ACT.Copy).then_inc(self.w_hi, 1)

    def low_part(self, eng, on, n, HI):
        eng.wait_ge(self.w_hi, n + 1)
        if n:
            eng.wait_ge(self.w_lo, n)
        on.tensor_tensor(self.LOW[:, n % SLOTS, :], self.ring[:, n % SLOTS, :], HI[n % 3], ALU.subtract).then_inc(self.w_lo, 1)

    def arrived(self, pe, n):
        pe.wait_ge(self.ring_in[n % SLOTS], 16 * (n // SLOTS + 1))

    def block_of_slot(self, pe, n, q, b, HI):
        pe.wait_ge(self.w_lo, n + 1)
        h, lo = (w.rearrange("p (j c) -> p j c", j=KB) for w in (HI[n % 3], self.LOW[:, n % SLOTS, :]))
        c = slice(128 * q, 128 * q + 128)
        for j in range(KB):
            self.nc.tensor.matmul(self.psum[b][:, 0:NT], h[:, j, c], self.hH[:, j, :], start=(j == 0), stop=False)
            self.nc.tensor.matmul(self.psum[b][:, 0:NT], h[:, j, c], self.hL[:, j, :], start=False, stop=False)
            ins = self.nc.tensor.matmul(self.psum[b][:, 0:NT], lo[:, j, c], self.hH[:, j, :], start=False, stop=(j == KB - 1))
        ins.then_inc(self.unit_done, 1)

    def block_of_projection(self, pe, n, q, b, moving):
        self.arrived(pe, n)
        for j in range(KB):
            ins = self.nc.tensor.matmul(self.psum[b][:, 0:NT], self.slot8(n)[:, j, 128 * q:128 * q + 128],
                                        moving(j), start=(j == 0), stop=(j == KB - 1))
        ins.then_inc(self.unit_done, 1)


A1 = 8576


def front(k):
    nc, i_, o_ = k.nc, k.i_, k.o_
    ident, U, SL, SU, BLK, PAIR, GR, GM = k.ident, k.U, k.SL, k.SU, k.BLK, k.PAIR, k.GR, k.GM
    U3, SL3, SU3, R03, ones, seg, masks = k.U3, k.SL3, k.SU3, k.R03, k.ones, k.seg, k.masks
    hH, hL, oaT, psum, unit_done, w_in, lrT = k.hH, k.hL, k.oaT, k.psum, k.unit_done, k.w_in, k.lrT
    epsc, ss, rstd, nm, nf, cw, na, nb, sm, t1, t2 = k.epsc, k.ss, k.rstd, k.nm, k.nf, k.cw, k.na, k.nb, k.sm, k.t1, k.t2
    beta, nbeg, gg, kw, egl, egl3, gm3, hrow, hbc, rbias = k.beta, k.nbeg, k.gg, k.kw, k.egl, k.egl3, k.gm3, k.hrow, k.hbc, k.rbias
    KT = k.carve(0, HA * NT, HA, NT)
    Kd = k.carve(2432, 3072, 3, 8, 128)
    V = k.carve(5504, 3072, 3, 8, 128)
    X = k.carve(A1, 3072, 3, D)
    XN = k.carve(A1 + 3072, 3072, 3, D)
    SC = k.carve(A1 + 6144, CONV)
    SCO = k.carve(A1 + 9216, CONV)
    CWR = k.carve(A1 + 12288, 128)
    wsm = k.carve(A1 + 12416, KB * 32, KB, 32)
    HI = [k.carve_r(21248, SW), k.carve_r(A1 + 9216, SW), k.carve_r(11480, SW)]
    XC = k.carve(A1, 3 * XW, 3, XW)
    CV = k.carve(A1 + 3 * XW, 2 * XW, 2, XW)
    VT = k.carve(A1 + 5 * XW, 2 * NT, 2, NT)
    LAST = k.carve(A1 + 5 * XW + 2 * NT, NCB * 27, NCB, 27)
    SQ = k.carve(A1 + 3 * XW, 2 * NT, 2, NT)
    RS = k.carve(A1 + 3 * XW + 2 * NT, 2 * NT, 2, NT)
    s = named(nc, "front", """x_in par_in late_in sc_in ident_ready mask_ready rstd_ready xn_ready xT_done xT_evac small_done small_ready
        hist_done hist_ready conv_ready conv_silu last_ready last_done last_evac sq_ready ssum_done rs_ready
        qk_ready vT_done vT_evac kT_done kT_evac par_done par_ready g_ready gsum_done gsum_ready lr_done lr_ready
        sc_out act_c dve_c pool_c""")
    ctx = ExitStack()
    block = ctx.enter_context(nc.Block())

    @block.sync
    def _(sp):
        k.load_x(sp, X, s["x_in"])
        sp.dma_start(nm, i_["norm_mix"][0].rearrange("(p j) -> p j", j=KB)).then_inc(s["par_in"], 16)
        sp.dma_start(wsm[:, :, 0:16], w_in[:, :, C_BA:C_BA + 16]).then_inc(s["par_in"], 16)
        sp.dma_start(wsm[:, :, 16:32], w_in[:, :, C_LR:C_LR + 16]).then_inc(s["par_in"], 16)
        sp.dma_start(CWR[0:CW * NCB, :], i_["conv_w"][0].rearrange("i (b c) -> (i b) c", c=128)).then_inc(s["par_in"], 16)
        sp.dma_start(hrow[0:1, 0:8], i_["a_log"]).then_inc(s["par_in"], 16)
        sp.dma_start(hrow[0:1, 8:16], i_["dt_bias"]).then_inc(s["par_in"], 16)
        sp.dma_start(SC[0:24, :], i_["state_conv"][0].rearrange("b r c -> (b r) c")).then_inc(s["sc_in"], 16)
        for n in range(N_VB):
            k.load_w(sp, n)
        sp.dma_start(na, i_["norm_a"][0].rearrange("(p a) -> p a", a=1)).then_inc(s["late_in"], 16)
        for a in range(2):
            sp.dma_start(nb[:, a:a + 1], i_["norm_b"][0, 128 * a:128 * a + 128].rearrange("(p a) -> p a", a=1)).then_inc(s["late_in"], 16)
        sp.dma_start(nf, i_["norm_ffn"][0].rearrange("(p j) -> p j", j=KB)).then_inc(s["late_in"], 16)
        sp.dma_start(rbias[0:1, 0:4], i_["router_group_b"]).then_inc(s["late_in"], 16)
        sp.dma_start(rbias[0:1, 4:36], i_["router_expert_b"]).then_inc(s["late_in"], 16)
        sp.wait_ge(s["last_evac"], 6)
        sp.dma_start(o_["conv_p"][0, 0], SCO[0:3, :]).then_inc(s["sc_out"], 16)
        sp.dma_start(o_["conv_s"][0].rearrange("b r c -> (b r) c"), SCO[3:27, :]).then_inc(s["sc_out"], 16)
        sp.wait_ge(s["sc_out"], 32)
        sp.wait_ge(s["late_in"], 96)


    @block.gpsimd
    def _(pl):
        link = Chain(pl, s["pool_c"])

        def keep(ap, pattern, base, cm):
            link(nc.gpsimd.affine_select(out=ap, in_=ap, compare_op=ALU.is_ge, fill=0.0, base=base,
                                   pattern=pattern, channel_multiplier=cm))

        def blocks(ap, m):
            v = ap.rearrange("p (a b) -> p a b", b=m)
            n = ap.shape[1] // m
            keep(v, [[-m, n], [0, m]], 0, 1)
            keep(v, [[m, n], [0, m]], m - 1, -1)
        link(nc.gpsimd.memset(epsc, EPS))
        link(nc.gpsimd.memset(ones[:, :], 1.0))
        link(nc.gpsimd.memset(ident, 1.0))
        keep(ident, [[1, 128]], 0, -1)
        keep(ident, [[-1, 128]], 0, 1)
        pl.drain().then_inc(s["ident_ready"], 1)
        link(nc.gpsimd.memset(masks[:, 1:, :], 1.0))
        link(nc.gpsimd.memset(seg[:, :], 1.0))
        keep(U, [[1, 128]], 0, -1)
        keep(SL, [[-1, 128]], -1, 1)
        keep(SU, [[1, 128]], -1, -1)
        blocks(BLK, 16)
        for M, m in zip(PAIR, (16, 32, 64)):
            v = M.rearrange("p (a h b) -> p a h b", h=2, b=m)
            n = 128 // (2 * m)
            keep(v, [[-2 * m, n], [-1000, 2], [0, m]], -m, 1)
            keep(v, [[2 * m, n], [0, 2], [0, m]], 2 * m - 1, -1)
        link(nc.gpsimd.tensor_copy(GR[:, 0, :], U))
        for r, m in ((1, 8), (2, 64), (3, 32), (4, 16)):
            v = GR[:, r, :].rearrange("p (a h b) -> p a h b", h=2, b=m)
            for h, src in ((0, SL), (1, U)):
                half = src.rearrange("p (a h b) -> p a h b", h=2, b=m)
                if r == 1 and h == 0:
                    link(nc.gpsimd.tensor_scalar(v[:, :, h, :], half[:, :, h, :], -1.0, None, ALU.mult))
                else:
                    link(nc.gpsimd.tensor_copy(v[:, :, h, :], half[:, :, h, :]))
            blocks(GR[:, r, :], m)
        link(nc.gpsimd.tensor_tensor(GM[:, 0, :], U, BLK, ALU.mult))
        for r, m in ((1, 64), (2, 32), (3, 16)):
            v = GM[:, r, :].rearrange("p (a h b) -> p a h b", h=2, b=m)
            n = 128 // (2 * m)
            keep(v, [[-2 * m, n], [0, 2], [0, m]], 0, 1)
            keep(v, [[2 * m, n], [1000, 2], [0, m]], m - 1 - 1000, -1)
        for M, src in ((U3, U), (SL3, SL), (SU3, SU)):
            link(nc.gpsimd.tensor_copy(M, src))
            keep(M[:, 0:TAIL], [[0, TAIL]], TAIL - 1, -1)
            v = M[:, TAIL:L[2]].rearrange("p (a b) -> p a b", b=TS)
            keep(v, [[-TS, NB], [0, TS]], -TAIL, 1)
            keep(v, [[TS, NB], [0, TS]], TAIL + TS - 1, -1)
        link(nc.gpsimd.tensor_copy(R03[:, 0:TAIL], GR[:, 1, 0:TAIL]))
        link(nc.gpsimd.tensor_copy(R03[:, TAIL:L[2]], U3[:, TAIL:L[2]]))
        keep(seg[:, 0:1], [[0, 1]], TAIL - 1, -1)
        keep(seg[:, 1:9], [[-TS, NB]], -TAIL, 1)
        keep(seg[:, 1:9], [[TS, NB]], TAIL + TS - 1, -1)
        pl.drain().then_inc(s["mask_ready"], 1)

        for b in range(NCB):
            pl.wait_ge(s["hist_ready"], b + 1)
            x = XC[:, b % 3, :]
            nc.gpsimd.tensor_copy(LAST[:, b, 0:3], x[:, TP:TP + 3])
            nc.gpsimd.tensor_copy(LAST[:, b, 3:27].rearrange("p (a r) -> p a r", r=3),
                            x[:, XS:].rearrange("p (a r) -> p a r", r=TS + 3)[:, :, TS:]).then_inc(s["last_ready"], 1)
            if b % 2 and b // 2 + 3 < N_QB:
                k.low_part(pl, nc.gpsimd, b // 2 + 3, HI)
        pl.wait_ge(s["conv_silu"], NCB)
        for b in range(16):
            if b >= 2:
                pl.wait_ge(s["ssum_done"], b - 1)
            src = (oaT if b < 8 else KT)[:, b % 8, :]
            nc.gpsimd.tensor_tensor(SQ[:, b % 2, :], src, src, ALU.mult).then_inc(s["sq_ready"], 1)


    @block.scalar
    def _(act):
        link = Chain(act, s["act_c"])
        act.preload_act_table_set(LN_EXP)
        act.wait_ge(s["x_in"], 80)
        act.wait_ge(s["ident_ready"], 1)
        for c in range(3):
            l = L[c]
            link(nc.scalar.activation(XN[0:l, c, :], X[0:l, c, :], ACT.Square, accum_out=ss[0:l, c:c + 1]))
            link(nc.scalar.activation(ss[0:l, c:c + 1], ss[0:l, c:c + 1], ACT.Ln, scale=1.0 / D, bias=epsc[0:l, :]))
            nc.scalar.activation(rstd[0:l, c:c + 1], ss[0:l, c:c + 1], ACT.Exp, scale=-0.5).then_inc(s["rstd_ready"], 1)
        k.high_part(act, 0, HI)
        k.high_part(act, 1, HI)
        act.wait_ge(s["par_done"], 2)
        link(nc.scalar.activation(hbc, psum[5][:, 0:16], ACT.Copy))
        link(nc.scalar.activation(hbc[:, 0:8], hbc[:, 0:8], ACT.Exp))
        nc.scalar.activation(cw.rearrange("p i b -> p (i b)"), psum[4][:, 0:CW * NCB], ACT.Copy).then_inc(s["par_ready"], 1)
        act.wait_ge(s["small_done"], 3)
        for c in range(3):
            nc.scalar.activation(sm[0:L[c], c, :], psum[6][0:L[c], 16 * c:16 * c + 16], ACT.Copy).then_inc(s["small_ready"], 1)
        act.wait_ge(s["lr_done"], 1)
        nc.scalar.activation(lrT[:, :], psum[7][0:16, 200:200 + NT], ACT.Copy).then_inc(s["lr_ready"], 1)
        act.wait_ge(s["small_ready"], 3)
        act.wait_ge(s["g_ready"], 1)
        for c in range(3):
            l = L[c]
            link(nc.scalar.activation(beta[0:l, c, :], sm[0:l, c, 0:8], ACT.Exp, scale=-1.0))
            link(nc.scalar.activation(t1[0:l, c, :], t1[0:l, c, :], ACT.Exp, scale=-1.0))
            nc.scalar.activation(t1[0:l, c, :], t1[0:l, c, :], ACT.Ln, bias=1.0).then_inc(s["g_ready"], 1)
        act.wait_ge(s["xT_evac"], 8)
        for r in range(3):
            nc.scalar.activation(XC[:, r, 0:3], ones[:, 0:3], ACT.Copy, scale=0.0)
        k.high_part(act, 2, HI)

        def decays():
            act.wait_ge(s["gsum_done"], 3)
            for c in range(3):
                l = L[c]
                p = psum[7][:, 32 * c:32 * c + 32]
                link(nc.scalar.activation(nbeg[0:l, c, :], p[0:l, 0:8], ACT.Exp))
                nc.scalar.activation(kw[0:l, c, :], p[0:l, 8:16], ACT.Exp)
                if c < 2:
                    nc.scalar.activation(egl[:, c, :], p[:, 16:24], ACT.Exp)
                else:
                    nc.scalar.activation(egl3.rearrange("p a b -> p (a b)"), psum[7][:, 96:168], ACT.Exp)
                link(nc.scalar.activation(nbeg[0:l, c, :], nbeg[0:l, c, :], ACT.Copy, scale=-1.0))
                act.drain().then_inc(s["gsum_ready"], 1)

        def silu(b):
            act.wait_ge(s["conv_ready"], b + 1)
            src = CV[:, b % 2, :]
            if b < 16:
                dst = (oaT if b < 8 else KT)[:, b % 8, :]
            else:
                if b >= 18:
                    act.wait_ge(s["vT_done"], b - 17)
                dst = VT[:, b % 2, :]
            nc.scalar.activation(dst[:, 0:TP], src[:, 0:TP], ACT.Silu)
            nc.scalar.activation(dst[:, TP:].rearrange("p (a r) -> p a r", r=TS),
                         src[:, XS:XS + 56].rearrange("p (a r) -> p a r", r=TS + 3)[:, :, 0:TS], ACT.Silu).then_inc(s["conv_silu"], 1)
        for b in range(NCB):
            if b == 3:
                decays()
            act.wait_ge(s["hist_done"], b + 1)
            act.wait_ge(unit_done, b + 1)
            if b >= 3:
                act.wait_ge(s["conv_ready"], b - 2)
                act.wait_ge(s["last_ready"], b - 2)
            x = XC[:, b % 3, :]
            xs = x[:, XS:].rearrange("p (a r) -> p a r", r=TS + 3)
            nc.scalar.activation(xs[:, :, 0:3], psum[4 + b % 2][:, 0:24].rearrange("p (a r) -> p a r", r=3), ACT.Copy)
            nc.scalar.activation(x[:, 3:XS], psum[b % 4][:, 0:TP], ACT.Copy)
            nc.scalar.activation(xs[:, :, 3:], psum[b % 4][:, TP:NT].rearrange("p (a r) -> p a r", r=TS), ACT.Copy)
            act.drain().then_inc(s["hist_ready"], 1)
            if b % 2 and b // 2 + 3 < N_QB:
                k.high_part(act, b // 2 + 3, HI)
            if b >= 2:
                silu(b - 2)
        silu(NCB - 2)
        silu(NCB - 1)
        act.preload_act_table_set(LN_EXP)
        for b in range(16):
            act.wait_ge(s["ssum_done"], b + 1)
            if b >= 2:
                act.wait_ge(s["qk_ready"], b - 1)
            link(nc.scalar.activation(RS[:, b % 2, :], psum[b % 4][:, 0:NT], ACT.Ln, bias=epsc))
            nc.scalar.activation(RS[:, b % 2, :], RS[:, b % 2, :], ACT.Exp, scale=-0.5).then_inc(s["rs_ready"], 1)
        for q in range(6):
            act.wait_ge(s["last_done"], q + 1)
            nc.scalar.activation(SCO[0:27, 512 * q:512 * q + 512], psum[4 + q % 2][0:27, :], ACT.Copy).then_inc(s["last_evac"], 1)


    @block.vector
    def _(dve):
        link = Chain(dve, s["dve_c"])
        for c in range(3):
            l = L[c]
            dve.wait_ge(s["rstd_ready"], c + 1)
            nc.vector.tensor_scalar(XN[0:l, c, :], X[0:l, c, :], rstd[0:l, c:c + 1], None, ALU.mult).then_inc(s["xn_ready"], 1)
        dve.wait_ge(s["par_in"], 96)
        for j in range(KB):
            dve.wait_ge(s["xT_done"], j + 1)
            link(nc.vector.tensor_scalar(hH[:, j, :], psum[j % 4][:, 0:NT], nm[:, j:j + 1], None, ALU.mult))
            nc.vector.scalar_tensor_tensor(hL[:, j, :], psum[j % 4][:, 0:NT], nm[:, j:j + 1], hH[:, j, :],
                                           ALU.mult, ALU.subtract).then_inc(s["xT_evac"], 1)
        k.low_part(dve, nc.vector, 0, HI)
        k.low_part(dve, nc.vector, 1, HI)
        dve.wait_ge(s["par_ready"], 1)
        dve.wait_ge(s["small_ready"], 3)
        for c in range(3):
            l = L[c]
            link(nc.vector.tensor_tensor(sm[0:l, c, 8:16], sm[0:l, c, 8:16], hbc[0:l, 8:16], ALU.add))
            link(nc.vector.tensor_scalar(t2[0:l, c, :], sm[0:l, c, 8:16], 0.0, None, ALU.max))
            link(nc.vector.scalar_tensor_tensor(t1[0:l, c, :], t2[0:l, c, :], 2.0, sm[0:l, c, 8:16], ALU.mult, ALU.subtract))
        dve.drain().then_inc(s["g_ready"], 1)
        dve.wait_ge(s["g_ready"], 4)
        for c in range(3):
            l = L[c]
            link(nc.vector.tensor_tensor(t2[0:l, c, :], t2[0:l, c, :], t1[0:l, c, :], ALU.add))
            link(nc.vector.scalar_tensor_tensor(gg[0:l, c, :], t2[0:l, c, :], -1.0, hbc[0:l, 0:8], ALU.mult, ALU.mult))
            link(nc.vector.tensor_scalar(beta[0:l, c, :], beta[0:l, c, :], 1.0, None, ALU.add))
            link(nc.vector.reciprocal(beta[0:l, c, :], beta[0:l, c, :]))
        dve.wait_ge(s["mask_ready"], 1)
        link(nc.vector.tensor_tensor(gm3[0:48, :, :], bc_mid(gg[0:48, 2, :], 9), bc_last(seg[0:48, :], 8), ALU.mult))
        dve.drain().then_inc(s["g_ready"], 1)
        k.low_part(dve, nc.vector, 2, HI)

        def vturn(h):
            dve.wait_ge(s["vT_done"], h + 1)
            for c in range(3):
                ins = nc.vector.tensor_copy(V[0:L[c], c, h, :], psum[6 + h % 2][0:L[c], 128 * c:128 * c + 128])
            ins.then_inc(s["vT_evac"], 1)

        for b in range(NCB):
            dve.wait_ge(s["hist_ready"], b + 1)
            if b >= 2:
                dve.wait_ge(s["conv_silu"], b - 1)
            x, o = XC[:, b % 3, :], CV[:, b % 2, 0:XW - 3]
            link(nc.vector.tensor_scalar(o, x[:, 0:XW - 3], cw[:, 0, b:b + 1], None, ALU.mult))
            for r in range(1, CW):
                ins = nc.vector.scalar_tensor_tensor(o, x[:, r:XW - 3 + r], cw[:, r, b:b + 1], o, ALU.mult, ALU.add)
                if r < 3:
                    link(ins)
            ins.then_inc(s["conv_ready"], 1)
            if b >= 19:
                vturn(b - 19)
        for h in range(NCB - 19, 8):
            vturn(h)
        for b in range(16):
            dve.wait_ge(s["rs_ready"], b + 1)
            t = (oaT if b < 8 else KT)[:, b % 8, :]
            nc.vector.scalar_tensor_tensor(t, t, 128 ** -0.5 if b < 8 else 1.0, RS[:, b % 2, :], ALU.mult, ALU.mult).then_inc(s["qk_ready"], 1)
        dve.wait_ge(s["gsum_ready"], 3)
        for h in range(8):
            dve.wait_ge(s["kT_done"], h + 1)
            for c in range(3):
                ins = nc.vector.tensor_scalar(Kd[0:L[c], c, h, :], psum[6 + h % 2][0:L[c], 128 * c:128 * c + 128], kw[0:L[c], c, h:h + 1], None, ALU.mult)
            ins.then_inc(s["kT_evac"], 1)


    @block.tensor
    def _(pe):
        mm = nc.tensor.matmul

        def tr(out, in_, n):
            return nc.tensor.transpose(out, in_, ident[0:n, 0:n])

        pe.wait_ge(s["ident_ready"], 1)
        for j in range(KB):
            if j >= 4:
                pe.wait_ge(s["xT_evac"], j - 3)
            for c in range(3):
                if j == 0:
                    pe.wait_ge(s["xn_ready"], c + 1)
                ins = tr(psum[j % 4][:, T0[c]:T0[c] + L[c]], XN[0:L[c], c, j::KB], L[c])
            ins.then_inc(s["xT_done"], 1)
        pe.wait_ge(s["par_in"], 96)
        tr(psum[4][:, 0:CW * NCB], CWR[0:CW * NCB, :], CW * NCB).then_inc(s["par_done"], 1)
        mm(psum[5][:, 0:16], ones[0:1, :], hrow[0:1, :], start=True, stop=True).then_inc(s["par_done"], 1)
        pe.wait_ge(s["xT_evac"], 8)
        for c in range(3):
            for j in range(KB):
                for x in (hH, hL):
                    ins = mm(psum[6][0:L[c], 16 * c:16 * c + 16], x[:, j, T0[c]:T0[c] + L[c]].bitcast(F32), wsm[:, j, 0:16],
                             start=(j == 0 and x is hH), stop=(j == KB - 1 and x is hL))
            ins.then_inc(s["small_done"], 1)
        for j in range(KB):
            for x in (hH, hL):
                ins = mm(psum[7][0:16, 200:200 + NT], wsm[:, j, 16:32], x[:, j, :].bitcast(F32),
                         start=(j == 0 and x is hH), stop=(j == KB - 1 and x is hL))
        ins.then_inc(s["lr_done"], 1)

        def turn_v(h):
            pe.wait_ge(s["conv_silu"], 17 + h)
            if h >= 2:
                pe.wait_ge(s["vT_evac"], h - 1)
            for c in range(3):
                ins = tr(psum[6 + h % 2][0:L[c], 128 * c:128 * c + 128], VT[:, h % 2, T0[c]:T0[c] + L[c]], 128)
            ins.then_inc(s["vT_done"], 1)
        pe.wait_ge(s["sc_in"], 16)
        for b in range(NCB):
            if b >= 2:
                pe.wait_ge(s["hist_ready"], b - 1)
            if b < 2:
                pe.wait_ge(s["par_ready"], 1)
                pe.wait_ge(s["small_ready"], 3)
            tr(psum[4 + b % 2][:, 0:24], SC[0:24, 128 * b:128 * b + 128], 24).then_inc(s["hist_done"], 1)
            if b >= 4:
                pe.wait_ge(s["hist_ready"], b - 3)
            k.block_of_slot(pe, b // 2, b % 2, b % 4, HI)
            if b == 2:
                pe.wait_ge(s["mask_ready"], 1)
                pe.wait_ge(s["g_ready"], 5)
                pe.wait_ge(s["lr_ready"], 1)
                for c in range(3):
                    l = L[c]
                    p = psum[7][:, 32 * c:32 * c + 32]
                    mm(p[0:l, 0:8], (U if c < 2 else U3)[0:l, 0:l], gg[0:l, c, :], start=True, stop=True)
                    ins = mm(p[0:l, 8:16], (SL if c < 2 else SL3)[0:l, 0:l], gg[0:l, c, :], start=True, stop=True)
                    if c < 2:
                        ins = mm(p[:, 16:24], ones[:, :], gg[:, c, :], start=True, stop=True)
                    else:
                        ins = mm(psum[7][:, 96:168], ones[0:l, :], gm3[0:l, :, :].rearrange("p a b -> p (a b)"), start=True, stop=True)
                    ins.then_inc(s["gsum_done"], 1)
            if b >= 19:
                if b == 19:
                    pe.wait_ge(s["gsum_ready"], 3)
                turn_v(b - 19)
        for h in range(NCB - 19, 8):
            turn_v(h)
        for b in range(16):
            pe.wait_ge(s["sq_ready"], b + 1)
            if b >= 4:
                pe.wait_ge(s["rs_ready"], b - 3)
            mm(psum[b % 4][:, 0:NT], ones[:, :], SQ[:, b % 2, :], start=True, stop=True).then_inc(s["ssum_done"], 1)
        for h in range(8):
            pe.wait_ge(s["qk_ready"], 9 + h)
            pe.wait_ge(s["vT_evac"], 8)
            if h >= 2:
                pe.wait_ge(s["kT_evac"], h - 1)
            for c in range(3):
                ins = tr(psum[6 + h % 2][0:L[c], 128 * c:128 * c + 128], KT[:, h, T0[c]:T0[c] + L[c]], 128)
            ins.then_inc(s["kT_done"], 1)
        pe.wait_ge(s["last_ready"], NCB)
        for q in range(6):
            if q >= 2:
                pe.wait_ge(s["last_evac"], q - 1)
            for r in range(4):
                ins = tr(psum[4 + q % 2][0:27, 128 * r:128 * r + 128], LAST[:, 4 * q + r, :], 128)
            ins.then_inc(s["last_done"], 1)

    ctx.close()
    nc.clear_and_free_semaphores(list(s.values()))
    nc.all_engine_barrier()


def delta(k):
    nc, i_, o_ = k.nc, k.i_, k.o_
    ident, U, SL, SU, BLK, PAIR = k.ident, k.U, k.SL, k.SU, k.BLK, k.PAIR
    U3, SL3, SU3, ones, seg = k.U3, k.SL3, k.SU3, k.ones, k.seg
    oaT, bank4, beta, nbeg, gg, egl, egl3 = k.oaT, k.bank4, k.beta, k.nbeg, k.gg, k.egl, k.egl3
    KT = k.carve(0, HA * NT, HA, NT)
    Kd = k.carve(2432, 3072, 3, 8, 128)
    V = k.carve(5504, 3072, 3, 8, 128)
    MB = [A1 + 5632 * hh for hh in range(2)]
    buf = [[k.carve(MB[hh] + 512 * x, 512, 4, 128) for x in range(11)] for hh in range(2)]
    (bDT, bB, bD0, bB0, bD2, bB2, bD, bE, bY, bAT, bEG) = range(11)
    KDM = [[k.carve(MB[hh] + 512 * (2 + 3 * x), 9 * 128, 9, 128) for x in range(2)] for hh in range(2)]
    SA = k.carve(A1 + 11264, 4096, 4, 8, 128)
    free = k.ring.rearrange("p s c -> p (s c)")
    SB = k.shaped(free[:, 0:4096], (4, 8, 128))
    MT = k.shaped(free[:, 4096:4096 + 9 * L[2]], (9, L[2]))
    SEGM = k.shaped(free[:, 4096 + 9 * L[2]:4096 + 81 * L[2]], (8, 9, L[2]))
    assert 4096 + 81 * L[2] <= 4 * SW

    def sample_state(h):
        return (SA if h < 4 else SB)[:, h % 4, :, :]
    S = k.carve(A1 + 15360, 1024, 8, 128)
    s = named(nc, "delta", """xg_ready sb_ready diff_done kk_done eg_done dt_ready eg_ready b_ready at1_ready at_ready qe_ready
        dT_done d0_ready d_ready b0_ready y1_ready e_ready sq2_done d2_ready b2_ready p4_done y2_ready d4_ready
        b4_ready p8_done y3_ready d8_ready p9_done y4_ready lz_done z_ready x_ready lw_done y_ready ks_done
        mt_ready ktm_ready qm_ready otok_ready otok_done r_ready vn_done vn_ready o_done oT_ready ds_done s_ready kdm_ready kdo_ready su_done su_ready
        sa_in sa_out sp_out dve_c""")
    ctx = ExitStack()
    block = ctx.enter_context(nc.Block())

    @block.sync
    def _(sp):
        for h in range(8):
            sp.dma_start(sample_state(h), i_["state_delta"][0, :, h].rearrange("b k v -> k b v")).then_inc(s["sa_in"], 16)
        for h in range(8):
            sp.wait_ge(s["su_ready"], h + 1)
            sp.dma_start(o_["sd_s"][0, :, h].rearrange("b k v -> k b v"), sample_state(h)).then_inc(s["sa_out"], 16)
        sp.wait_ge(s["s_ready"], 6)
        sp.dma_start(o_["sd_p"][0, 0].rearrange("h k v -> k h v"), S[:, :, :]).then_inc(s["sp_out"], 16)
        sp.wait_ge(s["sa_out"], 16 * 8)
        sp.wait_ge(s["sp_out"], 16)


    l3 = L[2]

    @block.gpsimd
    def _(pl):
        for c in range(3):
            l = L[c]
            if c == 1:
                tests = ((MT[:, 0, :], [[-1, l3]], TAIL - 1), (MT[:, 1:9, :], [[-TS, NB], [1, l3]], -TAIL),
                         (MT[:, 1:9, :], [[TS, NB], [-1, l3]], TAIL + TS - 1))
                nc.gpsimd.memset(MT[:, :, :], 1.0).then_inc(s["mt_ready"], 1)
                for n, (ap, pattern, base) in enumerate(tests):
                    pl.wait_ge(s["mt_ready"], n + 1)
                    nc.gpsimd.affine_select(out=ap, in_=ap, compare_op=ALU.is_ge, fill=0.0, base=base, pattern=pattern,
                                            channel_multiplier=0).then_inc(s["mt_ready"], 1)
                pl.wait_ge(s["mt_ready"], 4)
            if c == 2:
                for h in range(8):
                    nc.gpsimd.tensor_tensor(SEGM[:, h, :, :], bc_mid(KT[:, h, 256:NT], 9), MT[:, :, :], ALU.mult).then_inc(s["ktm_ready"], 1)
            mU, mSL, mSU = (U, SL, SU) if c < 2 else (U3, SL3, SU3)
            for hh in range(2):
                i = 2 * c + hh
                w = buf[hh]
                hs = slice(4 * hh, 4 * hh + 4)
                if c:
                    pl.wait_ge(s["s_ready"], i - 1)
                nc.gpsimd.tensor_tensor(w[bD2][0:l, :, 0:l], bc_mid(mSL[0:l, 0:l], 4), bc_last(gg[0:l, c, hs], l), ALU.mult)
                nc.gpsimd.tensor_tensor(w[bB2][0:l, :, :], bc_mid(ones[0:l, :], 4), bc_last(gg[0:l, c, hs], 128),
                                  ALU.mult).then_inc(s["xg_ready"], 1)
                nc.gpsimd.tensor_tensor(w[bE][0:l, :, 0:l], bc_mid(mSU[0:l, 0:l], 4), bc_last(beta[0:l, c, hs], l),
                                  ALU.mult).then_inc(s["sb_ready"], 1)
            for hh in range(2):
                i = 2 * c + hh
                w = buf[hh]
                hs = slice(4 * hh, 4 * hh + 4)
                tk = slice(T0[c], T0[c] + l)
                pl.wait_ge(s["b_ready"], i + 1)
                nc.gpsimd.tensor_tensor(w[bB0][0:l, :, 0:l], w[bB][0:l, :, 0:l], bc_mid(BLK[0:l, 0:l], 4),
                                  ALU.mult).then_inc(s["b0_ready"], 1)
                pl.wait_ge(s["b0_ready"], i + 1)
                nc.gpsimd.tensor_tensor(w[bY][0:l, :, 0:l], bc_mid(ident[0:l, 0:l], 4), w[bB0][0:l, :, 0:l],
                                  ALU.subtract).then_inc(s["y1_ready"], 1)
                pl.wait_ge(s["at1_ready"], i + 1)
                nc.gpsimd.tensor_tensor(w[bAT][0:l, :, 0:l], w[bAT][0:l, :, 0:l], bc_mid(mU[0:l, 0:l], 4),
                                  ALU.mult).then_inc(s["at_ready"], 1)
                pl.wait_ge(s["eg_ready"], i + 1)
                nc.gpsimd.tensor_tensor(w[bEG][:, :, 0:l], w[bEG][:, :, 0:l], oaT[:, hs, tk], ALU.mult).then_inc(s["qe_ready"], 1)
            if c < 2:
                for r, M in enumerate(PAIR):
                    for hh in range(2):
                        w = buf[hh]
                        pl.wait_ge(s["d_ready"], 2 * c + hh + 1)
                        if r:
                            pl.wait_ge(s["lz_done"], 6 * c + 2 * (r - 1) + hh + 1)
                        nc.gpsimd.tensor_tensor(w[bE][:, :, :], w[bD][:, :, :], bc_mid(M, 4), ALU.mult).then_inc(s["e_ready"], 1)
            else:
                for h in range(8):
                    hh = h // 4
                    pl.wait_ge(s["ks_done"], 3 + hh)
                    pl.wait_ge(s["qe_ready"], 5 + hh)
                    nc.gpsimd.tensor_tensor(SEGM[:, h, :, :], bc_mid(buf[hh][bEG][:, h % 4, 0:l], 9), MT[:, :, :],
                                            ALU.mult).then_inc(s["qm_ready"], 1)
                for h in range(0, 8, 2):
                    hh = h // 4
                    pl.wait_ge(s["vn_ready"], 5 + hh)
                    if h % 4:
                        pl.wait_ge(s["su_done"], h - 1)
                    nc.gpsimd.tensor_tensor(KDM[hh][0][0:l, :, :], bc_mid(Kd[0:l, 2, h, :], 9), bc_last(seg[0:l, :], 128),
                                            ALU.mult).then_inc(s["kdm_ready"], 1)


    @block.scalar
    def _(act):
        for c in range(3):
            l = L[c]
            for hh in range(2):
                i, w, b0 = 2 * c + hh, buf[hh], 4 * hh
                act.wait_ge(s["diff_done"], i + 1)
                nc.scalar.activation(w[bDT][0:l, :, 0:l], bank4(b0, l)[0:l], ACT.Exp).then_inc(s["dt_ready"], 1)
                act.wait_ge(s["eg_done"], i + 1)
                nc.scalar.activation(w[bEG][:, :, 0:l], bank4(b0 + 3, l), ACT.Exp).then_inc(s["eg_ready"], 1)
            for hh in range(2):
                i, w, b0 = 2 * c + hh, buf[hh], 4 * hh
                act.wait_ge(s["d0_ready"], i + 1)
                nc.scalar.activation(w[bD][0:l, :, 0:l], bank4(b0, l)[0:l], ACT.Copy).then_inc(s["d_ready"], 1)
            for hh in range(2):
                i, w, b0 = 2 * c + hh, buf[hh], 4 * hh
                act.wait_ge(s["sq2_done"], i + 1)
                nc.scalar.activation(w[bD2][0:l, :, 0:l], bank4(b0 + 1, l)[0:l], ACT.Copy).then_inc(s["d2_ready"], 1)
            for hh in range(2):
                i, w, b0 = 2 * c + hh, buf[hh], 4 * hh
                act.wait_ge(s["p4_done"], i + 1)
                nc.scalar.activation(w[bD0][0:l, :, 0:l], bank4(b0, l)[0:l], ACT.Copy).then_inc(s["d4_ready"], 1)
                nc.scalar.activation(w[bB0][0:l, :, 0:l], bank4(b0 + 1, l)[0:l], ACT.Copy).then_inc(s["b4_ready"], 1)
            for hh in range(2):
                i, w, b0 = 2 * c + hh, buf[hh], 4 * hh
                act.wait_ge(s["p8_done"], i + 1)
                nc.scalar.activation(w[bD2][0:l, :, 0:l], bank4(b0 + 3, l)[0:l], ACT.Copy).then_inc(s["d8_ready"], 1)
            if c < 2:
                for k in range(3):
                    for hh in range(2):
                        w, b0 = buf[hh], 4 * hh
                        act.wait_ge(s["lz_done"], 6 * c + 2 * k + hh + 1)
                        nc.scalar.activation(w[bD0], bank4(b0 + 2, l), ACT.Copy).then_inc(s["x_ready"], 1)
            for hh in range(2):
                i, w, b0 = 2 * c + hh, buf[hh], 4 * hh
                hs = slice(4 * hh, 4 * hh + 4)
                if c < 2:
                    act.wait_ge(s["o_done"], i + 1)
                    nc.scalar.activation(oaT[:, hs, T0[c]:T0[c] + l], bank4(b0 + 2, l), ACT.Copy).then_inc(s["oT_ready"], 1)
                else:
                    def masked_keys(h):
                        act.wait_ge(s["vn_ready"], 5 + hh)
                        if h % 4 == 3:
                            act.wait_ge(s["su_done"], h - 1)
                        for q in range(9):
                            ins = nc.scalar.activation(KDM[hh][1][0:l, q, :], Kd[0:l, 2, h, :], ACT.Copy, scale=seg[0:l, q:q + 1])
                        ins.then_inc(s["kdo_ready"], 1)
                    masked_keys(4 * hh + 1)
                    act.wait_ge(s["o_done"], i + 1)
                    nc.scalar.activation(w[bB][0:l, :, :], bank4(b0 + 2, 128)[0:l], ACT.Copy).then_inc(s["otok_ready"], 1)
                    act.wait_ge(s["otok_done"], hh + 1)
                    nc.scalar.activation(oaT[:, hs, T0[c]:T0[c] + l], bank4(b0 + 2, l), ACT.Copy).then_inc(s["oT_ready"], 1)
                    masked_keys(4 * hh + 3)


    @block.vector
    def _(dve):
        link = Chain(dve, s["dve_c"])
        for c in range(3):
            l = L[c]
            for hh in range(2):
                i, w, b0 = 2 * c + hh, buf[hh], 4 * hh

                def m(x):
                    return w[x][0:l, :, 0:l]
                dve.wait_ge(s["kk_done"], i + 1)
                dve.wait_ge(s["dt_ready"], i + 1)
                link(nc.vector.tensor_tensor(m(bB), bank4(b0 + 1, l)[0:l], m(bDT), ALU.mult))
                dve.wait_ge(s["sb_ready"], i + 1)
                nc.vector.tensor_tensor(m(bB), m(bB), m(bE), ALU.mult).then_inc(s["b_ready"], 1)
                nc.vector.tensor_tensor(m(bAT), bank4(b0 + 2, l)[0:l], m(bDT), ALU.mult).then_inc(s["at1_ready"], 1)
            for hh in range(2):
                i, w, b0 = 2 * c + hh, buf[hh], 4 * hh
                dve.wait_ge(s["dT_done"], i + 1)
                nc.vector.tensor_tensor(w[bD0][0:l, :, 0:l], bank4(b0, l)[0:l], bc_mid(BLK[0:l, 0:l], 4), ALU.mult).then_inc(s["d0_ready"], 1)
            for hh in range(2):
                i, w, b0 = 2 * c + hh, buf[hh], 4 * hh
                dve.wait_ge(s["sq2_done"], i + 1)
                nc.vector.tensor_copy(w[bB2][0:l, :, 0:l], bank4(b0 + 2, l)[0:l]).then_inc(s["b2_ready"], 1)
            for done, ready, bk in ((s["p4_done"], s["y2_ready"], 3), (s["p8_done"], s["y3_ready"], 2), (s["p9_done"], s["y4_ready"], 0)):
                for hh in range(2):
                    i, w, b0 = 2 * c + hh, buf[hh], 4 * hh
                    dve.wait_ge(done, i + 1)
                    nc.vector.tensor_tensor(w[bY][0:l, :, 0:l], w[bY][0:l, :, 0:l], bank4(b0 + bk, l)[0:l], ALU.add).then_inc(ready, 1)
            if c < 2:
                for k in range(3):
                    for hh in range(2):
                        w, b0 = buf[hh], 4 * hh
                        n = 6 * c + 2 * k + hh + 1
                        dve.wait_ge(s["lz_done"], n)
                        nc.vector.tensor_copy(w[bB2], bank4(b0 + 1, l)).then_inc(s["z_ready"], 1)
                    for hh in range(2):
                        w, b0 = buf[hh], 4 * hh
                        n = 6 * c + 2 * k + hh + 1
                        dve.wait_ge(s["lw_done"], n)
                        nc.vector.tensor_tensor(w[bY], w[bY], bank4(b0 + 3, l), ALU.subtract).then_inc(s["y_ready"], 1)
            def residual(hh):
                w, hs = buf[hh], slice(4 * hh, 4 * hh + 4)
                dve.wait_ge(s["ks_done"], 2 * (c - 1) + hh + 1)
                r = w[bE][0:l, :, :]
                link(nc.vector.tensor_tensor(r, bank4(4 * hh, 128)[0:l], bc_last(nbeg[0:l, c, hs], 128), ALU.mult))
                nc.vector.tensor_tensor(r, r, V[0:l, c, hs, :], ALU.add).then_inc(s["r_ready"], 1)

            def new_values(hh):
                w, hs = buf[hh], slice(4 * hh, 4 * hh + 4)
                dve.wait_ge(s["vn_done"], 2 * c + hh + 1)
                nc.vector.tensor_tensor(w[bDT][0:l, :, :], bank4(4 * hh + 1, 128)[0:l], bc_last(beta[0:l, c, hs], 128), ALU.mult).then_inc(s["vn_ready"], 1)

            def prompt_state(hh):
                hs = slice(4 * hh, 4 * hh + 4)
                dve.wait_ge(s["ds_done"], 2 * c + hh + 1)
                if c == 0:
                    nc.vector.tensor_copy(S[:, hs, :], bank4(4 * hh + 3, 128)).then_inc(s["s_ready"], 1)
                else:
                    e = egl[:, 1, hs] if c == 1 else egl3[:, 0, hs]
                    link(nc.vector.tensor_tensor(S[:, hs, :], S[:, hs, :], bc_last(e, 128), ALU.mult))
                    nc.vector.tensor_tensor(S[:, hs, :], S[:, hs, :], bank4(4 * hh + 3, 128), ALU.add).then_inc(s["s_ready"], 1)
            if c < 2:
                for hh in range(2):
                    if c:
                        residual(hh)
                    new_values(hh)
                    prompt_state(hh)
            else:
                residual(0)
                residual(1)
                new_values(0)
                new_values(1)
                for hh in range(2):
                    for h in range(4 * hh, 4 * hh + 4):
                        dve.wait_ge(s["su_done"], h + 1)
                        for q in range(8):
                            st = sample_state(h)[:, q, :]
                            ins = nc.vector.scalar_tensor_tensor(st, st, egl3[:, 1 + q, h:h + 1], bank4(4 * (h % 2) + q // 4, 128)[:, q % 4, :],
                                                                 ALU.mult, ALU.add)
                        ins.then_inc(s["su_ready"], 1)
                    prompt_state(hh)


    @block.tensor
    def _(pe):
        mm = nc.tensor.matmul

        def tr(out, in_, n):
            return nc.tensor.transpose(out, in_, ident[0:n, 0:n])

        for c in range(3):
            l = L[c]
            tk = slice(T0[c], T0[c] + l)
            mU = U if c < 2 else U3

            def four(b, lhs, rhs, hh, start=True):
                for h in range(4):
                    ins = mm(bank4(b, l)[0:l, h, :], lhs[0:l, h, 0:l], rhs[0:l, h, 0:l], start=True, stop=True)
                return ins
            for hh in range(2):
                i, w, b0 = 2 * c + hh, buf[hh], 4 * hh
                if c:
                    pe.wait_ge(s["s_ready"], i - 1)
                    pe.wait_ge(s["oT_ready"], i - 1)
                for h in range(4):
                    ins = mm(bank4(b0 + 1, l)[0:l, h, :], KT[:, 4 * hh + h, tk], KT[:, 4 * hh + h, tk], start=True, stop=True)
                for h in range(4):
                    ins = mm(bank4(b0 + 2, l)[0:l, h, :], KT[:, 4 * hh + h, tk], oaT[:, 4 * hh + h, tk], start=True, stop=True)
                ins.then_inc(s["kk_done"], 1)
                pe.wait_ge(s["xg_ready"], i + 1)
                for h in range(4):
                    ins = mm(bank4(b0, l)[0:l, h, :], w[bD2][0:l, h, 0:l], mU[0:l, 0:l], start=True, stop=True)
                ins.then_inc(s["diff_done"], 1)
                for h in range(4):
                    ins = mm(bank4(b0 + 3, l)[:, h, :], w[bB2][0:l, h, :], mU[0:l, 0:l], start=True, stop=True)
                ins.then_inc(s["eg_done"], 1)
            for hh in range(2):
                i, w, b0 = 2 * c + hh, buf[hh], 4 * hh
                pe.wait_ge(s["b_ready"], i + 1)
                for h in range(4):
                    ins = tr(bank4(b0, l)[0:l, h, :], w[bB][0:l, h, 0:l], l)
                ins.then_inc(s["dT_done"], 1)
            for hh in range(2):
                i, w, b0 = 2 * c + hh, buf[hh], 4 * hh
                pe.wait_ge(s["d0_ready"], i + 1)
                pe.wait_ge(s["b0_ready"], i + 1)
                pe.wait_ge(s["at1_ready"], i + 1)
                four(b0 + 1, w[bB0], w[bD0], hh)
                four(b0 + 2, w[bD0], w[bB0], hh).then_inc(s["sq2_done"], 1)
            for hh in range(2):
                i, w, b0 = 2 * c + hh, buf[hh], 4 * hh
                pe.wait_ge(s["d2_ready"], i + 1)
                pe.wait_ge(s["b2_ready"], i + 1)
                pe.wait_ge(s["y1_ready"], i + 1)
                pe.wait_ge(s["eg_ready"], i + 1)
                pe.wait_ge(s["d_ready"], i + 1)
                four(b0 + 3, w[bD2], w[bY], hh)
                four(b0, w[bB2], w[bD2], hh)
                four(b0 + 1, w[bD2], w[bB2], hh).then_inc(s["p4_done"], 1)
            for hh in range(2):
                i, w, b0 = 2 * c + hh, buf[hh], 4 * hh
                pe.wait_ge(s["d4_ready"], i + 1)
                pe.wait_ge(s["y2_ready"], i + 1)
                four(b0 + 2, w[bD0], w[bY], hh)
                pe.wait_ge(s["b4_ready"], i + 1)
                four(b0 + 3, w[bB0], w[bD0], hh).then_inc(s["p8_done"], 1)
            for hh in range(2):
                i, w, b0 = 2 * c + hh, buf[hh], 4 * hh
                pe.wait_ge(s["d8_ready"], i + 1)
                pe.wait_ge(s["y3_ready"], i + 1)
                four(b0, w[bD2], w[bY], hh).then_inc(s["p9_done"], 1)
            if c < 2:
                for k in range(3):
                    for hh in range(2):
                        w, b0 = buf[hh], 4 * hh
                        n = 6 * c + 2 * k + hh + 1
                        if k == 0:
                            pe.wait_ge(s["y4_ready"], 2 * c + hh + 1)
                        else:
                            pe.wait_ge(s["y_ready"], n - 2)
                        pe.wait_ge(s["e_ready"], n)
                        four(b0 + 1, w[bE], w[bY], hh)
                        for h in range(4):
                            ins = tr(bank4(b0 + 2, l)[:, h, :], w[bY][:, h, :], l)
                        ins.then_inc(s["lz_done"], 1)
                    for hh in range(2):
                        w, b0 = buf[hh], 4 * hh
                        n = 6 * c + 2 * k + hh + 1
                        pe.wait_ge(s["z_ready"], n)
                        pe.wait_ge(s["x_ready"], n)
                        four(b0 + 3, w[bD0], w[bB2], hh).then_inc(s["lw_done"], 1)
            def values(hh):
                i, w, b0 = 2 * c + hh, buf[hh], 4 * hh
                if c:
                    pe.wait_ge(s["r_ready"], i - 1)
                for h in range(4):
                    rhs = w[bE][0:l, h, :] if c else V[0:l, 0, 4 * hh + h, :]
                    ins = mm(bank4(b0 + 1, 128)[0:l, h, :], w[bY][0:l, h, 0:l], rhs, start=True, stop=True)
                ins.then_inc(s["vn_done"], 1)

            if c < 2:
                for hh in range(2):
                    i, w, b0 = 2 * c + hh, buf[hh], 4 * hh
                    pe.wait_ge(s["y_ready"], 6 * c + 4 + hh + 1)
                    if c == 1:
                        for h in range(4):
                            ins = mm(bank4(b0, 128)[:, h, :], KT[:, 4 * hh + h, tk], S[:, 4 * hh + h, :], start=True, stop=True)
                        ins.then_inc(s["ks_done"], 1)
                    values(hh)
                    pe.wait_ge(s["vn_ready"], i + 1)
                    pe.wait_ge(s["at_ready"], i + 1)
                    pe.wait_ge(s["qe_ready"], i + 1)
                    o = bank4(b0 + 2, l)
                    for h in range(4):
                        if c == 1:
                            mm(o[:, h, :], S[:, 4 * hh + h, :], w[bEG][:, h, 0:l], start=True, stop=False)
                        ins = mm(o[:, h, :], w[bDT][0:l, h, :], w[bAT][0:l, h, 0:l], start=(c == 0), stop=True)
                    ins.then_inc(s["o_done"], 1)
                    for h in range(4):
                        ins = mm(bank4(b0 + 3, 128)[:, h, :], Kd[0:l, c, 4 * hh + h, :], w[bDT][0:l, h, :], start=True, stop=True)
                    ins.then_inc(s["ds_done"], 1)
            else:
                def old_states(b, hh, stop):
                    for h in range(4):
                        for q in range(9):
                            st = S[:, 4 * hh + h, :] if q == 0 else sample_state(4 * hh + h)[:, q - 1, :]
                            ins = mm(bank4(b, 128)[0:l, h, :], SEGM[:, 4 * hh + h, q, :], st, start=(q == 0), stop=(stop and q == 8))
                        if not stop:
                            ins = mm(bank4(b, 128)[0:l, h, :], buf[hh][bAT][0:l, h, 0:l], buf[hh][bDT][0:l, h, :], start=False, stop=True)
                    return ins
                pe.wait_ge(s["ktm_ready"], 8)
                for hh in range(2):
                    pe.wait_ge(s["y4_ready"], 5 + hh)
                    if hh == 0:
                        pe.wait_ge(s["sa_in"], 16 * 8)
                    old_states(4 * hh, hh, True).then_inc(s["ks_done"], 1)
                values(0)
                values(1)
                for hh in range(2):
                    i, w, b0 = 2 * c + hh, buf[hh], 4 * hh
                    pe.wait_ge(s["vn_ready"], i + 1)
                    pe.wait_ge(s["at_ready"], i + 1)
                    pe.wait_ge(s["qm_ready"], 4 * hh + 4)
                    old_states(b0 + 2, hh, False).then_inc(s["o_done"], 1)
                    for h in range(4):
                        hd = 4 * hh + h
                        if h % 2:
                            pe.wait_ge(s["kdo_ready"], hd // 2 + 1)
                        else:
                            pe.wait_ge(s["kdm_ready"], hd // 2 + 1)
                        keys = KDM[hh][h % 2]
                        ins = mm(bank4(b0 + 3, 128)[:, h, :], keys[0:l, 0, :], w[bDT][0:l, h, :], start=True, stop=True)
                        if h == 3:
                            ins.then_inc(s["ds_done"], 1)
                        if hd >= 2:
                            pe.wait_ge(s["su_ready"], hd - 1)
                        else:
                            pe.wait_ge(s["vn_ready"], 6)
                        for q in range(8):
                            ins = mm(bank4(4 * (hd % 2) + q // 4, 128)[:, q % 4, :], keys[0:l, 1 + q, :], w[bDT][0:l, h, :], start=True, stop=True)
                        ins.then_inc(s["su_done"], 1)
                        if h == 1:
                            pe.wait_ge(s["otok_ready"], hh + 1)
                            for g in range(4):
                                ins = tr(bank4(b0 + 2, l)[:, g, :], w[bB][0:l, g, :], l)
                            ins.then_inc(s["otok_done"], 1)

    ctx.close()


def gla(k):
    nc, i_, o_ = k.nc, k.i_, k.o_
    ident, SL, SL3, U3, R03, GR, GM, ones, seg = k.ident, k.SL, k.SL3, k.U3, k.R03, k.GR, k.GM, k.ones, k.seg
    hH, hL, psum, bank4, unit_done, lrT = k.hH, k.hL, k.psum, k.bank4, k.unit_done, k.lrT
    QK = k.carve(0, 8 * NT, 8, NT)
    V = k.carve(2432, 3072, 3, D)
    Kd = k.carve(5504, 1536, 3, 512)
    LG = k.carve(7040, 1536, 3, 512)
    EX = [k.carve(8576 + 768 * p, 768, 6, 128) for p in range(2)]
    QP = [k.carve(10112 + 640 * p, 640, 5, 128) for p in range(2)]
    KP = [k.carve(11392 + 512 * p, 512, 4, 128) for p in range(2)]
    AM = [k.carve(12416 + 512 * p, 512, 4, 128) for p in range(2)]
    AT = [k.carve(13440 + 128 * p, 128) for p in range(2)]
    S = k.carve(13696, 1024, HB, 256)
    SS = [k.carve(14720 + 2048 * p, 2048, 8, 256) for p in range(2)]
    KM = [k.carve(18816 + 1152 * p, 1152, 9, 128) for p in range(2)]
    UP = k.carve(21120, 512)
    GB = k.carve(21632, 512)
    TL = [k.carve(22144 + 512 * p, 512) for p in range(2)]
    s = named(nc, "gla", """up_in qk_ready v_ready lg_done soft_ready lg_ready kb_done kd_done kdec_ready kd_ready
        ex_done ex_ready q_ready kp_ready pair_done at_ready o_done oT_ready ds_done s_ready
        ss_in0 ss_in1 ss_out sp_out km_ready su_done su_ready act_c dve_c""")
    ctx = ExitStack()
    block = ctx.enter_context(nc.Block())
    ss_in = (s["ss_in0"], s["ss_in1"])
    HI = [k.carve_r(8576 + SW * p, SW) for p in range(3)]
    SC3 = 3 * HB

    @block.sync
    def _(sp):
        for n in range(N_VB, N_Z):
            k.load_w(sp, n)
        sp.dma_start(UP[0:16, :], i_["gla_gate_up"][0]).then_inc(s["up_in"], 16)
        sp.dma_start(GB[0:1, :], i_["gla_gate_bias"]).then_inc(s["up_in"], 16)
        for h in range(2):
            sp.dma_start(SS[h][:, :, :], i_["state_gla"][0, :, h].rearrange("b k v -> k b v")).then_inc(ss_in[h], 16)
        for n in range(N_Z, N_Z + 8):
            k.load_w(sp, n)
        for h in range(HB):
            sp.wait_ge(s["su_ready"], 8 * h + 8)
            sp.dma_start(o_["sg_s"][0, :, h].rearrange("b k v -> k b v"), SS[h % 2][:, :, :]).then_inc(s["ss_out"], 16)
            if h < 2:
                sp.wait_ge(s["ss_out"], 16 * (h + 1))
                sp.dma_start(SS[h][:, :, :], i_["state_gla"][0, :, h + 2].rearrange("b k v -> k b v")).then_inc(ss_in[h], 16)
        sp.wait_ge(s["s_ready"], SC3)
        sp.dma_start(o_["sg_p"][0, 0].rearrange("h k v -> k h v"), S[:, :, :]).then_inc(s["sp_out"], 16)
        sp.wait_ge(s["ss_out"], 16 * HB)
        sp.wait_ge(s["sp_out"], 16)

    @block.gpsimd
    def _(pl):
        for c in range(3):
            l = L[c]
            for h in range(HB):
                i = HB * c + h
                p = i % 2
                pl.wait_ge(s["ex_ready"], i + 1)
                if i >= 2:
                    pl.wait_ge(s["pair_done"], i - 1)
                kk = QK[:, 4 + h, T0[c]:T0[c] + l]
                if c < 2:
                    nc.gpsimd.tensor_tensor(KP[p][:, :, :], bc_mid(kk, 4), EX[p][:, 2:6, :], ALU.mult).then_inc(s["kp_ready"], 1)
                else:
                    nc.gpsimd.tensor_tensor(KP[p][:, 3, 0:l], kk, EX[p][:, 5, 0:l], ALU.mult).then_inc(s["kp_ready"], 1)
                    pl.wait_ge(s["kd_ready"], 3)
                    if h >= 2:
                        pl.wait_ge(s["su_done"], 8 * (h - 1))
                    nc.gpsimd.tensor_tensor(KM[p][0:l, :, :], bc_mid(Kd[0:l, 2, 128 * h:128 * h + 128], 9), bc_last(seg[0:l, :], 128),
                                            ALU.mult).then_inc(s["km_ready"], 1)

    def out(act, i):
        c, h = divmod(i, HB)
        act.wait_ge(s["o_done"], i + 1)
        nc.scalar.activation(QK[:, h::4, T0[c]:T0[c] + L[c]], bank4(4 * (i % 2) + 3)[:, 0:2, 0:L[c]], ACT.Copy).then_inc(s["oT_ready"], 1)

    @block.scalar
    def _(act):
        link = Chain(act, s["act_c"])
        base = units(N_QB)
        for n in range(N_QB, N_QB + 3):
            k.high_part(act, n, HI)
        for b in range(8):
            act.wait_ge(unit_done, base + b + 1)
            nc.scalar.activation(QK[:, b, :], psum[b % 4][:, 0:NT], ACT.Copy, scale=128 ** -0.5 if b < 4 else 1.0).then_inc(s["qk_ready"], 1)
            if b % 2:
                k.high_part(act, N_QB + b // 2 + 3, HI)
        act.preload_act_table_set(LN_EXP)
        for c in range(3):
            l = L[c]
            act.wait_ge(s["lg_done"], c + 1)
            t = TL[c % 2][0:l, :]
            if c == 2:
                act.wait_ge(s["lg_ready"], 1)
            link(nc.scalar.activation(t, psum[4 + c][0:l, :], ACT.Abs))
            link(nc.scalar.activation(t, t, ACT.Exp, scale=-1.0))
            nc.scalar.activation(t, t, ACT.Ln, bias=1.0).then_inc(s["soft_ready"], 1)
        for u in range(12):
            q, c = divmod(u, 3)
            act.wait_ge(unit_done, base + 8 + u + 1)
            nc.scalar.activation(V[0:L[c], c, 256 * q:256 * q + 256], psum[u % 4][0:L[c], 0:256], ACT.Copy).then_inc(s["v_ready"], 1)
            if u == 2:
                k.high_part(act, N_Z - 1, HI)
        for c in range(3):
            l = L[c]
            act.wait_ge(s["kd_done"], c + 1)
            if c == 2:
                act.wait_ge(s["kd_ready"], 1)
            nc.scalar.activation(TL[c % 2][0:l, :], psum[4 + c % 2][0:l, :], ACT.Exp, scale=1 / TAU).then_inc(s["kdec_ready"], 1)
        for c in range(3):
            l = L[c]
            for h in range(HB):
                i = HB * c + h
                p = i % 2
                act.wait_ge(s["ex_done"], i + 1)
                if i >= 2:
                    act.wait_ge(s["q_ready"], i - 1)
                    act.wait_ge(s["kp_ready"], i - 1)
                    act.wait_ge(s["s_ready"], i - 1)
                if c == 2 and h >= 2:
                    act.wait_ge(s["su_ready"], 8 * (h - 1))
                a, b = bank4(4 * p), bank4(4 * p + 1)
                if c < 2:
                    nc.scalar.activation(EX[p][:, 0:4, :], a, ACT.Exp, scale=1 / TAU)
                    nc.scalar.activation(EX[p][:, 4, :], b[:, 0, :], ACT.Exp, scale=1 / TAU)
                    nc.scalar.activation(EX[p][:, 5, :], a[:, 1, :], ACT.Exp, scale=-1 / TAU).then_inc(s["ex_ready"], 1)
                else:
                    nc.scalar.activation(EX[p][:, 0:2, 0:l], a[:, 0:2, 0:l], ACT.Exp, scale=1 / TAU)
                    nc.scalar.activation(EX[p][:, 5, 0:l], a[:, 1, 0:l], ACT.Exp, scale=-1 / TAU).then_inc(s["ex_ready"], 1)
                if i:
                    out(act, i - 1)
        out(act, SC3 - 1)

    @block.vector
    def _(dve):
        link = Chain(dve, s["dve_c"])
        for n in range(N_QB, N_Z - 1):
            k.low_part(dve, nc.vector, n, HI)
        for c in range(3):
            l = L[c]
            dve.wait_ge(s["soft_ready"], c + 1)
            nc.vector.scalar_tensor_tensor(LG[0:l, c, :], psum[4 + c][0:l, :], 0.0, TL[c % 2][0:l, :], ALU.min, ALU.subtract).then_inc(s["lg_ready"], 1)
        k.low_part(dve, nc.vector, N_Z - 1, HI)
        for c in range(3):
            l = L[c]
            dve.wait_ge(s["kb_done"], c + 1)
            dve.wait_ge(s["kdec_ready"], c + 1)
            nc.vector.tensor_tensor(Kd[0:l, c, :], psum[6 + c % 2][0:l, :], TL[c % 2][0:l, :], ALU.mult).then_inc(s["kd_ready"], 1)

        def state(i):
            c, h = divmod(i, HB)
            p = i % 2
            e = EX[p][:, 0, (TAIL if c == 2 else 128) - 1:][:, 0:1]
            dve.wait_ge(s["ds_done"], i + 1)
            d = psum[4 * p + 2][:, 0:256]
            if c == 0:
                nc.vector.tensor_copy(S[:, h, :], d).then_inc(s["s_ready"], 1)
            else:
                nc.vector.scalar_tensor_tensor(S[:, h, :], S[:, h, :], e, d, ALU.mult, ALU.add).then_inc(s["s_ready"], 1)
            if c == 2:
                for b in range(8):
                    dve.wait_ge(s["su_done"], 8 * h + b + 1)
                    x = TAIL + TS * b + TS - 1
                    nc.vector.scalar_tensor_tensor(SS[h % 2][:, b, :], SS[h % 2][:, b, :], EX[p][:, 0, x:x + 1],
                                                   psum[4 * p + b % 2][:, 0:256], ALU.mult, ALU.add).then_inc(s["su_ready"], 1)
        for c in range(3):
            l = L[c]
            for h in range(HB):
                i = HB * c + h
                p = i % 2
                q = QK[:, h, T0[c]:T0[c] + l]
                dve.wait_ge(s["ex_ready"], i + 1)
                if i >= 2:
                    dve.wait_ge(s["o_done"], i - 1)
                if c < 2:
                    nc.vector.tensor_tensor(QP[p][:, :, :], bc_mid(q, 5), EX[p][:, 0:5, :], ALU.mult).then_inc(s["q_ready"], 1)
                else:
                    nc.vector.tensor_tensor(QP[p][:, 0:2, 0:l], bc_mid(q, 2), EX[p][:, 0:2, 0:l], ALU.mult).then_inc(s["q_ready"], 1)
                dve.wait_ge(s["pair_done"], i + 1)
                if c < 2:
                    link(nc.vector.tensor_tensor(AM[p][:, :, :], bank4(4 * p + 2), GM[:, :, :], ALU.mult))
                    nc.vector.tensor_reduce(AT[p][:, :], AM[p][:, :, :].rearrange("p a t -> p t a"), AX.X, ALU.add).then_inc(s["at_ready"], 1)
                else:
                    nc.vector.tensor_tensor(AT[p][0:l, 0:l], bank4(4 * p + 2)[0:l, 0, 0:l], U3[0:l, 0:l], ALU.mult).then_inc(s["at_ready"], 1)
                state(i)

    @block.tensor
    def _(pe):
        mm = nc.tensor.matmul
        for b in range(8):
            if b >= 4:
                pe.wait_ge(s["qk_ready"], b - 3)
            k.block_of_slot(pe, N_QB + b // 2, b % 2, b % 4, HI)
        pe.wait_ge(s["up_in"], 32)
        for c in range(3):
            l = L[c]
            mm(psum[4 + c][0:l, :], lrT[:, T0[c]:T0[c] + l], UP[0:16, :], start=True, stop=False)
            mm(psum[4 + c][0:l, :], ones[0:1, 0:l], GB[0:1, :], start=False, stop=True).then_inc(s["lg_done"], 1)
        for u in range(12):
            q, c = divmod(u, 3)
            n = N_VB + q
            if u < 4:
                pe.wait_ge(s["qk_ready"], 5 + u)
            else:
                pe.wait_ge(s["v_ready"], u - 3)
            pe.wait_ge(k.w_lo, n + 1)
            hi, lo = (w.rearrange("p (j c) -> p j c", j=KB) for w in (HI[n % 3], k.LOW[:, n % SLOTS, :]))
            for j in range(KB):
                x, y = (h[:, j, T0[c]:T0[c] + L[c]] for h in (hH, hL))
                mm(psum[u % 4][0:L[c], 0:256], x, hi[:, j, :], start=(j == 0), stop=False)
                mm(psum[u % 4][0:L[c], 0:256], x, lo[:, j, :], start=False, stop=False)
                ins = mm(psum[u % 4][0:L[c], 0:256], y, hi[:, j, :], start=False, stop=(j == KB - 1))
            ins.then_inc(unit_done, 1)
        pe.wait_ge(s["lg_ready"], 3)
        for c in range(3):
            l = L[c]
            if c == 2:
                pe.wait_ge(s["kd_ready"], 1)
            for h in range(HB):
                ins = nc.tensor.transpose(bank4(6 + c % 2)[0:l, h, :], QK[:, 4 + h, T0[c]:T0[c] + l], ident)
            ins.then_inc(s["kb_done"], 1)
            mm(psum[4 + c % 2][0:l, :], (SL if c < 2 else SL3)[0:l, 0:l], LG[0:l, c, :], start=True, stop=True).then_inc(s["kd_done"], 1)

        def exps(i):
            c, h = divmod(i, HB)
            l, p = L[c], i % 2
            lg = LG[0:l, c, 128 * h:128 * h + 128]
            if c < 2:
                mm(psum[4 * p][:, :], lg, GR[:, 0:4, :], start=True, stop=True)
                mm(bank4(4 * p + 1)[:, 0, :], lg, GR[:, 4, :], start=True, stop=True).then_inc(s["ex_done"], 1)
            else:
                mm(bank4(4 * p)[:, 0, 0:l], lg, U3[0:l, 0:l], start=True, stop=True)
                mm(bank4(4 * p)[:, 1, 0:l], lg, R03[0:l, 0:l], start=True, stop=True).then_inc(s["ex_done"], 1)

        pe.wait_ge(s["v_ready"], 12)
        pe.wait_ge(s["kd_ready"], 3)
        pe.wait_ge(s["kdec_ready"], 3)
        exps(0)
        for i in range(SC3):
            c, h = divmod(i, HB)
            l, p = L[c], i % 2
            tk = slice(T0[c], T0[c] + l)
            if c < 2 and i + 1 < SC3:
                if i >= 1:
                    pe.wait_ge(s["ex_ready"], i)
                exps(i + 1)
            pe.wait_ge(s["q_ready"], i + 1)
            pe.wait_ge(s["kp_ready"], i + 1)
            if i >= 2:
                pe.wait_ge(s["s_ready"], i - 1)
            if c < 2:
                for r, (kx, qx) in enumerate(((3, 1), (0, 2), (1, 3), (2, 4))):
                    ins = mm(bank4(4 * p + 2)[:, r, :], KP[p][:, kx, :], QP[p][:, qx, :], start=True, stop=True)
            else:
                ins = mm(bank4(4 * p + 2)[0:l, 0, 0:l], KP[p][:, 3, 0:l], QP[p][:, 1, 0:l], start=True, stop=True)
            ins.then_inc(s["pair_done"], 1)
            if i >= 2:
                pe.wait_ge(s["oT_ready"], i - 1)
            o = bank4(4 * p + 3)
            if c == 2:
                pe.wait_ge(ss_in[h % 2], 16 * (h // 2 + 1))
                for e in range(2):
                    for b in range(9):
                        t0, t1 = (0, TAIL) if b == 0 else (TAIL + TS * (b - 1), TAIL + TS * b)
                        st = S[:, h, :] if b == 0 else SS[h % 2][:, b - 1, :]
                        mm(o[:, e, t0:t1], st[:, 128 * e:128 * e + 128], QP[p][:, 0, t0:t1], start=(e == 0 and b == 0), stop=False, skip_group_check=True)
            pe.wait_ge(s["at_ready"], i + 1)
            for e in range(2):
                if c == 1:
                    pe.wait_ge(s["s_ready"], i - 3)
                    mm(o[:, e, 0:l], S[:, h, 128 * e:128 * e + 128], QP[p][:, 0, 0:l], start=True, stop=False)
                ins = mm(o[:, e, 0:l], V[0:l, c, 256 * h + 128 * e:256 * h + 128 * e + 128], AT[p][0:l, 0:l],
                         start=(c == 0), stop=True, skip_group_check=(c == 2))
            ins.then_inc(s["o_done"], 1)
            if c == 2:
                pe.wait_ge(s["km_ready"], h + 1)
            mm(psum[4 * p + 2][:, 0:256], KM[p][0:l, 0, :] if c == 2 else Kd[0:l, c, 128 * h:128 * h + 128],
               V[0:l, c, 256 * h:256 * h + 256], start=True, stop=True).then_inc(s["ds_done"], 1)
            if c == 2:
                pe.wait_ge(s["ex_ready"], i + 1)
                for b in range(8):
                    if b >= 2:
                        pe.wait_ge(s["su_ready"], 8 * h + b - 1)
                    mm(psum[4 * p + b % 2][:, 0:256], KM[p][0:l, 1 + b, :], V[0:l, 2, 256 * h:256 * h + 256], start=True, stop=True).then_inc(s["su_done"], 1)
                if i + 1 < SC3:
                    if h >= 1:
                        pe.wait_ge(s["su_ready"], 8 * h)
                    exps(i + 1)
    ctx.close()


X_AT = 17696


def merge(k):
    nc, i_, o_ = k.nc, k.i_, k.o_
    oaT, ones, psum, unit_done, epsc, na, nb = k.oaT, k.ones, k.psum, k.unit_done, k.epsc, k.na, k.nb
    obT = k.carve(0, 8 * NT, 8, NT)
    WN = k.carve(3072, D)
    WR = k.carve(4096, 288, KB, 36)
    GA = k.carve(8576, 8 * NT, 8, NT)
    GB = k.carve(11008, 8 * NT, 8, NT)
    MG = k.carve(13440, 8 * NT, 8, NT)
    ZT = k.carve(15872, 2 * NT, 2, NT)
    RS = k.carve(15872 + 2 * NT, 2 * NT, 2, NT)
    assert 15872 + 4 * NT <= X_AT
    HI = [k.carve_r(at, SW) for at in (4384, 4384 + SW, 21984)]
    X = k.carve(X_AT, 3072, 3, D)
    SQ = [k.carve(X_AT + 3072 + 2 * NT * p, 2 * NT, 2, NT) for p in range(2)]
    s = named(nc, "merge", """x_in par_in sq_ready sum_done rs_ready on_ready silu_ready gated gate_ready ya_ready yb_ready mg_ready
        x1_ready act_c""")
    ctx = ExitStack()
    block = ctx.enter_context(nc.Block())
    base = units(N_Z)

    def ob(j):
        return obT[:, j // 2 + 4 * (j % 2), :]

    @block.sync
    def _(sp):
        k.load_x(sp, X, s["x_in"])
        sp.dma_start(WN, i_["norm_final"].partition_broadcast(128)).then_inc(s["par_in"], 16)
        sp.dma_start(WR[:, :, 0:4], i_["router_group_w"][0].rearrange("(p j) g -> p j g", j=KB)).then_inc(s["par_in"], 16)
        sp.dma_start(WR[:, :, 4:36], i_["router_expert_w"][0].rearrange("(p j) e -> p j e", j=KB)).then_inc(s["par_in"], 16)
        for n in range(N_Z + 8, N_PRE):
            k.load_w(sp, n)
        sp.wait_ge(s["par_in"], 48)

    @block.gpsimd
    def _(pl):
        for h in range(12):
            if h >= 2:
                pl.wait_ge(s["sum_done"], h - 1)
            if h < 8:
                nc.gpsimd.tensor_tensor(SQ[h % 2][:, 0, :], oaT[:, h, :], oaT[:, h, :], ALU.mult).then_inc(s["sq_ready"], 1)
            else:
                v = obT[:, h - 8::4, :]
                nc.gpsimd.tensor_tensor(SQ[h % 2][:, :, :], v, v, ALU.mult).then_inc(s["sq_ready"], 1)
        for b in range(8):
            pl.wait_ge(s["yb_ready"], b + 1)
            nc.gpsimd.tensor_tensor(MG[:, b, :], MG[:, b, :], GB[:, b, :], ALU.add).then_inc(s["mg_ready"], 1)

    @block.scalar
    def _(act):
        link = Chain(act, s["act_c"])
        act.preload_act_table_set(LN_EXP)
        for n in range(N_Z, N_Z + 3):
            k.high_part(act, n, HI)
        for h in range(12):
            act.wait_ge(s["sum_done"], h + 1)
            if h >= 2:
                act.wait_ge(s["on_ready"], h - 1 if h - 1 <= 8 else 8 + 2 * (h - 9))
            link(nc.scalar.activation(RS[:, h % 2, :], psum[4 + h % 4][:, 0:NT], ACT.Ln, scale=1 / 128 if h < 8 else 1 / 256, bias=epsc))
            nc.scalar.activation(RS[:, h % 2, :], RS[:, h % 2, :], ACT.Exp, scale=-0.5).then_inc(s["rs_ready"], 1)
        for u in range(16):
            act.wait_ge(unit_done, base + u + 1)
            if u >= 2:
                act.wait_ge(s["gated"], u - 1)
            nc.scalar.activation(ZT[:, u % 2, :], psum[u % 4][:, 0:NT], ACT.Silu).then_inc(s["silu_ready"], 1)
            if u % 2:
                k.high_part(act, N_Z + u // 2 + 3, HI)
        for u in range(16, 32):
            act.wait_ge(unit_done, base + u + 1)
            nc.scalar.activation((GA if u < 24 else GB)[:, u % 8, :], psum[u % 4][:, 0:NT], ACT.Sigmoid).then_inc(s["gate_ready"], 1)
            if u % 2 and N_Z + u // 2 + 3 < N_PA:
                k.high_part(act, N_Z + u // 2 + 3, HI)

    @block.vector
    def _(dve):
        for n in range(N_Z, N_Z + 3):
            k.low_part(dve, nc.vector, n, HI)
        for h in range(12):
            dve.wait_ge(s["rs_ready"], h + 1)
            if h < 8:
                nc.vector.scalar_tensor_tensor(oaT[:, h, :], oaT[:, h, :], na, RS[:, h % 2, :], ALU.mult, ALU.mult).then_inc(s["on_ready"], 1)
            else:
                for e in range(2):
                    v = obT[:, h - 8 + 4 * e, :]
                    nc.vector.scalar_tensor_tensor(v, v, nb[:, e:e + 1], RS[:, h % 2, :], ALU.mult, ALU.mult).then_inc(s["on_ready"], 1)
        dve.wait_ge(s["on_ready"], 16)
        for u in range(16):
            dve.wait_ge(s["silu_ready"], u + 1)
            v = oaT[:, u, :] if u < 8 else ob(u - 8)
            nc.vector.tensor_tensor(v, v, ZT[:, u % 2, :], ALU.mult).then_inc(s["gated"], 1)
            if u % 2:
                k.low_part(dve, nc.vector, N_Z + u // 2 + 3, HI)
        for n in range(N_Z + 11, N_PA):
            k.low_part(dve, nc.vector, n, HI)
        for b in range(8):
            dve.wait_ge(unit_done, base + 32 + b + 1)
            dve.wait_ge(s["gate_ready"], b + 1)
            nc.vector.tensor_tensor(MG[:, b, :], psum[b % 4][:, 0:NT], GA[:, b, :], ALU.mult).then_inc(s["ya_ready"], 1)
        for b in range(8):
            dve.wait_ge(unit_done, base + 40 + b + 1)
            dve.wait_ge(s["gate_ready"], 8 + b + 1)
            dve.wait_ge(s["ya_ready"], b + 1)
            nc.vector.tensor_tensor(GB[:, b, :], psum[b % 4][:, 0:NT], GB[:, b, :], ALU.mult).then_inc(s["yb_ready"], 1)
        dve.wait_ge(s["x_in"], 80)
        for u in range(12):
            q, c = divmod(u, 3)
            dve.wait_ge(unit_done, base + 48 + u + 1)
            x = X[0:L[c], c, 256 * q:256 * q + 256]
            nc.vector.tensor_tensor(x, x, psum[4 + u % 4][0:L[c], 0:256], ALU.add).then_inc(s["x1_ready"], 1)

    @block.tensor
    def _(pe):
        mm = nc.tensor.matmul
        for h in range(12):
            pe.wait_ge(s["sq_ready"], h + 1)
            if h >= 4:
                pe.wait_ge(s["rs_ready"], h - 3)
            if h < 8:
                ins = mm(psum[4 + h % 4][:, 0:NT], ones[:, :], SQ[h % 2][:, 0, :], start=True, stop=True)
            else:
                mm(psum[4 + h % 4][:, 0:NT], ones[:, :], SQ[h % 2][:, 0, :], start=True, stop=False)
                ins = mm(psum[4 + h % 4][:, 0:NT], ones[:, :], SQ[h % 2][:, 1, :], start=False, stop=True)
            ins.then_inc(s["sum_done"], 1)
            if h in (3, 5, 7, 9):
                u = (h - 3) // 2
                k.block_of_slot(pe, N_Z + u // 2, u % 2, u, HI)
        for u in range(4, 48):
            if u - 4 < 16:
                pe.wait_ge(s["silu_ready"], u - 3)
            elif u - 4 < 32:
                pe.wait_ge(s["gate_ready"], u - 19)
            elif u - 4 < 40:
                pe.wait_ge(s["ya_ready"], u - 35)
            else:
                pe.wait_ge(s["yb_ready"], u - 43)
            if u == 32:
                pe.wait_ge(s["gated"], 8)
            if u == 40:
                pe.wait_ge(s["gated"], 16)
            if 32 <= u < 40:
                moving = lambda j: oaT[:, j, :]
            elif u >= 40:
                moving = ob
            if u < 32:
                k.block_of_slot(pe, N_Z + u // 2, u % 2, u % 4, HI)
            else:
                k.block_of_projection(pe, N_Z + u // 2, u % 2, u % 4, moving)
        for u in range(12):
            q, c = divmod(u, 3)
            n = N_WO + q
            k.arrived(pe, n)
            if u >= 4:
                pe.wait_ge(s["x1_ready"], u - 3)
            for j in range(KB):
                if u == 0:
                    pe.wait_ge(s["mg_ready"], j + 1)
                ins = mm(psum[4 + u % 4][0:L[c], 0:256], MG[:, j, T0[c]:T0[c] + L[c]], k.slot8(n)[:, j, :], start=(j == 0), stop=(j == KB - 1))
            ins.then_inc(unit_done, 1)
    ctx.close()


def experts(k):
    nc, i_, o_ = k.nc, k.i_, k.o_
    ident, SU, ones, hT, psum, bank4, epsc, nf, rbias = k.ident, k.SU, k.ones, k.hT, k.psum, k.bank4, k.epsc, k.nf, k.rbias
    X = k.carve(X_AT, 3072, 3, D)
    XN = k.carve(0, 3072, 3, D)
    WN = k.carve(3072, D)
    WR = k.carve(4096, 288, KB, 36)
    XGH = k.carve_r(4384, 1024, KB, 128)
    XGL = k.hL.rearrange("p a b -> p (a b)")[:, 0:1024].rearrange("p (j t) -> p j t", j=KB)
    P = k.carve_r(5408, 384, 3, 128)
    PT = k.carve_r(5792, NT)
    SIL = [k.carve(6096 + 256 * p, 256) for p in range(2)]
    H = [k.carve(6608 + 256 * p, 256) for p in range(2)]
    HXH = [k.carve_r(7120 + 256 * p, 256, 2, 128) for p in range(2)]
    HXL = [k.carve_r(16896 + 256 * p, 256, 2, 128) for p in range(2)]
    OGH = k.carve_r(7632, 1024)
    OGL = k.rounded("masks", 8 * 128, 1024)
    WF = k.carve(7632, 1024)
    HIGU = [k.carve_r(9728, 4096, KB, 512), k.carve_r(20768, 4096, KB, 512)]
    HIDN = [k.carve_r(13824, 2048, 2, 1024), k.rounded("oaT", 0, 2048, 2, 1024)]
    XNH = [k.rounded("hT", 0, 1024), k.rounded("hT", 1024, 1024), k.carve_r(15872, 1024)]
    XNL = k.carve_r(0, 3072, 3, D)
    LOW = k.LOW
    IO = k.carve(8656, 128)
    LT = k.carve(8784, 108, 3, 36)
    TE = k.carve(8892, 96)
    WT = k.carve(8988, 1)
    DESC = k.carve(8989, 8)
    at = [9000]

    def take(n, *dims):
        at[0] += n
        return k.carve(at[0] - n, n, *dims)
    gmax, gkey, gsum, pg, a1, a2, b1, b2, w1, w2, key, ss, rstd, tcount, tmax = (take(3) for _ in range(15))
    eq4, ky4, oh4, ex4 = (take(12, 3, 4) for _ in range(4))
    le, eq8, ky8, oh1, oh2, comb = (take(24, 3, 8) for _ in range(6))
    CMB = take(8)
    IOI = k.carve(9600, 128).bitcast(I32)
    TE4 = TE.rearrange("p (c g e) -> p c g e", g=4, e=8)
    s = named(nc, "experts", """io_ready rstd_ready xn_ready xT_done xT_ready rt_done d4_ready ex4_ready d2_ready w2_ready oh_ready
        rank_done comb_ready cnt_ready p_ready pt_done pt_ready xg_done xgh_ready xgl_ready cmb_ready gu_done sil_ready
        h_ready hx_done hxh_ready hxl_ready wf_in xnh_ready xnl_ready hi_gu lo_gu hi_dn lo_dn
        dn_done ogh_ready og_ready sc_done y_added x2_ready r3_ready key_back fin_ready out_done act_c dve_c pool_c""")
    ctx = ExitStack()
    block = ctx.enter_context(nc.Block())
    PASSES = 3
    assert PASSES * CAP >= NT

    def place(kind, e):
        g, e = divmod(e, EPG)
        if kind < 2:
            m = kind if e == 0 else 3 * e - 1 + kind
        else:
            m = 3 * e + 4 if e < EPG - 1 else PER_GROUP - 1
        return m + PER_GROUP * g
    ORDER = sorted(((place(kind, e), kind, e) for kind in range(3) for e in range(EPG)))

    def expert_load(sp, v, g, p, m):
        _, kind, e = ORDER[m]
        before = m - SLOTS
        if before >= 0:
            _, kb, eb = ORDER[before]
            sp.wait_ge(s["dn_done"] if kb == 2 else s["gu_done"], v * EPG + (eb + 1))
        elif isinstance(v, int) and v == 0:
            sp.wait_ge(k.unit_done, units(N_PRE + before + 1))
        else:
            _, kb, eb = ORDER[before + PER_GROUP]
            sp.wait_ge(s["dn_done"] if kb == 2 else s["gu_done"], (v - 1) * EPG + (eb + 1))
        w = i_[("expert_w_gate", "expert_w_up", "expert_w_down")[kind]][0][g * EPG + e]
        sp.dma_start(k.ring[:, m % SLOTS, :], w.rearrange("(p j) c -> p (j c)", p=128)).then_inc(k.ring_in[m % SLOTS], 16)

    def slot(m):
        return LOW[:, m % SLOTS, :].rearrange("p (j c) -> p j c", j=KB)

    def slot_wait(eng, v, m):
        eng.wait_ge(k.ring_in[m % SLOTS], v * 48 + 16 * (N_PRE // SLOTS + 1 + m // SLOTS))

    def groups(eng, p, body):
        with eng.Fori(0, NG - 1) as g:
            body(g + NG * p, True)
        body(NG * p + NG - 1, False)

    def before(p):
        return (0, 0) if p == 0 else (NG * p - 1, EPG)

    def passes(eng, body):
        body(0)
        eng.wait_ge(s["cnt_ready"], 1)
        count = eng.value_load(k.cnti[0:1, 0:1], min_val=0, max_val=NT)
        for p in range(1, PASSES):
            with eng.If(count > CAP * p):
                body(p)

    @block.sync
    def _(sp):
        sp.dma_start(WF, i_["norm_ffn"][0].partition_broadcast(128)).then_inc(s["wf_in"], 16)

        def one_pass(p):
            for m in range(SLOTS):
                expert_load(sp, NG * p, 0, p, m)
            with sp.Fori(0, NG - 1) as g:
                v = g + NG * p
                for m in range(SLOTS, PER_GROUP):
                    expert_load(sp, v, g, p, m)
                for m in range(SLOTS):
                    expert_load(sp, v + 1, g + 1, p, m)
            for m in range(SLOTS, PER_GROUP):
                expert_load(sp, NG * p + NG - 1, NG - 1, p, m)
        passes(sp, one_pass)
        sp.wait_ge(s["wf_in"], 16)
        yp, ys = o_["y_p"][0], o_["y_s"].rearrange("b t d -> (b t) d")
        for c in range(3):
            sp.wait_ge(s["fin_ready"], c + 1)
            if c == 0:
                sp.dma_start(yp[0:112, :], X[META:128, 0, :]).then_inc(s["out_done"], 16)
            elif c == 1:
                sp.dma_start(yp[112:240, :], X[:, 1, :]).then_inc(s["out_done"], 16)
            else:
                sp.dma_start(yp[240:256, :], X[0:TAIL, 2, :]).then_inc(s["out_done"], 16)
                sp.dma_start(ys, X[TAIL:L[2], 2, :]).then_inc(s["out_done"], 16)
        sp.wait_ge(s["out_done"], 64)

    @block.gpsimd
    def _(pl):
        link = Chain(pl, s["pool_c"])
        link(nc.gpsimd.iota(IOI, [[1, 128]], base=0, channel_multiplier=0))
        for e in range(8):
            nc.gpsimd.memset(DESC[:, e:e + 1], float(8 - e))
        nc.gpsimd.memset(LT[:, :, :], 0.0)
        link(nc.gpsimd.tensor_copy(IO, IOI))
        pl.drain().then_inc(s["io_ready"], 1)
        for c in range(3):
            pl.wait_ge(s["xnh_ready"], c + 1)
            nc.gpsimd.tensor_tensor(XNL[0:L[c], c, :], XN[0:L[c], c, :], XNH[c][0:L[c], :], ALU.subtract).then_inc(s["xnl_ready"], 1)

        def low_down(v, e):
            m = place(2, e)
            pl.wait_ge(s["hi_dn"], v * EPG + (e + 1))
            nc.gpsimd.tensor_tensor(LOW[:, m % SLOTS, :], k.ring[:, m % SLOTS, :],
                                    HIDN[e % 2].rearrange("p j c -> p (j c)"), ALU.subtract).then_inc(s["lo_dn"], 1)

        def one_pass(p):
            low_down(*before(p))

            def one_group(v, more):
                for e in range(1, EPG + more):
                    low_down(v, e)
            groups(pl, p, one_group)
        passes(pl, one_pass)

    @block.scalar
    def _(act):
        link = Chain(act, s["act_c"])

        def inverse_rms(signal):
            for c in range(3):
                l = L[c]
                link(nc.scalar.activation(XN[0:l, c, :], X[0:l, c, :], ACT.Square, accum_out=ss[0:l, c:c + 1]))
                link(nc.scalar.activation(ss[0:l, c:c + 1], ss[0:l, c:c + 1], ACT.Ln, scale=1 / D, bias=epsc[0:l, :]))
                nc.scalar.activation(rstd[0:l, c:c + 1], ss[0:l, c:c + 1], ACT.Exp, scale=-0.5).then_inc(signal, 1)
        act.preload_act_table_set(LN_EXP)
        inverse_rms(s["rstd_ready"])
        act.wait_ge(s["d4_ready"], 1)
        nc.scalar.activation(ex4[:, :, :], ex4[:, :, :], ACT.Exp).then_inc(s["ex4_ready"], 1)
        act.wait_ge(s["d2_ready"], 1)
        nc.scalar.activation(w2[:, :], w2[:, :], ACT.Exp).then_inc(s["w2_ready"], 1)

        act.wait_ge(s["rt_done"], 3)
        for c in range(3):
            nc.scalar.activation(XNH[c][0:L[c], :], XN[0:L[c], c, :], ACT.Copy).then_inc(s["xnh_ready"], 1)

        def high_gate_up(v, e):
            for half in range(2):
                m = place(half, e)
                slot_wait(act, v, m)
                nc.scalar.activation(HIGU[e % 2][:, :, 256 * half:256 * half + 256], k.slot8(m), ACT.Copy).then_inc(s["hi_gu"], 1)

        def high_down(v, e):
            m = place(2, e)
            slot_wait(act, v, m)
            nc.scalar.activation(HIDN[e % 2].rearrange("p j c -> p (j c)"), k.ring[:, m % SLOTS, :], ACT.Copy).then_inc(s["hi_dn"], 1)

        def tokens(v, last):
            for q in range(2):
                act.wait_ge(s["xg_done"], v * 3 + (q + 1))
                nc.scalar.activation(XGH[:, 4 * q:4 * q + 4, :], bank4(6 + q), ACT.Copy).then_inc(s["xgh_ready"], 1)
            act.wait_ge(s["xg_done"], v * 3 + 3)
            if not (isinstance(v, int) and v == 0):
                act.wait_ge(s["h_ready"], last)
            nc.scalar.activation(CMB[:, :], psum[2][:, 400:408], ACT.Copy).then_inc(s["cmb_ready"], 1)

        def turned_places(v):
            act.wait_ge(s["pt_done"], v + 1)
            nc.scalar.activation(PT[:, :], psum[3][:, 0:NT], ACT.Copy).then_inc(s["pt_ready"], 1)

        def high_hidden(v, e):
            act.wait_ge(s["hx_done"], v * EPG + (e + 1))
            if e >= 2:
                act.wait_ge(s["dn_done"], v * EPG + (e - 1))
            nc.scalar.activation(HXH[e % 2][:, :, :], psum[2 + e % 2][:, 0:256].rearrange("p (j t) -> p j t", j=2),
                                 ACT.Copy).then_inc(s["hxh_ready"], 1)

        def one_pass(p):
            v0, e0 = before(p)
            high_gate_up(v0, e0)
            high_down(v0, e0)
            high_gate_up(v0, e0 + 1)
            tokens(NG * p, EPG * NG * p)
            turned_places(NG * p)

            def one_group(v, more):
                for e in range(EPG):
                    if e >= 1:
                        high_hidden(v, e - 1)
                    act.wait_ge(s["gu_done"], v * EPG + (e + 1))
                    nc.scalar.activation(SIL[e % 2][:, :], psum[e % 2][:, 0:256], ACT.Silu).then_inc(s["sil_ready"], 1)
                    if more or e + 2 < EPG:
                        high_gate_up(v, e + 2)
                    if more or e + 1 < EPG:
                        if e:
                            act.wait_ge(s["dn_done"], v * EPG + e)
                        high_down(v, e + 1)
                if more:
                    tokens(v + 1, v * EPG + EPG)
                high_hidden(v, EPG - 1)
                act.wait_ge(s["dn_done"], v * EPG + EPG)
                for half in range(2):
                    nc.scalar.activation(OGH[:, 512 * half:512 * half + 512], psum[4 + half][:, :], ACT.Copy).then_inc(s["ogh_ready"], 1)
                if more:
                    turned_places(v + 1)
            groups(act, p, one_group)
        passes(act, one_pass)
        act.preload_act_table_set(LN_EXP)
        act.wait_ge(s["x2_ready"], 1)
        inverse_rms(s["r3_ready"])

    @block.vector
    def _(dve):
        V = nc.vector
        link = Chain(dve, s["dve_c"])
        for c in range(3):
            l = L[c]
            dve.wait_ge(s["rstd_ready"], c + 1)
            if c == 0:
                dve.wait_ge(s["wf_in"], 16)
            V.scalar_tensor_tensor(XN[0:l, c, :], X[0:l, c, :], rstd[0:l, c:c + 1], WF[0:l, :], ALU.mult, ALU.mult).then_inc(s["xn_ready"], 1)
        for j in range(KB):
            dve.wait_ge(s["xT_done"], j + 1)
            V.tensor_copy(hT[:, j, :], psum[j % 4][:, 0:NT]).then_inc(s["xT_ready"], 1)
        dve.wait_ge(s["io_ready"], 1)
        for c in range(3):
            dve.wait_ge(s["rt_done"], c + 1)
            link(V.tensor_copy(LT[0:L[c], c, :], psum[4 + c][0:L[c], 0:36]))

        def first_of_max(v, n, out_max, eq, ky, oh, top):
            link(V.tensor_reduce(out_max, v, AX.X, ALU.max))
            link(V.tensor_tensor(eq, v, bc_last(out_max, n), ALU.is_equal))
            link(V.tensor_tensor(ky, eq, bc_mid(DESC[:, 8 - n:8], 3), ALU.mult))
            link(V.tensor_reduce(top, ky, AX.X, ALU.max))
            link(V.tensor_tensor(oh, ky, bc_last(top, n), ALU.is_equal))
        lg = LT[:, :, 0:4]
        first_of_max(lg, 4, gmax, eq4, ky4, oh4, gkey)
        dve.drain().then_inc(s["oh_ready"], 1)
        V.tensor_tensor(ex4, lg, bc_last(gmax, 4), ALU.subtract).then_inc(s["d4_ready"], 1)
        link(V.tensor_tensor(TE4, LT[:, :, 4:36].rearrange("p c (g e) -> p c g e", g=4), bc_last(oh4, 8), ALU.mult))
        link(V.tensor_reduce(le, TE4.rearrange("p c g e -> p c e g"), AX.X, ALU.add))
        first_of_max(le, 8, a1, eq8, ky8, oh1, b1)
        link(V.scalar_tensor_tensor(le, oh1, -1e30, le, ALU.mult, ALU.add))
        first_of_max(le, 8, a2, eq8, ky8, oh2, b2)
        V.tensor_tensor(w2, a2, a1, ALU.subtract).then_inc(s["d2_ready"], 1)
        dve.wait_ge(s["ex4_ready"], 1)
        link(V.tensor_reduce(gsum, ex4, AX.X, ALU.add))
        link(V.reciprocal(pg, gsum))
        dve.wait_ge(s["w2_ready"], 1)
        link(V.tensor_scalar(w1, w2, 1.0, None, ALU.add))
        link(V.reciprocal(w1, w1))
        link(V.tensor_tensor(w1, w1, pg, ALU.mult))
        link(V.tensor_tensor(w2, w2, w1, ALU.mult))
        link(V.tensor_tensor(comb, oh1, bc_last(w1, 8), ALU.mult))
        link(V.tensor_tensor(oh2, oh2, bc_last(w2, 8), ALU.mult))
        V.tensor_tensor(comb, comb, oh2, ALU.add).then_inc(s["comb_ready"], 1)
        dve.wait_ge(s["rank_done"], 4)
        link(V.tensor_scalar(tmax, gkey, -1024.0, 4096.0, ALU.mult, ALU.add))
        for c in range(3):
            l = L[c]
            link(V.tensor_tensor(ky4[0:l, c, :], psum[4 + c][0:l, 0:4], oh4[0:l, c, :], ALU.mult))
            link(V.tensor_reduce(key[0:l, c:c + 1], ky4[0:l, c, :], AX.X, ALU.add))
            link(V.tensor_tensor(key[0:l, c:c + 1], key[0:l, c:c + 1], tmax[0:l, c:c + 1], ALU.add))
        link(V.tensor_reduce(tcount[:, 0:1], psum[7][:, 0:4], AX.X, ALU.max))
        V.tensor_copy(k.cnti[:, :], tcount[:, 0:1]).then_inc(s["cnt_ready"], 1)

        def places(v):
            for c in range(3):
                ins = V.tensor_scalar(P[0:L[c], c, :], IO[0:L[c], :], key[0:L[c], c:c + 1], None, ALU.is_equal)
            ins.then_inc(s["p_ready"], 1)
            dve.wait_ge(s["p_ready"], v + 1)
            for c in range(3):
                V.tensor_scalar(key[0:L[c], c:c + 1], key[0:L[c], c:c + 1], -1024.0, None, ALU.add)

        def low_gate_up(v, e):
            for half in range(2):
                m = place(half, e)
                dve.wait_ge(s["hi_gu"], v * 2 * EPG + (2 * e + half + 1))
                V.tensor_tensor(slot(m), k.slot8(m), HIGU[e % 2][:, :, 256 * half:256 * half + 256], ALU.subtract).then_inc(s["lo_gu"], 1)

        def tokens(v):
            for q in range(2):
                dve.wait_ge(s["xgh_ready"], v * 2 + (q + 1))
                V.tensor_tensor(XGL[:, 4 * q:4 * q + 4, :], bank4(6 + q), XGH[:, 4 * q:4 * q + 4, :], ALU.subtract).then_inc(s["xgl_ready"], 1)

        def low_hidden(v, e):
            dve.wait_ge(s["hxh_ready"], v * EPG + (e + 1))
            V.tensor_tensor(HXL[e % 2][:, :, :], psum[2 + e % 2][:, 0:256].rearrange("p (j t) -> p j t", j=2),
                            HXH[e % 2][:, :, :], ALU.subtract).then_inc(s["hxl_ready"], 1)

        def one_pass(p):
            if p:
                dve.wait_ge(s["key_back"], p)
                dve.wait_ge(s["pt_done"], NG * p)
            places(NG * p)
            v0, e0 = before(p)
            low_gate_up(v0, e0)
            tokens(NG * p)
            low_gate_up(v0, e0 + 1)

            def one_group(v, more):
                dve.wait_ge(s["cmb_ready"], v + 1)
                for e in range(EPG):
                    if e >= 1:
                        low_hidden(v, e - 1)
                    dve.wait_ge(s["sil_ready"], v * EPG + (e + 1))
                    if e >= 2:
                        dve.wait_ge(s["hx_done"], v * EPG + (e - 1))
                    V.scalar_tensor_tensor(H[e % 2][:, :], SIL[e % 2][:, :], CMB[:, e:e + 1], psum[e % 2][:, 256:512],
                                           ALU.mult, ALU.mult).then_inc(s["h_ready"], 1)
                    if more or e + 2 < EPG:
                        low_gate_up(v, e + 2)
                    if more and e == 1:
                        dve.wait_ge(s["pt_done"], v + 1)
                        places(v + 1)
                if more:
                    tokens(v + 1)
                low_hidden(v, EPG - 1)
                for half in range(2):
                    dve.wait_ge(s["ogh_ready"], v * 2 + (half + 1))
                    o = slice(512 * half, 512 * half + 512)
                    V.tensor_tensor(OGL[:, o], psum[4 + half][:, :], OGH[:, o], ALU.subtract).then_inc(s["og_ready"], 1)
                for q in range(6):
                    c, half = divmod(q, 2)
                    dve.wait_ge(s["sc_done"], v * 6 + (q + 1))
                    x = X[0:L[c], c, 512 * half:512 * half + 512]
                    V.tensor_tensor(x, x, psum[6 + q % 2][0:L[c], :], ALU.add).then_inc(s["y_added"], 1)
                dve.wait_ge(s["y_added"], v * 6 + 6)
            groups(dve, p, one_group)
            if p + 1 < PASSES:
                for c in range(3):
                    ins = V.tensor_scalar(key[0:L[c], c:c + 1], key[0:L[c], c:c + 1], 1024.0 * NG - CAP, None, ALU.add)
                ins.then_inc(s["key_back"], 1)
        passes(dve, one_pass)
        dve.drain().then_inc(s["x2_ready"], 1)
        for c in range(3):
            l = L[c]
            dve.wait_ge(s["r3_ready"], c + 1)
            V.scalar_tensor_tensor(X[0:l, c, :], X[0:l, c, :], rstd[0:l, c:c + 1], WN[0:l, :], ALU.mult, ALU.mult).then_inc(s["fin_ready"], 1)

    @block.tensor
    def _(pe):
        mm, tr = nc.tensor.matmul, nc.tensor.transpose
        for j in range(KB):
            if j >= 4:
                pe.wait_ge(s["xT_ready"], j - 3)
            for c in range(3):
                if j == 0:
                    pe.wait_ge(s["xn_ready"], c + 1)
                ins = tr(psum[j % 4][:, T0[c]:T0[c] + L[c]], XN[0:L[c], c, j::KB], ident[0:L[c], 0:L[c]])
            ins.then_inc(s["xT_done"], 1)
        pe.wait_ge(s["xT_ready"], KB)
        for c in range(3):
            l = L[c]
            for j in range(KB):
                mm(psum[4 + c][0:l, 0:36], hT[:, j, T0[c]:T0[c] + l], WR[:, j, :], start=(j == 0), stop=False)
            mm(psum[4 + c][0:l, 0:36], ones[0:1, 0:l], rbias[0:1, :], start=False, stop=True).then_inc(s["rt_done"], 1)
        pe.wait_ge(s["oh_ready"], 1)
        for c in range(3):
            l = L[c]
            ins = mm(psum[4 + c][0:l, 0:4], SU[0:l, 0:l], oh4[0:l, c, :], start=True, stop=(c == 0))
            for b in range(c):
                ins = mm(psum[4 + c][0:l, 0:4], ones[:, 0:l], oh4[:, b, :], start=False, stop=(b == c - 1))
            ins.then_inc(s["rank_done"], 1)
        for c in range(3):
            ins = mm(psum[7][:, 0:4], ones[0:L[c], :], oh4[0:L[c], c, :], start=(c == 0), stop=(c == 2))
        ins.then_inc(s["rank_done"], 1)
        pe.wait_ge(s["comb_ready"], 1)
        pe.wait_ge(s["cnt_ready"], 1)

        pe.wait_ge(s["xnl_ready"], 3)

        def gather(v):
            pe.wait_ge(s["p_ready"], v + 1)
            for q in range(2):
                for j in range(4):
                    for c in range(3):
                        l = L[c]
                        mm(bank4(6 + q)[:, j, :], XNH[c][0:l, 4 * q + j::KB], P[0:l, c, :], start=(c == 0), stop=False)
                        ins = mm(bank4(6 + q)[:, j, :], XNL[0:l, c, 4 * q + j::KB], P[0:l, c, :], start=False, stop=(c == 2))
                ins.then_inc(s["xg_done"], 1)
            for c in range(3):
                ins = mm(psum[2][:, 400:408], P[0:L[c], c, :].bitcast(F32), comb[0:L[c], c, :], start=(c == 0), stop=(c == 2))
            ins.then_inc(s["xg_done"], 1)

        def turn_places(v):
            for c in range(3):
                ins = tr(psum[3][:, T0[c]:T0[c] + L[c]], P[0:L[c], c, :].bitcast(F32), ident[0:L[c], 0:L[c]])
            ins.then_inc(s["pt_done"], 1)

        def gate_up(v, e, part):
            if part == 0:
                pe.wait_ge(s["lo_gu"], v * 2 * EPG + (2 * e + 2))
                if e >= 2 and e < EPG:
                    pe.wait_ge(s["h_ready"], v * EPG + (e - 1))
            b = psum[e % 2]
            for j in range(4 * part, 4 * part + 4):
                mm(b[:, :], XGH[:, j, :], HIGU[e % 2][:, j, :], start=(j == 0), stop=False)
                for half in range(2):
                    mm(b[:, 256 * half:256 * half + 256], XGH[:, j, :], slot(place(half, e))[:, j, :], start=False, stop=False)
                ins = mm(b[:, :], XGL[:, j, :], HIGU[e % 2][:, j, :], start=False, stop=(j == KB - 1))
            if part == 1:
                ins.then_inc(s["gu_done"], 1)

        def turn(v, e):
            pe.wait_ge(s["h_ready"], v * EPG + (e + 1))
            if e == 1:
                pe.wait_ge(s["pt_ready"], v + 1)
            if e >= 2:
                pe.wait_ge(s["hxl_ready"], v * EPG + (e - 1))
            for j in range(2):
                ins = tr(psum[2 + e % 2][:, 128 * j:128 * j + 128], H[e % 2][:, j::2], ident)
            ins.then_inc(s["hx_done"], 1)

        def down(v, e):
            pe.wait_ge(s["lo_dn"], v * EPG + (e + 1))
            pe.wait_ge(s["hxl_ready"], v * EPG + (e + 1))
            w = k.shaped(LOW[:, place(2, e) % SLOTS, :], (2, 1024))
            for j in range(2):
                for x, y in ((HXH, HIDN[e % 2]), (HXH, w), (HXL, HIDN[e % 2])):
                    for half in range(2):
                        ins = mm(psum[4 + half][:, :], x[e % 2][:, j, :], y[:, j, 512 * half:512 * half + 512],
                                 start=(e == 0 and j == 0 and x is HXH and y is not w), stop=(e == EPG - 1 and j == 1 and x is HXL))
            ins.then_inc(s["dn_done"], 1)

        def scatter(v, q):
            c, half = divmod(q, 2)
            if q < 2:
                pe.wait_ge(s["og_ready"], v * 2 + (half + 1))
            else:
                pe.wait_ge(s["y_added"], v * 6 + (q - 1))
            o = slice(512 * half, 512 * half + 512)
            mm(psum[6 + q % 2][0:L[c], :], PT[:, T0[c]:T0[c] + L[c]], OGH[:, o], start=True, stop=False)
            mm(psum[6 + q % 2][0:L[c], :], PT[:, T0[c]:T0[c] + L[c]], OGL[:, o], start=False, stop=True).then_inc(s["sc_done"], 1)

        def one_pass(p):
            gather(NG * p)
            turn_places(NG * p)
            pe.wait_ge(s["xgl_ready"], 2 * NG * p + 2)
            v0, e0 = before(p)
            gate_up(v0, e0, 0)
            gate_up(v0, e0, 1)

            def one_group(v, more):
                for e in range(1, EPG):
                    gate_up(v, e, 0)
                    turn(v, e - 1)
                    gate_up(v, e, 1)
                    down(v, e - 1)
                if more:
                    gather(v + 1)
                turn(v, EPG - 1)
                down(v, EPG - 1)
                if more:
                    pe.wait_ge(s["xgl_ready"], v * 2 + 4)
                    gate_up(v, EPG, 0)
                scatter(v, 0)
                scatter(v, 1)
                if more:
                    gate_up(v, EPG, 1)
                for q in range(2, 6):
                    scatter(v, q)
                if more:
                    turn_places(v + 1)
                    pe.wait_ge(s["y_added"], v * 6 + 6)
            groups(pe, p, one_group)
            pe.wait_ge(s["y_added"], 6 * NG * p + 6 * NG)
        passes(pe, one_pass)
    ctx.close()


def build(nc, i_, o_):
    with ExitStack() as ctx:
        k = Core(nc, ctx, i_, o_)
        front(k)
        delta(k)
        gla(k)
        merge(k)
        experts(k)


_INS = ['x_prompt', 'x_sample', 'state_delta', 'state_conv', 'state_gla', 'meta_tokens', 'norm_mix', 'w_in',
        'conv_w', 'a_log', 'dt_bias', 'norm_a', 'gla_gate_up', 'gla_gate_bias', 'norm_b', 'w_proj_a', 'w_proj_b',
        'w_out', 'norm_ffn', 'router_group_w', 'router_group_b', 'router_expert_w', 'router_expert_b',
        'expert_w_gate', 'expert_w_up', 'expert_w_down', 'norm_final']
_OUTS = {'y_p': (1, SEQ, D), 'y_s': (NB, TS, D), 'sd_p': (1, 1, HA, 128, 128), 'conv_p': (1, 1, CW - 1, CONV),
         'sg_p': (1, 1, HB, 128, 256), 'sd_s': (1, NB, HA, 128, 128), 'conv_s': (1, NB, CW - 1, CONV),
         'sg_s': (1, NB, HB, 128, 256)}


def kernel(**inputs):
    import numpy as _np
    import concourse.bacc as _bacc
    from concourse import mybir as _mybir
    from concourse.bass_utils import run_bass_kernel_spmd as _run

    nc = _bacc.Bacc("TRN2", target_bir_lowering=False, num_devices=1)
    arrays, ins, outs = {}, {}, {}
    for name in _INS:
        a = _np.ascontiguousarray(inputs[name])
        arrays[f"in_{name}"] = a
        ins[name] = nc.dram_tensor(f"in_{name}", a.shape, _mybir.dt.from_np(a.dtype), kind="ExternalInput").ap()
    for name, shape in _OUTS.items():
        outs[name] = nc.dram_tensor(f"out_{name}", shape, _mybir.dt.float32, kind="ExternalOutput").ap()
    build(nc, ins, outs)
    r = _run(nc, [arrays], core_ids=[0])
    return tuple(r.results[0][f"out_{name}"] for name in _OUTS)
```

```python
from contextlib import ExitStack

import numpy as np

import concourse.bass as bass
from concourse import mybir

F32 = mybir.dt.float32
F32R = mybir.dt.float32r
I32 = mybir.dt.int32
ALU = mybir.AluOpType
ACT = mybir.ActivationFunctionType
AX = mybir.AxisListType

D = 1024
KB = D // 128
META, SEQ = 16, 256
TP = META + SEQ
NB, TS = 8, 4
NT = TP + NB * TS
L = (128, 128, NT - 256)
T0 = (0, 128, 256)
TAIL = TP - 256
HA, HB = 8, 4
CONV = 3 * D
NCB = CONV // 128
CW = 4
XW = TP + CW - 1 + NB * (TS + CW - 1)
XS = TP + CW - 1
NG, EPG = 4, 8
FF = 256
CAP = 128
SLOTS = 8
SW = 2048
EPS = 1e-6
LN_EXP = "natural_log_exp_and_others"
TAU = 16.0
C_QKV, C_Z, C_BA, C_QB, C_KB, C_VB, C_RB, C_LR, C_GA, C_GB = 0, 3072, 4096, 4112, 4624, 5136, 6160, 7184, 7200, 8224
WIN = ([C_QKV + 256 * i for i in range(12)] + [C_QB, C_QB + 256, C_KB, C_KB + 256] + [C_VB + 256 * i for i in range(4)]
       + [C_Z + 256 * i for i in range(4)] + [C_RB + 256 * i for i in range(4)]
       + [C_GA + 256 * i for i in range(4)] + [C_GB + 256 * i for i in range(4)])
N_QB, N_VB, N_Z, N_PA = 12, 16, 20, len(WIN)
N_WO = N_PA + 8
N_PRE = N_WO + 4
PER_GROUP = 3 * EPG


def units(n):
    return sum(3 if N_VB <= k < N_Z or k >= N_WO else 2 for k in range(n))


def named(nc, stage, names):
    return {n: nc.alloc_semaphore(f"{stage}_{n}") for n in names.split()}


class Chain:
    def __init__(self, eng, sem):
        self.eng, self.sem, self.n = eng, sem, 0

    def __call__(self, ins):
        self.n += 1
        ins.then_inc(self.sem, 1)
        self.eng.wait_ge(self.sem, self.n)


def bc_mid(ap2, n):
    return ap2.unsqueeze(1).to_broadcast([ap2.shape[0], n, ap2.shape[1]])


def bc_last(ap, n):
    k = len(ap.shape)
    return ap.unsqueeze(k).to_broadcast([*ap.shape, n])


def segment_mask(nc, pl, MT, ready):
    tests = ((MT[:, 0, :], [[-1, L[2]]], TAIL - 1), (MT[:, 1:9, :], [[-TS, NB], [1, L[2]]], -TAIL),
             (MT[:, 1:9, :], [[TS, NB], [-1, L[2]]], TAIL + TS - 1))
    nc.gpsimd.memset(MT[:, :, :], 1.0).then_inc(ready, 1)
    for n, (ap, pattern, base) in enumerate(tests):
        pl.wait_ge(ready, n + 1)
        nc.gpsimd.affine_select(out=ap, in_=ap, compare_op=ALU.is_ge, fill=0.0, base=base, pattern=pattern,
                                channel_multiplier=0).then_inc(ready, 1)
    pl.wait_ge(ready, 4)


class Core:

    def __init__(self, nc, ctx, i_, o_):
        self.nc, self.ctx, self.i_, self.o_ = nc, ctx, i_, o_

        self.addr, self.views = {}, 0

        def sb(name, shape, dt=F32):
            v = ctx.enter_context(nc.sbuf_tensor(name, shape, dt))
            self.addr[name] = nc.sbuf_base - 4 * int(np.prod(shape[1:]))
            return v
        self.ring = sb("ring", [128, SLOTS, SW])
        self.hT = sb("hT", [128, KB, NT])
        self.hH = self.rounded("hT", 0, KB * NT, KB, NT)
        self.hL = sb("hL", [128, KB, NT], F32R)
        self.oaT = sb("oaT", [128, HA, NT])
        m = self.masks = sb("masks", [128, 21, 128])
        self.ident, self.U, self.SL, self.SU, self.BLK = (m[:, k, :] for k in range(5))
        self.PAIR = [m[:, k, :] for k in range(5, 8)]
        self.GR = m[:, 8:13, :]
        self.GM = m[:, 13:17, :]
        self.U3, self.SL3, self.SU3, self.R03 = (m[:, k, :] for k in range(17, 21))
        self.ones = sb("ones", [128, 128])
        self.seg = sb("seg", [128, 9])
        self.lrT = sb("lrT", [48, NT])[32:48, :]
        self.small = sb("small", [128, 1300])
        self.at = 0
        self.cnti = sb("cnti", [128, 1], I32)
        self.AR = 24960
        self.arena = sb("arena", [128, self.AR])
        P = self.piece
        self.epsc = P(1)
        self.ss, self.rstd = P(3), P(3)
        self.nm, self.nf = P(8), P(8)
        self.cw = P(CW * NCB, CW, NCB)
        self.na, self.nb = P(1), P(2)
        self.sm = P(48, 3, 16)
        self.t1, self.t2 = P(24, 3, 8), P(24, 3, 8)
        self.beta = P(24, 3, 8)
        self.nbeg = P(24, 3, 8)
        self.gg = P(24, 3, 8)
        self.kw = P(24, 3, 8)
        self.egl = P(16, 2, 8)
        self.egl3, self.gm3 = P(72, 9, 8), P(72, 9, 8)
        self.hrow, self.hbc = P(16), P(16)
        self.rbias = P(36)
        self.psum = [ctx.enter_context(nc.psum_tensor(f"ps{k}", [128, 512], F32)) for k in range(8)]
        self.ring_in = [ctx.enter_context(nc.semaphore(f"ring_in{s}")) for s in range(SLOTS)]
        self.unit_done = ctx.enter_context(nc.semaphore("unit_done"))
        self.w_hi = ctx.enter_context(nc.semaphore("w_hi"))
        self.w_lo = ctx.enter_context(nc.semaphore("w_lo"))
        self.stored = ctx.enter_context(nc.semaphore("stored"))
        self.LOW = self.rounded("ring", 0, SLOTS * SW, SLOTS, SW)
        self.w_in = i_["w_in"][0].rearrange("(p j) c -> p j c", j=KB)

    @staticmethod
    def shaped(v, dims):
        if len(dims) == 2:
            return v.rearrange("p (a b) -> p a b", b=dims[1])
        if len(dims) == 3:
            return v.rearrange("p (a b c) -> p a b c", b=dims[1], c=dims[2])
        return v

    def piece(self, n, *dims):
        v = self.small[:, self.at:self.at + n]
        self.at += n
        assert self.at <= 1300
        return self.shaped(v, dims)

    def carve(self, off, n, *dims):
        assert off + n <= self.AR, (off, n)
        return self.shaped(self.arena[:, off:off + n], dims)

    def rounded(self, tensor, off, n, *dims):
        self.views += 1
        v = self.nc.alloc_sbuf_tensor_at(f"rounded{self.views}", [128, n], F32R, offset=self.addr[tensor] + 4 * off)
        return self.shaped(v[:, :], dims)

    def carve_r(self, off, n, *dims):
        assert off + n <= self.AR, (off, n)
        return self.rounded("arena", off, n, *dims)

    def slot8(self, n):
        return self.ring[:, n % SLOTS, :].rearrange("p (j c) -> p j c", j=KB)

    def bank4(self, b, l=128):
        return self.psum[b][:, :].rearrange("p (h t) -> p h t", h=4)[:, :, 0:l]

    def load_w(self, sp, n):
        if n >= SLOTS:
            sp.wait_ge(self.unit_done, units(n - SLOTS + 1))
        if n < N_PA:
            src = self.w_in[:, :, WIN[n]:WIN[n] + 256]
        else:
            m, q = divmod(n - N_PA, 4)
            w = self.i_[("w_proj_a", "w_proj_b", "w_out")[m]][0]
            src = w.rearrange("(j p) c -> p j c", p=128)[:, :, 256 * q:256 * q + 256]
        sp.dma_start(self.slot8(n), src).then_inc(self.ring_in[n % SLOTS], 16)

    def load_x(self, sp, X, signal):
        xp = self.i_["x_prompt"]
        sp.dma_start(X[0:META, 0, :], self.i_["meta_tokens"][:, :]).then_inc(signal, 16)
        sp.dma_start(X[META:128, 0, :], xp[0, 0:112, :]).then_inc(signal, 16)
        sp.dma_start(X[:, 1, :], xp[0, 112:240, :]).then_inc(signal, 16)
        sp.dma_start(X[0:TAIL, 2, :], xp[0, 240:256, :]).then_inc(signal, 16)
        sp.dma_start(X[TAIL:L[2], 2, :], self.i_["x_sample"].rearrange("b t d -> (b t) d")).then_inc(signal, 16)

    def high_part(self, act, n, HI):
        self.arrived(act, n)
        if n >= 3:
            act.wait_ge(self.unit_done, units(n - 2))
        self.nc.scalar.activation(HI[n % 3], self.ring[:, n % SLOTS, :], ACT.Copy).then_inc(self.w_hi, 1)

    def low_part(self, eng, on, n, HI):
        eng.wait_ge(self.w_hi, n + 1)
        if n:
            eng.wait_ge(self.w_lo, n)
        on.tensor_tensor(self.LOW[:, n % SLOTS, :], self.ring[:, n % SLOTS, :], HI[n % 3], ALU.subtract).then_inc(self.w_lo, 1)

    def arrived(self, pe, n):
        pe.wait_ge(self.ring_in[n % SLOTS], 16 * (n // SLOTS + 1))

    def block_of_slot(self, pe, n, q, b, HI, xh=None, xl=None):
        xh, xl = xh or (lambda j: self.hH[:, j, :]), xl or (lambda j: self.hL[:, j, :])
        pe.wait_ge(self.w_lo, n + 1)
        h, lo = (w.rearrange("p (j c) -> p j c", j=KB) for w in (HI[n % 3], self.LOW[:, n % SLOTS, :]))
        c = slice(128 * q, 128 * q + 128)
        for j in range(KB):
            self.nc.tensor.matmul(self.psum[b][:, 0:NT], h[:, j, c], xh(j), start=(j == 0), stop=False)
            self.nc.tensor.matmul(self.psum[b][:, 0:NT], h[:, j, c], xl(j), start=False, stop=False)
            ins = self.nc.tensor.matmul(self.psum[b][:, 0:NT], lo[:, j, c], xh(j), start=False, stop=(j == KB - 1))
        ins.then_inc(self.unit_done, 1)


KEYS_FIRST = tuple(enumerate([*range(8, 16), *range(8)]))
STORED_FRONT = 16 * 2
STORED_DELTA = 16 * (2 + HA + 1)
STORED_GLA = STORED_DELTA + 16 * 3
A1 = 8576


def front(k):
    nc, i_, o_ = k.nc, k.i_, k.o_
    ident, U, SL, SU, BLK, PAIR, GR, GM = k.ident, k.U, k.SL, k.SU, k.BLK, k.PAIR, k.GR, k.GM
    U3, SL3, SU3, R03, ones, seg, masks = k.U3, k.SL3, k.SU3, k.R03, k.ones, k.seg, k.masks
    hH, hL, oaT, psum, unit_done, w_in, lrT = k.hH, k.hL, k.oaT, k.psum, k.unit_done, k.w_in, k.lrT
    epsc, ss, rstd, nm, nf, cw, na, nb, sm, t1, t2 = k.epsc, k.ss, k.rstd, k.nm, k.nf, k.cw, k.na, k.nb, k.sm, k.t1, k.t2
    beta, nbeg, gg, kw, egl, egl3, gm3, hrow, hbc, rbias = k.beta, k.nbeg, k.gg, k.kw, k.egl, k.egl3, k.gm3, k.hrow, k.hbc, k.rbias
    KT = k.carve(0, HA * NT, HA, NT)
    Kd = k.carve(2432, 3072, 3, 8, 128)
    V = k.carve(5504, 3072, 3, 8, 128)
    X = k.carve(A1, 3072, 3, D)
    XN = k.carve(A1 + 3072, 3072, 3, D)
    SC = k.carve(A1 + 6144, CONV)
    SCO = k.carve(A1 + 9216, CONV)
    CWR = k.carve(A1 + 12288, 128)
    wsm = k.carve(A1 + 12416, KB * 48, KB, 48)
    smT = k.carve(23424, NT)
    HI = [k.carve_r(21376, SW), k.carve_r(A1 + 9216, SW), k.carve_r(11480, SW)]
    XC = k.carve(A1, 3 * XW, 3, XW)
    CV = k.carve(A1 + 3 * XW, 2 * XW, 2, XW)
    VT = k.carve(A1 + 5 * XW, 2 * NT, 2, NT)
    LAST = k.carve(A1 + 5 * XW + 2 * NT, NCB * 27, NCB, 27)
    SQ = k.carve(A1 + 3 * XW, 2 * NT, 2, NT)
    RS = k.carve(A1 + 3 * XW + 2 * NT, 2 * NT, 2, NT)
    s = named(nc, "front", """x_in par_in late_in sc_in ident_ready mask_ready rstd_ready xn_ready xT_done xT_evac small_done smT_ready small_ready
        hist_done hist_ready conv_ready conv_silu last_ready last_done last_evac sq_ready ssum_done rs_ready
        qk_ready vT_done vT_evac kT_done kT_evac par_done par_ready g_ready gsum_done gsum_ready lr_done lr_ready
        act_c dve_c pool_c""")
    ctx = ExitStack()
    block = ctx.enter_context(nc.Block())

    @block.sync
    def _(sp):
        k.load_x(sp, X, s["x_in"])
        sp.dma_start(nm, i_["norm_mix"][0].rearrange("(p j) -> p j", j=KB)).then_inc(s["par_in"], 16)
        sp.dma_start(wsm[:, :, 0:16], w_in[:, :, C_BA:C_BA + 16]).then_inc(s["par_in"], 16)
        for q in (16, 32):
            sp.dma_start(wsm[:, :, q:q + 16], w_in[:, :, C_LR:C_LR + 16]).then_inc(s["par_in"], 16)
        sp.dma_start(CWR[0:CW * NCB, :], i_["conv_w"][0].rearrange("i (b c) -> (i b) c", c=128)).then_inc(s["par_in"], 16)
        sp.dma_start(hrow[0:1, 0:8], i_["a_log"]).then_inc(s["par_in"], 16)
        sp.dma_start(hrow[0:1, 8:16], i_["dt_bias"]).then_inc(s["par_in"], 16)
        sp.dma_start(SC[0:24, :], i_["state_conv"][0].rearrange("b r c -> (b r) c")).then_inc(s["sc_in"], 16)
        for n in range(N_VB):
            k.load_w(sp, n)
        sp.dma_start(na, i_["norm_a"][0].rearrange("(p a) -> p a", a=1)).then_inc(s["late_in"], 16)
        for a in range(2):
            sp.dma_start(nb[:, a:a + 1], i_["norm_b"][0, 128 * a:128 * a + 128].rearrange("(p a) -> p a", a=1)).then_inc(s["late_in"], 16)
        sp.dma_start(nf, i_["norm_ffn"][0].rearrange("(p j) -> p j", j=KB)).then_inc(s["late_in"], 16)
        sp.dma_start(rbias[0:1, 0:4], i_["router_group_b"]).then_inc(s["late_in"], 16)
        sp.dma_start(rbias[0:1, 4:36], i_["router_expert_b"]).then_inc(s["late_in"], 16)
        sp.wait_ge(s["last_evac"], 6)
        sp.dma_start(o_["conv_p"][0, 0], SCO[0:3, :]).then_inc(k.stored, 16)
        sp.dma_start(o_["conv_s"][0].rearrange("b r c -> (b r) c"), SCO[3:27, :]).then_inc(k.stored, 16)
        sp.wait_ge(s["late_in"], 96)


    @block.gpsimd
    def _(pl):
        link = Chain(pl, s["pool_c"])

        def keep(ap, pattern, base, cm):
            link(nc.gpsimd.affine_select(out=ap, in_=ap, compare_op=ALU.is_ge, fill=0.0, base=base,
                                   pattern=pattern, channel_multiplier=cm))

        def blocks(ap, m):
            v = ap.rearrange("p (a b) -> p a b", b=m)
            n = ap.shape[1] // m
            keep(v, [[-m, n], [0, m]], 0, 1)
            keep(v, [[m, n], [0, m]], m - 1, -1)
        link(nc.gpsimd.memset(epsc, EPS))
        link(nc.gpsimd.memset(ones[:, :], 1.0))
        link(nc.gpsimd.memset(ident, 1.0))
        keep(ident, [[1, 128]], 0, -1)
        keep(ident, [[-1, 128]], 0, 1)
        pl.drain().then_inc(s["ident_ready"], 1)
        link(nc.gpsimd.memset(masks[:, 1:, :], 1.0))
        link(nc.gpsimd.memset(seg[:, :], 1.0))
        keep(U, [[1, 128]], 0, -1)
        keep(SL, [[-1, 128]], -1, 1)
        keep(SU, [[1, 128]], -1, -1)
        blocks(BLK, 16)
        for M, m in zip(PAIR, (16, 32, 64)):
            v = M.rearrange("p (a h b) -> p a h b", h=2, b=m)
            n = 128 // (2 * m)
            keep(v, [[-2 * m, n], [-1000, 2], [0, m]], -m, 1)
            keep(v, [[2 * m, n], [0, 2], [0, m]], 2 * m - 1, -1)
        link(nc.gpsimd.tensor_copy(GR[:, 0, :], U))
        for r, m in ((1, 8), (2, 64), (3, 32), (4, 16)):
            v = GR[:, r, :].rearrange("p (a h b) -> p a h b", h=2, b=m)
            for h, src in ((0, SL), (1, U)):
                half = src.rearrange("p (a h b) -> p a h b", h=2, b=m)
                if r == 1 and h == 0:
                    link(nc.gpsimd.tensor_scalar(v[:, :, h, :], half[:, :, h, :], -1.0, None, ALU.mult))
                else:
                    link(nc.gpsimd.tensor_copy(v[:, :, h, :], half[:, :, h, :]))
            blocks(GR[:, r, :], m)
        link(nc.gpsimd.tensor_tensor(GM[:, 0, :], U, BLK, ALU.mult))
        for r, m in ((1, 64), (2, 32), (3, 16)):
            v = GM[:, r, :].rearrange("p (a h b) -> p a h b", h=2, b=m)
            n = 128 // (2 * m)
            keep(v, [[-2 * m, n], [0, 2], [0, m]], 0, 1)
            keep(v, [[2 * m, n], [1000, 2], [0, m]], m - 1 - 1000, -1)
        for M, src in ((U3, U), (SL3, SL), (SU3, SU)):
            link(nc.gpsimd.tensor_copy(M, src))
            keep(M[:, 0:TAIL], [[0, TAIL]], TAIL - 1, -1)
            v = M[:, TAIL:L[2]].rearrange("p (a b) -> p a b", b=TS)
            keep(v, [[-TS, NB], [0, TS]], -TAIL, 1)
            keep(v, [[TS, NB], [0, TS]], TAIL + TS - 1, -1)
        link(nc.gpsimd.tensor_copy(R03[:, 0:TAIL], GR[:, 1, 0:TAIL]))
        link(nc.gpsimd.tensor_copy(R03[:, TAIL:L[2]], U3[:, TAIL:L[2]]))
        keep(seg[:, 0:1], [[0, 1]], TAIL - 1, -1)
        keep(seg[:, 1:9], [[-TS, NB]], -TAIL, 1)
        keep(seg[:, 1:9], [[TS, NB]], TAIL + TS - 1, -1)
        pl.drain().then_inc(s["mask_ready"], 1)

        for b in range(NCB):
            pl.wait_ge(s["hist_ready"], b + 1)
            x = XC[:, b % 3, :]
            nc.gpsimd.tensor_copy(LAST[:, b, 0:3], x[:, TP:TP + 3])
            nc.gpsimd.tensor_copy(LAST[:, b, 3:27].rearrange("p (a r) -> p a r", r=3),
                            x[:, XS:].rearrange("p (a r) -> p a r", r=TS + 3)[:, :, TS:]).then_inc(s["last_ready"], 1)
            if b % 2 and b // 2 + 3 < N_QB:
                k.low_part(pl, nc.gpsimd, b // 2 + 3, HI)
        pl.wait_ge(s["conv_silu"], NCB)
        for i, b in KEYS_FIRST:
            if i >= 2:
                pl.wait_ge(s["ssum_done"], i - 1)
            src = (oaT if b < 8 else KT)[:, b % 8, :]
            nc.gpsimd.tensor_tensor(SQ[:, i % 2, :], src, src, ALU.mult).then_inc(s["sq_ready"], 1)


    @block.scalar
    def _(act):
        link = Chain(act, s["act_c"])
        act.preload_act_table_set(LN_EXP)
        act.wait_ge(s["x_in"], 80)
        act.wait_ge(s["ident_ready"], 1)
        for c in range(3):
            l = L[c]
            link(nc.scalar.activation(XN[0:l, c, :], X[0:l, c, :], ACT.Square, accum_out=ss[0:l, c:c + 1]))
            link(nc.scalar.activation(ss[0:l, c:c + 1], ss[0:l, c:c + 1], ACT.Ln, scale=1.0 / D, bias=epsc[0:l, :]))
            nc.scalar.activation(rstd[0:l, c:c + 1], ss[0:l, c:c + 1], ACT.Exp, scale=-0.5).then_inc(s["rstd_ready"], 1)
        k.high_part(act, 0, HI)
        k.high_part(act, 1, HI)
        act.wait_ge(s["par_done"], 2)
        link(nc.scalar.activation(hbc, psum[5][:, 0:16], ACT.Copy))
        link(nc.scalar.activation(hbc[:, 0:8], hbc[:, 0:8], ACT.Exp))
        nc.scalar.activation(cw.rearrange("p i b -> p (i b)"), psum[4][:, 0:CW * NCB], ACT.Copy).then_inc(s["par_ready"], 1)
        act.wait_ge(s["lr_done"], 1)
        nc.scalar.activation(smT[0:16, :], psum[7][0:16, 200:200 + NT], ACT.Copy).then_inc(s["smT_ready"], 1)
        nc.scalar.activation(lrT, psum[7][32:48, 200:200 + NT], ACT.Copy).then_inc(s["lr_ready"], 1)
        act.wait_ge(s["small_done"], 3)
        for c in range(3):
            nc.scalar.activation(sm[0:L[c], c, :], psum[6][0:L[c], 16 * c:16 * c + 16], ACT.Copy).then_inc(s["small_ready"], 1)
        act.wait_ge(s["small_ready"], 3)
        act.wait_ge(s["g_ready"], 1)
        for c in range(3):
            l = L[c]
            link(nc.scalar.activation(beta[0:l, c, :], sm[0:l, c, 0:8], ACT.Exp, scale=-1.0))
            link(nc.scalar.activation(t1[0:l, c, :], t1[0:l, c, :], ACT.Exp, scale=-1.0))
            nc.scalar.activation(t1[0:l, c, :], t1[0:l, c, :], ACT.Ln, bias=1.0).then_inc(s["g_ready"], 1)
        act.wait_ge(s["xT_evac"], 8)
        for r in range(3):
            nc.scalar.activation(XC[:, r, 0:3], ones[:, 0:3], ACT.Copy, scale=0.0)
        k.high_part(act, 2, HI)

        def decays():
            act.wait_ge(s["gsum_done"], 3)
            for c in range(3):
                l = L[c]
                p = psum[7][:, 32 * c:32 * c + 32]
                link(nc.scalar.activation(nbeg[0:l, c, :], p[0:l, 0:8], ACT.Exp))
                nc.scalar.activation(kw[0:l, c, :], p[0:l, 8:16], ACT.Exp)
                if c < 2:
                    nc.scalar.activation(egl[:, c, :], p[:, 16:24], ACT.Exp)
                else:
                    nc.scalar.activation(egl3.rearrange("p a b -> p (a b)"), psum[7][:, 96:168], ACT.Exp)
                link(nc.scalar.activation(nbeg[0:l, c, :], nbeg[0:l, c, :], ACT.Copy, scale=-1.0))
                act.drain().then_inc(s["gsum_ready"], 1)

        def silu(b):
            act.wait_ge(s["conv_ready"], b + 1)
            src = CV[:, b % 2, :]
            if b < 16:
                dst = (oaT if b < 8 else KT)[:, b % 8, :]
            else:
                if b >= 18:
                    act.wait_ge(s["vT_done"], b - 17)
                dst = VT[:, b % 2, :]
            nc.scalar.activation(dst[:, 0:TP], src[:, 0:TP], ACT.Silu)
            nc.scalar.activation(dst[:, TP:].rearrange("p (a r) -> p a r", r=TS),
                         src[:, XS:XS + 56].rearrange("p (a r) -> p a r", r=TS + 3)[:, :, 0:TS], ACT.Silu).then_inc(s["conv_silu"], 1)
        for b in range(NCB):
            if b == 3:
                decays()
            act.wait_ge(s["hist_done"], b + 1)
            act.wait_ge(unit_done, b + 1)
            if b >= 3:
                act.wait_ge(s["conv_ready"], b - 2)
                act.wait_ge(s["last_ready"], b - 2)
            x = XC[:, b % 3, :]
            xs = x[:, XS:].rearrange("p (a r) -> p a r", r=TS + 3)
            nc.scalar.activation(xs[:, :, 0:3], psum[4 + b % 2][:, 0:24].rearrange("p (a r) -> p a r", r=3), ACT.Copy)
            nc.scalar.activation(x[:, 3:XS], psum[b % 4][:, 0:TP], ACT.Copy)
            nc.scalar.activation(xs[:, :, 3:], psum[b % 4][:, TP:NT].rearrange("p (a r) -> p a r", r=TS), ACT.Copy)
            act.drain().then_inc(s["hist_ready"], 1)
            if b % 2 and b // 2 + 3 < N_QB:
                k.high_part(act, b // 2 + 3, HI)
            if b >= 2:
                silu(b - 2)
        silu(NCB - 2)
        silu(NCB - 1)
        act.preload_act_table_set(LN_EXP)
        for i, b in KEYS_FIRST:
            act.wait_ge(s["ssum_done"], i + 1)
            if i >= 2:
                act.wait_ge(s["qk_ready"], i - 1)
            link(nc.scalar.activation(RS[:, i % 2, :], psum[i % 4][:, 0:NT], ACT.Ln, bias=epsc))
            nc.scalar.activation(RS[:, i % 2, :], RS[:, i % 2, :], ACT.Exp, scale=-0.5).then_inc(s["rs_ready"], 1)
        for q in range(6):
            act.wait_ge(s["last_done"], q + 1)
            nc.scalar.activation(SCO[0:27, 512 * q:512 * q + 512], psum[4 + q % 2][0:27, :], ACT.Copy).then_inc(s["last_evac"], 1)


    @block.vector
    def _(dve):
        link = Chain(dve, s["dve_c"])
        for c in range(3):
            l = L[c]
            dve.wait_ge(s["rstd_ready"], c + 1)
            nc.vector.tensor_scalar(XN[0:l, c, :].rearrange("t (j p) -> t p j", j=KB), X[0:l, c, :].rearrange("t (p j) -> t p j", j=KB),
                                    rstd[0:l, c:c + 1], None, ALU.mult).then_inc(s["xn_ready"], 1)
        dve.wait_ge(s["par_in"], 112)
        for j in range(KB):
            dve.wait_ge(s["xT_done"], j + 1)
            link(nc.vector.tensor_scalar(hH[:, j, :], psum[j % 4][:, 0:NT], nm[:, j:j + 1], None, ALU.mult))
            nc.vector.scalar_tensor_tensor(hL[:, j, :], psum[j % 4][:, 0:NT], nm[:, j:j + 1], hH[:, j, :],
                                           ALU.mult, ALU.subtract).then_inc(s["xT_evac"], 1)
        k.low_part(dve, nc.vector, 0, HI)
        k.low_part(dve, nc.vector, 1, HI)
        dve.wait_ge(s["par_ready"], 1)
        dve.wait_ge(s["small_ready"], 3)
        for c in range(3):
            l = L[c]
            link(nc.vector.tensor_tensor(sm[0:l, c, 8:16], sm[0:l, c, 8:16], hbc[0:l, 8:16], ALU.add))
            link(nc.vector.tensor_scalar(t2[0:l, c, :], sm[0:l, c, 8:16], 0.0, None, ALU.max))
            link(nc.vector.scalar_tensor_tensor(t1[0:l, c, :], t2[0:l, c, :], 2.0, sm[0:l, c, 8:16], ALU.mult, ALU.subtract))
        dve.drain().then_inc(s["g_ready"], 1)
        dve.wait_ge(s["g_ready"], 4)
        for c in range(3):
            l = L[c]
            link(nc.vector.tensor_tensor(t2[0:l, c, :], t2[0:l, c, :], t1[0:l, c, :], ALU.add))
            link(nc.vector.scalar_tensor_tensor(gg[0:l, c, :], t2[0:l, c, :], -1.0, hbc[0:l, 0:8], ALU.mult, ALU.mult))
            link(nc.vector.tensor_scalar(beta[0:l, c, :], beta[0:l, c, :], 1.0, None, ALU.add))
            link(nc.vector.reciprocal(beta[0:l, c, :], beta[0:l, c, :]))
        dve.wait_ge(s["mask_ready"], 1)
        link(nc.vector.tensor_tensor(gm3[0:48, :, :], bc_mid(gg[0:48, 2, :], 9), bc_last(seg[0:48, :], 8), ALU.mult))
        dve.drain().then_inc(s["g_ready"], 1)
        k.low_part(dve, nc.vector, 2, HI)

        def vturn(h):
            dve.wait_ge(s["vT_done"], h + 1)
            for c in range(3):
                ins = nc.vector.tensor_copy(V[0:L[c], c, h, :], psum[6 + h % 2][0:L[c], 128 * c:128 * c + 128])
            ins.then_inc(s["vT_evac"], 1)

        for b in range(NCB):
            dve.wait_ge(s["hist_ready"], b + 1)
            if b >= 2:
                dve.wait_ge(s["conv_silu"], b - 1)
            x, o = XC[:, b % 3, :], CV[:, b % 2, 0:XW - 3]
            link(nc.vector.tensor_scalar(o, x[:, 0:XW - 3], cw[:, 0, b:b + 1], None, ALU.mult))
            for r in range(1, CW):
                ins = nc.vector.scalar_tensor_tensor(o, x[:, r:XW - 3 + r], cw[:, r, b:b + 1], o, ALU.mult, ALU.add)
                if r < 3:
                    link(ins)
            ins.then_inc(s["conv_ready"], 1)
            if b >= 19:
                vturn(b - 19)
        for h in range(NCB - 19, 8):
            vturn(h)
        dve.wait_ge(s["gsum_ready"], 3)
        for i, b in KEYS_FIRST:
            dve.wait_ge(s["rs_ready"], i + 1)
            t = (oaT if b < 8 else KT)[:, b % 8, :]
            nc.vector.scalar_tensor_tensor(t, t, 128 ** -0.5 if b < 8 else 1.0, RS[:, i % 2, :], ALU.mult, ALU.mult).then_inc(s["qk_ready"], 1)
            if b >= 8:
                continue
            h = b
            dve.wait_ge(s["kT_done"], h + 1)
            for c in range(3):
                ins = nc.vector.tensor_scalar(Kd[0:L[c], c, h, :], psum[6 + h % 2][0:L[c], 128 * c:128 * c + 128], kw[0:L[c], c, h:h + 1], None, ALU.mult)
            ins.then_inc(s["kT_evac"], 1)


    @block.tensor
    def _(pe):
        mm = nc.tensor.matmul

        def tr(out, in_, n):
            return nc.tensor.transpose(out, in_, ident[0:n, 0:n])

        pe.wait_ge(s["ident_ready"], 1)
        for j in range(KB):
            if j >= 4:
                pe.wait_ge(s["xT_evac"], j - 3)
            for c in range(3):
                if j == 0:
                    pe.wait_ge(s["xn_ready"], c + 1)
                ins = tr(psum[j % 4][:, T0[c]:T0[c] + L[c]], XN[0:L[c], c, 128 * j:128 * j + 128], L[c])
            ins.then_inc(s["xT_done"], 1)
        pe.wait_ge(s["par_in"], 112)
        tr(psum[4][:, 0:CW * NCB], CWR[0:CW * NCB, :], CW * NCB).then_inc(s["par_done"], 1)
        mm(psum[5][:, 0:16], ones[0:1, :], hrow[0:1, :], start=True, stop=True).then_inc(s["par_done"], 1)
        pe.wait_ge(s["xT_evac"], 8)
        for j in range(KB):
            for x in (hH, hL):
                ins = mm(psum[7][0:48, 200:200 + NT], wsm[:, j, :], x[:, j, :].bitcast(F32),
                         start=(j == 0 and x is hH), stop=(j == KB - 1 and x is hL))
        ins.then_inc(s["lr_done"], 1)
        pe.wait_ge(s["smT_ready"], 1)
        for c in range(3):
            tr(psum[6][0:L[c], 16 * c:16 * c + 16], smT[0:16, T0[c]:T0[c] + L[c]], 16).then_inc(s["small_done"], 1)

        def turn_v(h):
            pe.wait_ge(s["conv_silu"], 17 + h)
            if h >= 2:
                pe.wait_ge(s["vT_evac"], h - 1)
            for c in range(3):
                ins = tr(psum[6 + h % 2][0:L[c], 128 * c:128 * c + 128], VT[:, h % 2, T0[c]:T0[c] + L[c]], 128)
            ins.then_inc(s["vT_done"], 1)
        pe.wait_ge(s["sc_in"], 16)
        for b in range(NCB):
            if b >= 2:
                pe.wait_ge(s["hist_ready"], b - 1)
            if b < 2:
                pe.wait_ge(s["par_ready"], 1)
            tr(psum[4 + b % 2][:, 0:24], SC[0:24, 128 * b:128 * b + 128], 24).then_inc(s["hist_done"], 1)
            if b >= 4:
                pe.wait_ge(s["hist_ready"], b - 3)
            k.block_of_slot(pe, b // 2, b % 2, b % 4, HI)
            if b == 2:
                pe.wait_ge(s["mask_ready"], 1)
                pe.wait_ge(s["g_ready"], 5)
                pe.wait_ge(s["lr_ready"], 1)
                for c in range(3):
                    l = L[c]
                    p = psum[7][:, 32 * c:32 * c + 32]
                    mm(p[0:l, 0:8], (U if c < 2 else U3)[0:l, 0:l], gg[0:l, c, :], start=True, stop=True)
                    ins = mm(p[0:l, 8:16], (SL if c < 2 else SL3)[0:l, 0:l], gg[0:l, c, :], start=True, stop=True)
                    if c < 2:
                        ins = mm(p[:, 16:24], ones[:, :], gg[:, c, :], start=True, stop=True)
                    else:
                        ins = mm(psum[7][:, 96:168], ones[0:l, :], gm3[0:l, :, :].rearrange("p a b -> p (a b)"), start=True, stop=True)
                    ins.then_inc(s["gsum_done"], 1)
            if b >= 19:
                if b == 19:
                    pe.wait_ge(s["gsum_ready"], 3)
                turn_v(b - 19)
        for h in range(NCB - 19, 8):
            turn_v(h)
        for i, b in KEYS_FIRST:
            pe.wait_ge(s["sq_ready"], i + 1)
            if i >= 4:
                pe.wait_ge(s["rs_ready"], i - 3)
            mm(psum[i % 4][:, 0:NT], ones[:, :], SQ[:, i % 2, :], start=True, stop=True).then_inc(s["ssum_done"], 1)
            if b >= 8:
                continue
            h = b
            pe.wait_ge(s["qk_ready"], h + 1)
            pe.wait_ge(s["vT_evac"], 8)
            if h >= 2:
                pe.wait_ge(s["kT_evac"], h - 1)
            for c in range(3):
                ins = tr(psum[6 + h % 2][0:L[c], 128 * c:128 * c + 128], KT[:, h, T0[c]:T0[c] + L[c]], 128)
            ins.then_inc(s["kT_done"], 1)
        pe.wait_ge(s["last_ready"], NCB)
        for q in range(6):
            if q >= 2:
                pe.wait_ge(s["last_evac"], q - 1)
            for r in range(4):
                ins = tr(psum[4 + q % 2][0:27, 128 * r:128 * r + 128], LAST[:, 4 * q + r, :], 128)
            ins.then_inc(s["last_done"], 1)

    ctx.close()
    nc.clear_and_free_semaphores(list(s.values()))
    nc.all_engine_barrier()


def delta(k):
    nc, i_, o_ = k.nc, k.i_, k.o_
    ident, U, SL, SU, BLK, PAIR = k.ident, k.U, k.SL, k.SU, k.BLK, k.PAIR
    U3, SL3, SU3, ones, seg = k.U3, k.SL3, k.SU3, k.ones, k.seg
    oaT, bank4, beta, nbeg, gg, egl, egl3 = k.oaT, k.bank4, k.beta, k.nbeg, k.gg, k.egl, k.egl3
    KT = k.carve(0, HA * NT, HA, NT)
    Kd = k.carve(2432, 3072, 3, 8, 128)
    V = k.carve(5504, 3072, 3, 8, 128)
    MB = [A1 + 5632 * hh for hh in range(2)]
    buf = [[k.carve(MB[hh] + 512 * x, 512, 4, 128) for x in range(11)] for hh in range(2)]
    (bDT, bB, bD0, bB0, bD2, bB2, bD, bE, bY, bAT, bEG) = range(11)
    KDM = [[k.carve(MB[hh] + 512 * (2 + 3 * x), 9 * 128, 9, 128) for x in range(2)] for hh in range(2)]
    SA = k.carve(A1 + 11264, 4096, 4, 8, 128)
    free = k.ring.rearrange("p s c -> p (s c)")
    SB = k.shaped(free[:, 0:4096], (4, 8, 128))
    MT = k.shaped(free[:, 4096:4096 + 9 * L[2]], (9, L[2]))
    SEGM = k.shaped(free[:, 4096 + 9 * L[2]:4096 + 81 * L[2]], (8, 9, L[2]))
    assert 4096 + 81 * L[2] <= 4 * SW

    def sample_state(h):
        return (SA if h < 4 else SB)[:, h % 4, :, :]
    S = k.carve(A1 + 15360, 1024, 8, 128)
    s = named(nc, "delta", """xg_ready sb_ready diff_done kk_done eg_done dt_ready eg_ready b_ready at1_ready at_ready qe_ready
        dT_done d0_ready d_ready b0_ready y1_ready e_ready sq2_done d2_ready b2_ready p4_done y2_ready d4_ready
        b4_ready p8_done y3_ready d8_ready p9_done y4_ready lz_done z_ready x_ready lw_done y_ready ks_done
        mt_ready ktm_ready qm_ready otok_ready otok_done r_ready vn_done vn_ready o_done oT_ready ds_done s_ready kdm_ready kdo_ready su_done su_ready
        sa_in dve_c""")
    ctx = ExitStack()
    block = ctx.enter_context(nc.Block())

    @block.sync
    def _(sp):
        for h in range(8):
            if h == 0:
                sp.wait_ge(k.stored, STORED_FRONT)
            sp.dma_start(sample_state(h), i_["state_delta"][0, :, h].rearrange("b k v -> k b v")).then_inc(s["sa_in"], 16)
        for h in range(8):
            sp.wait_ge(s["su_ready"], h + 1)
            sp.dma_start(o_["sd_s"][0, :, h].rearrange("b k v -> k b v"), sample_state(h)).then_inc(k.stored, 16)
        sp.wait_ge(s["s_ready"], 6)
        sp.dma_start(o_["sd_p"][0, 0].rearrange("h k v -> k h v"), S[:, :, :]).then_inc(k.stored, 16)


    @block.gpsimd
    def _(pl):
        for c in range(3):
            l = L[c]
            if c == 1:
                segment_mask(nc, pl, MT, s["mt_ready"])
            if c == 2:
                for h in range(8):
                    nc.gpsimd.tensor_tensor(SEGM[:, h, :, :], bc_mid(KT[:, h, 256:NT], 9), MT[:, :, :], ALU.mult).then_inc(s["ktm_ready"], 1)
            mU, mSL, mSU = (U, SL, SU) if c < 2 else (U3, SL3, SU3)
            for hh in range(2):
                i = 2 * c + hh
                w = buf[hh]
                hs = slice(4 * hh, 4 * hh + 4)
                if c:
                    pl.wait_ge(s["s_ready"], i - 1)
                elif hh:
                    pl.wait_ge(k.stored, STORED_FRONT)
                nc.gpsimd.tensor_tensor(w[bD2][0:l, :, 0:l], bc_mid(mSL[0:l, 0:l], 4), bc_last(gg[0:l, c, hs], l), ALU.mult)
                nc.gpsimd.tensor_tensor(w[bB2][0:l, :, :], bc_mid(ones[0:l, :], 4), bc_last(gg[0:l, c, hs], 128),
                                  ALU.mult).then_inc(s["xg_ready"], 1)
                nc.gpsimd.tensor_tensor(w[bE][0:l, :, 0:l], bc_mid(mSU[0:l, 0:l], 4), bc_last(beta[0:l, c, hs], l),
                                  ALU.mult).then_inc(s["sb_ready"], 1)
            for hh in range(2):
                i = 2 * c + hh
                w = buf[hh]
                hs = slice(4 * hh, 4 * hh + 4)
                tk = slice(T0[c], T0[c] + l)
                pl.wait_ge(s["b_ready"], i + 1)
                nc.gpsimd.tensor_tensor(w[bB0][0:l, :, 0:l], w[bB][0:l, :, 0:l], bc_mid(BLK[0:l, 0:l], 4),
                                  ALU.mult).then_inc(s["b0_ready"], 1)
                pl.wait_ge(s["b0_ready"], i + 1)
                nc.gpsimd.tensor_tensor(w[bY][0:l, :, 0:l], bc_mid(ident[0:l, 0:l], 4), w[bB0][0:l, :, 0:l],
                                  ALU.subtract).then_inc(s["y1_ready"], 1)
                pl.wait_ge(s["at1_ready"], i + 1)
                nc.gpsimd.tensor_tensor(w[bAT][0:l, :, 0:l], w[bAT][0:l, :, 0:l], bc_mid(mU[0:l, 0:l], 4),
                                  ALU.mult).then_inc(s["at_ready"], 1)
                pl.wait_ge(s["eg_ready"], i + 1)
                nc.gpsimd.tensor_tensor(w[bEG][:, :, 0:l], w[bEG][:, :, 0:l], oaT[:, hs, tk], ALU.mult).then_inc(s["qe_ready"], 1)
            if c < 2:
                for r, M in enumerate(PAIR):
                    for hh in range(2):
                        w = buf[hh]
                        pl.wait_ge(s["d_ready"], 2 * c + hh + 1)
                        if r:
                            pl.wait_ge(s["lz_done"], 6 * c + 2 * (r - 1) + hh + 1)
                        nc.gpsimd.tensor_tensor(w[bE][:, :, :], w[bD][:, :, :], bc_mid(M, 4), ALU.mult).then_inc(s["e_ready"], 1)
            else:
                for h in range(8):
                    hh = h // 4
                    pl.wait_ge(s["ks_done"], 3 + hh)
                    pl.wait_ge(s["qe_ready"], 5 + hh)
                    nc.gpsimd.tensor_tensor(SEGM[:, h, :, :], bc_mid(buf[hh][bEG][:, h % 4, 0:l], 9), MT[:, :, :],
                                            ALU.mult).then_inc(s["qm_ready"], 1)
                for h in range(0, 8, 2):
                    hh = h // 4
                    pl.wait_ge(s["vn_ready"], 5 + hh)
                    if h % 4:
                        pl.wait_ge(s["su_done"], h - 1)
                    nc.gpsimd.tensor_tensor(KDM[hh][0][0:l, :, :], bc_mid(Kd[0:l, 2, h, :], 9), bc_last(seg[0:l, :], 128),
                                            ALU.mult).then_inc(s["kdm_ready"], 1)


    @block.scalar
    def _(act):
        for c in range(3):
            l = L[c]
            for hh in range(2):
                i, w, b0 = 2 * c + hh, buf[hh], 4 * hh
                act.wait_ge(s["diff_done"], i + 1)
                nc.scalar.activation(w[bDT][0:l, :, 0:l], bank4(b0, l)[0:l], ACT.Exp).then_inc(s["dt_ready"], 1)
                act.wait_ge(s["eg_done"], i + 1)
                nc.scalar.activation(w[bEG][:, :, 0:l], bank4(b0 + 3, l), ACT.Exp).then_inc(s["eg_ready"], 1)
            for hh in range(2):
                i, w, b0 = 2 * c + hh, buf[hh], 4 * hh
                act.wait_ge(s["d0_ready"], i + 1)
                nc.scalar.activation(w[bD][0:l, :, 0:l], bank4(b0, l)[0:l], ACT.Copy).then_inc(s["d_ready"], 1)
            for hh in range(2):
                i, w, b0 = 2 * c + hh, buf[hh], 4 * hh
                act.wait_ge(s["sq2_done"], i + 1)
                nc.scalar.activation(w[bD2][0:l, :, 0:l], bank4(b0 + 1, l)[0:l], ACT.Copy).then_inc(s["d2_ready"], 1)
            for hh in range(2):
                i, w, b0 = 2 * c + hh, buf[hh], 4 * hh
                act.wait_ge(s["p4_done"], i + 1)
                nc.scalar.activation(w[bD0][0:l, :, 0:l], bank4(b0, l)[0:l], ACT.Copy).then_inc(s["d4_ready"], 1)
                nc.scalar.activation(w[bB0][0:l, :, 0:l], bank4(b0 + 1, l)[0:l], ACT.Copy).then_inc(s["b4_ready"], 1)
            for hh in range(2):
                i, w, b0 = 2 * c + hh, buf[hh], 4 * hh
                act.wait_ge(s["p8_done"], i + 1)
                nc.scalar.activation(w[bD2][0:l, :, 0:l], bank4(b0 + 3, l)[0:l], ACT.Copy).then_inc(s["d8_ready"], 1)
            if c < 2:
                for k in range(3):
                    for hh in range(2):
                        w, b0 = buf[hh], 4 * hh
                        act.wait_ge(s["lz_done"], 6 * c + 2 * k + hh + 1)
                        nc.scalar.activation(w[bD0], bank4(b0 + 2, l), ACT.Copy).then_inc(s["x_ready"], 1)
            for hh in range(2):
                i, w, b0 = 2 * c + hh, buf[hh], 4 * hh
                hs = slice(4 * hh, 4 * hh + 4)
                if c < 2:
                    act.wait_ge(s["o_done"], i + 1)
                    nc.scalar.activation(oaT[:, hs, T0[c]:T0[c] + l], bank4(b0 + 2, l), ACT.Copy).then_inc(s["oT_ready"], 1)
                else:
                    def masked_keys(h):
                        act.wait_ge(s["vn_ready"], 5 + hh)
                        if h % 4 == 3:
                            act.wait_ge(s["su_done"], h - 1)
                        for q in range(9):
                            ins = nc.scalar.activation(KDM[hh][1][0:l, q, :], Kd[0:l, 2, h, :], ACT.Copy, scale=seg[0:l, q:q + 1])
                        ins.then_inc(s["kdo_ready"], 1)
                    masked_keys(4 * hh + 1)
                    act.wait_ge(s["o_done"], i + 1)
                    nc.scalar.activation(w[bB][0:l, :, :], bank4(b0 + 2, 128)[0:l], ACT.Copy).then_inc(s["otok_ready"], 1)
                    act.wait_ge(s["otok_done"], hh + 1)
                    nc.scalar.activation(oaT[:, hs, T0[c]:T0[c] + l], bank4(b0 + 2, l), ACT.Copy).then_inc(s["oT_ready"], 1)
                    masked_keys(4 * hh + 3)


    @block.vector
    def _(dve):
        link = Chain(dve, s["dve_c"])
        for c in range(3):
            l = L[c]
            for hh in range(2):
                i, w, b0 = 2 * c + hh, buf[hh], 4 * hh

                def m(x):
                    return w[x][0:l, :, 0:l]
                dve.wait_ge(s["kk_done"], i + 1)
                dve.wait_ge(s["dt_ready"], i + 1)
                link(nc.vector.tensor_tensor(m(bB), bank4(b0 + 1, l)[0:l], m(bDT), ALU.mult))
                dve.wait_ge(s["sb_ready"], i + 1)
                nc.vector.tensor_tensor(m(bB), m(bB), m(bE), ALU.mult).then_inc(s["b_ready"], 1)
                nc.vector.tensor_tensor(m(bAT), bank4(b0 + 2, l)[0:l], m(bDT), ALU.mult).then_inc(s["at1_ready"], 1)
            for hh in range(2):
                i, w, b0 = 2 * c + hh, buf[hh], 4 * hh
                dve.wait_ge(s["dT_done"], i + 1)
                nc.vector.tensor_tensor(w[bD0][0:l, :, 0:l], bank4(b0, l)[0:l], bc_mid(BLK[0:l, 0:l], 4), ALU.mult).then_inc(s["d0_ready"], 1)
            for hh in range(2):
                i, w, b0 = 2 * c + hh, buf[hh], 4 * hh
                dve.wait_ge(s["sq2_done"], i + 1)
                nc.vector.tensor_copy(w[bB2][0:l, :, 0:l], bank4(b0 + 2, l)[0:l]).then_inc(s["b2_ready"], 1)
            for done, ready, bk in ((s["p4_done"], s["y2_ready"], 3), (s["p8_done"], s["y3_ready"], 2), (s["p9_done"], s["y4_ready"], 0)):
                for hh in range(2):
                    i, w, b0 = 2 * c + hh, buf[hh], 4 * hh
                    dve.wait_ge(done, i + 1)
                    nc.vector.tensor_tensor(w[bY][0:l, :, 0:l], w[bY][0:l, :, 0:l], bank4(b0 + bk, l)[0:l], ALU.add).then_inc(ready, 1)
            if c < 2:
                for k in range(3):
                    for hh in range(2):
                        w, b0 = buf[hh], 4 * hh
                        n = 6 * c + 2 * k + hh + 1
                        dve.wait_ge(s["lz_done"], n)
                        nc.vector.tensor_copy(w[bB2], bank4(b0 + 1, l)).then_inc(s["z_ready"], 1)
                    for hh in range(2):
                        w, b0 = buf[hh], 4 * hh
                        n = 6 * c + 2 * k + hh + 1
                        dve.wait_ge(s["lw_done"], n)
                        nc.vector.tensor_tensor(w[bY], w[bY], bank4(b0 + 3, l), ALU.subtract).then_inc(s["y_ready"], 1)
            def residual(hh):
                w, hs = buf[hh], slice(4 * hh, 4 * hh + 4)
                dve.wait_ge(s["ks_done"], 2 * (c - 1) + hh + 1)
                r = w[bE][0:l, :, :]
                link(nc.vector.tensor_tensor(r, bank4(4 * hh, 128)[0:l], bc_last(nbeg[0:l, c, hs], 128), ALU.mult))
                nc.vector.tensor_tensor(r, r, V[0:l, c, hs, :], ALU.add).then_inc(s["r_ready"], 1)

            def new_values(hh):
                w, hs = buf[hh], slice(4 * hh, 4 * hh + 4)
                dve.wait_ge(s["vn_done"], 2 * c + hh + 1)
                nc.vector.tensor_tensor(w[bDT][0:l, :, :], bank4(4 * hh + 1, 128)[0:l], bc_last(beta[0:l, c, hs], 128), ALU.mult).then_inc(s["vn_ready"], 1)

            def prompt_state(hh):
                hs = slice(4 * hh, 4 * hh + 4)
                dve.wait_ge(s["ds_done"], 2 * c + hh + 1)
                if c == 0:
                    nc.vector.tensor_copy(S[:, hs, :], bank4(4 * hh + 3, 128)).then_inc(s["s_ready"], 1)
                else:
                    e = egl[:, 1, hs] if c == 1 else egl3[:, 0, hs]
                    link(nc.vector.tensor_tensor(S[:, hs, :], S[:, hs, :], bc_last(e, 128), ALU.mult))
                    nc.vector.tensor_tensor(S[:, hs, :], S[:, hs, :], bank4(4 * hh + 3, 128), ALU.add).then_inc(s["s_ready"], 1)
            if c < 2:
                for hh in range(2):
                    if c:
                        residual(hh)
                    new_values(hh)
                    prompt_state(hh)
            else:
                residual(0)
                residual(1)
                new_values(0)
                new_values(1)
                for hh in range(2):
                    for h in range(4 * hh, 4 * hh + 4):
                        dve.wait_ge(s["su_done"], h + 1)
                        for q in range(8):
                            st = sample_state(h)[:, q, :]
                            ins = nc.vector.scalar_tensor_tensor(st, st, egl3[:, 1 + q, h:h + 1], bank4(4 * (h % 2) + q // 4, 128)[:, q % 4, :],
                                                                 ALU.mult, ALU.add)
                        ins.then_inc(s["su_ready"], 1)
                    prompt_state(hh)


    @block.tensor
    def _(pe):
        mm = nc.tensor.matmul

        def tr(out, in_, n):
            return nc.tensor.transpose(out, in_, ident[0:n, 0:n])

        for c in range(3):
            l = L[c]
            tk = slice(T0[c], T0[c] + l)
            mU = U if c < 2 else U3

            def four(b, lhs, rhs, hh, start=True):
                for h in range(4):
                    ins = mm(bank4(b, l)[0:l, h, :], lhs[0:l, h, 0:l], rhs[0:l, h, 0:l], start=True, stop=True)
                return ins
            for hh in range(2):
                i, w, b0 = 2 * c + hh, buf[hh], 4 * hh
                if c:
                    pe.wait_ge(s["s_ready"], i - 1)
                    pe.wait_ge(s["oT_ready"], i - 1)
                for h in range(4):
                    ins = mm(bank4(b0 + 1, l)[0:l, h, :], KT[:, 4 * hh + h, tk], KT[:, 4 * hh + h, tk], start=True, stop=True)
                for h in range(4):
                    ins = mm(bank4(b0 + 2, l)[0:l, h, :], KT[:, 4 * hh + h, tk], oaT[:, 4 * hh + h, tk], start=True, stop=True)
                ins.then_inc(s["kk_done"], 1)
                pe.wait_ge(s["xg_ready"], i + 1)
                for h in range(4):
                    ins = mm(bank4(b0, l)[0:l, h, :], w[bD2][0:l, h, 0:l], mU[0:l, 0:l], start=True, stop=True)
                ins.then_inc(s["diff_done"], 1)
                for h in range(4):
                    ins = mm(bank4(b0 + 3, l)[:, h, :], w[bB2][0:l, h, :], mU[0:l, 0:l], start=True, stop=True)
                ins.then_inc(s["eg_done"], 1)
            for hh in range(2):
                i, w, b0 = 2 * c + hh, buf[hh], 4 * hh
                pe.wait_ge(s["b_ready"], i + 1)
                for h in range(4):
                    ins = tr(bank4(b0, l)[0:l, h, :], w[bB][0:l, h, 0:l], l)
                ins.then_inc(s["dT_done"], 1)
            for hh in range(2):
                i, w, b0 = 2 * c + hh, buf[hh], 4 * hh
                pe.wait_ge(s["d0_ready"], i + 1)
                pe.wait_ge(s["b0_ready"], i + 1)
                pe.wait_ge(s["at1_ready"], i + 1)
                four(b0 + 1, w[bB0], w[bD0], hh)
                four(b0 + 2, w[bD0], w[bB0], hh).then_inc(s["sq2_done"], 1)
            for hh in range(2):
                i, w, b0 = 2 * c + hh, buf[hh], 4 * hh
                pe.wait_ge(s["d2_ready"], i + 1)
                pe.wait_ge(s["b2_ready"], i + 1)
                pe.wait_ge(s["y1_ready"], i + 1)
                pe.wait_ge(s["eg_ready"], i + 1)
                pe.wait_ge(s["d_ready"], i + 1)
                four(b0 + 3, w[bD2], w[bY], hh)
                four(b0, w[bB2], w[bD2], hh)
                four(b0 + 1, w[bD2], w[bB2], hh).then_inc(s["p4_done"], 1)
            for hh in range(2):
                i, w, b0 = 2 * c + hh, buf[hh], 4 * hh
                pe.wait_ge(s["d4_ready"], i + 1)
                pe.wait_ge(s["y2_ready"], i + 1)
                four(b0 + 2, w[bD0], w[bY], hh)
                pe.wait_ge(s["b4_ready"], i + 1)
                four(b0 + 3, w[bB0], w[bD0], hh).then_inc(s["p8_done"], 1)
            for hh in range(2):
                i, w, b0 = 2 * c + hh, buf[hh], 4 * hh
                pe.wait_ge(s["d8_ready"], i + 1)
                pe.wait_ge(s["y3_ready"], i + 1)
                four(b0, w[bD2], w[bY], hh).then_inc(s["p9_done"], 1)
            if c < 2:
                for k in range(3):
                    for hh in range(2):
                        w, b0 = buf[hh], 4 * hh
                        n = 6 * c + 2 * k + hh + 1
                        if k == 0:
                            pe.wait_ge(s["y4_ready"], 2 * c + hh + 1)
                        else:
                            pe.wait_ge(s["y_ready"], n - 2)
                        pe.wait_ge(s["e_ready"], n)
                        four(b0 + 1, w[bE], w[bY], hh)
                        for h in range(4):
                            ins = tr(bank4(b0 + 2, l)[:, h, :], w[bY][:, h, :], l)
                        ins.then_inc(s["lz_done"], 1)
                    for hh in range(2):
                        w, b0 = buf[hh], 4 * hh
                        n = 6 * c + 2 * k + hh + 1
                        pe.wait_ge(s["z_ready"], n)
                        pe.wait_ge(s["x_ready"], n)
                        four(b0 + 3, w[bD0], w[bB2], hh).then_inc(s["lw_done"], 1)
            def values(hh):
                i, w, b0 = 2 * c + hh, buf[hh], 4 * hh
                if c:
                    pe.wait_ge(s["r_ready"], i - 1)
                for h in range(4):
                    rhs = w[bE][0:l, h, :] if c else V[0:l, 0, 4 * hh + h, :]
                    ins = mm(bank4(b0 + 1, 128)[0:l, h, :], w[bY][0:l, h, 0:l], rhs, start=True, stop=True)
                ins.then_inc(s["vn_done"], 1)

            if c < 2:
                for hh in range(2):
                    i, w, b0 = 2 * c + hh, buf[hh], 4 * hh
                    pe.wait_ge(s["y_ready"], 6 * c + 4 + hh + 1)
                    if c == 1:
                        for h in range(4):
                            ins = mm(bank4(b0, 128)[:, h, :], KT[:, 4 * hh + h, tk], S[:, 4 * hh + h, :], start=True, stop=True)
                        ins.then_inc(s["ks_done"], 1)
                    values(hh)
                    pe.wait_ge(s["vn_ready"], i + 1)
                    pe.wait_ge(s["at_ready"], i + 1)
                    pe.wait_ge(s["qe_ready"], i + 1)
                    o = bank4(b0 + 2, l)
                    for h in range(4):
                        if c == 1:
                            mm(o[:, h, :], S[:, 4 * hh + h, :], w[bEG][:, h, 0:l], start=True, stop=False)
                        ins = mm(o[:, h, :], w[bDT][0:l, h, :], w[bAT][0:l, h, 0:l], start=(c == 0), stop=True)
                    ins.then_inc(s["o_done"], 1)
                    for h in range(4):
                        ins = mm(bank4(b0 + 3, 128)[:, h, :], Kd[0:l, c, 4 * hh + h, :], w[bDT][0:l, h, :], start=True, stop=True)
                    ins.then_inc(s["ds_done"], 1)
            else:
                def old_states(b, hh, stop):
                    for h in range(4):
                        for q in range(9):
                            st = S[:, 4 * hh + h, :] if q == 0 else sample_state(4 * hh + h)[:, q - 1, :]
                            ins = mm(bank4(b, 128)[0:l, h, :], SEGM[:, 4 * hh + h, q, :], st, start=(q == 0), stop=(stop and q == 8))
                        if not stop:
                            ins = mm(bank4(b, 128)[0:l, h, :], buf[hh][bAT][0:l, h, 0:l], buf[hh][bDT][0:l, h, :], start=False, stop=True)
                    return ins
                pe.wait_ge(s["ktm_ready"], 8)
                for hh in range(2):
                    pe.wait_ge(s["y4_ready"], 5 + hh)
                    if hh == 0:
                        pe.wait_ge(s["sa_in"], 16 * 8)
                    old_states(4 * hh, hh, True).then_inc(s["ks_done"], 1)
                values(0)
                values(1)
                for hh in range(2):
                    i, w, b0 = 2 * c + hh, buf[hh], 4 * hh
                    pe.wait_ge(s["vn_ready"], i + 1)
                    pe.wait_ge(s["at_ready"], i + 1)
                    pe.wait_ge(s["qm_ready"], 4 * hh + 4)
                    old_states(b0 + 2, hh, False).then_inc(s["o_done"], 1)
                    for h in range(4):
                        hd = 4 * hh + h
                        if h % 2:
                            pe.wait_ge(s["kdo_ready"], hd // 2 + 1)
                        else:
                            pe.wait_ge(s["kdm_ready"], hd // 2 + 1)
                        keys = KDM[hh][h % 2]
                        ins = mm(bank4(b0 + 3, 128)[:, h, :], keys[0:l, 0, :], w[bDT][0:l, h, :], start=True, stop=True)
                        if h == 3:
                            ins.then_inc(s["ds_done"], 1)
                        if hd >= 2:
                            pe.wait_ge(s["su_ready"], hd - 1)
                        else:
                            pe.wait_ge(s["vn_ready"], 6)
                        for q in range(8):
                            ins = mm(bank4(4 * (hd % 2) + q // 4, 128)[:, q % 4, :], keys[0:l, 1 + q, :], w[bDT][0:l, h, :], start=True, stop=True)
                        ins.then_inc(s["su_done"], 1)
                        if h == 1:
                            pe.wait_ge(s["otok_ready"], hh + 1)
                            for g in range(4):
                                ins = tr(bank4(b0 + 2, l)[:, g, :], w[bB][0:l, g, :], l)
                            ins.then_inc(s["otok_done"], 1)

    ctx.close()
    nc.clear_and_free_semaphores(list(s.values()))
    nc.all_engine_barrier()


def gla(k):
    nc, i_, o_ = k.nc, k.i_, k.o_
    ident, SL, SL3, U3, R03, GR, GM, ones, seg = k.ident, k.SL, k.SL3, k.U3, k.R03, k.GR, k.GM, k.ones, k.seg
    hH, hL, psum, bank4, unit_done, lrT = k.hH, k.hL, k.psum, k.bank4, k.unit_done, k.lrT
    QK = k.carve(0, 8 * NT, 8, NT)
    V = k.carve(2432, 3072, 3, D)
    Kd = k.carve(5504, 1536, 3, 512)
    LG = k.carve(7040, 1536, 3, 512)
    EX = [k.carve(at, 768, 6, 128) for at in (8576, 8576 + 768, 22400)]
    QP = [k.carve(at, 640, 5, 128) for at in (10112, 10112 + 640, 21632)]
    KP = [k.carve(11392 + 512 * p, 512, 4, 128) for p in range(2)]
    AM = [k.carve(12416 + 512 * p, 512, 4, 128) for p in range(2)]
    AT = [k.carve(13440 + 128 * p, 128) for p in range(2)]
    S = k.carve(13696, 1024, HB, 256)
    SS = [k.carve(14720 + 2048 * p, 2048, 8, 256) for p in range(2)]
    KM = [k.carve(18816 + 1152 * p, 1152, 9, 128) for p in range(2)]
    UP = k.carve(21120, 512)
    GB = k.carve(21632, 512)
    TL = [k.carve(22144 + 512 * p, 512) for p in range(2)]
    s = named(nc, "gla", """up_in qk_ready v_ready lg_done soft_ready lg_ready kb_done kd_done kdec_ready kd_ready
        ex_done ex_ready q_ready kp_ready pair_done at_ready o_done oT_ready ds_done s_ready
        mt_ready qs_ready otok_ready otok_done ss_in0 ss_in1 ss_out km_ready su_done su_ready act_c dve_c""")
    ctx = ExitStack()
    block = ctx.enter_context(nc.Block())
    ss_in = (s["ss_in0"], s["ss_in1"])
    HI = [k.carve_r(8576 + SW * p, SW) for p in range(3)]
    l3 = L[2]
    MT = k.carve(23168, 9 * l3, 9, l3)
    QS = [k.carve(23600 + 9 * l3 * p, 9 * l3, 9, l3) for p in range(2)]
    OT = [k.carve(21120 + 256 * p, 256) for p in range(2)]
    SC3 = 3 * HB

    @block.sync
    def _(sp):
        sp.wait_ge(k.stored, STORED_DELTA)
        for n in range(N_VB, N_Z):
            k.load_w(sp, n)
        sp.dma_start(UP[32:48, :], i_["gla_gate_up"][0]).then_inc(s["up_in"], 16)
        sp.dma_start(GB[32:33, :], i_["gla_gate_bias"]).then_inc(s["up_in"], 16)
        for h in range(2):
            sp.dma_start(SS[h][:, :, :], i_["state_gla"][0, :, h].rearrange("b k v -> k b v")).then_inc(ss_in[h], 16)
        for n in range(N_Z, N_Z + 8):
            k.load_w(sp, n)
        for h in range(HB):
            sp.wait_ge(s["su_ready"], 8 * h + 8)
            sp.dma_start(o_["sg_s"][0, :, h].rearrange("b k v -> k b v"), SS[h % 2][:, :, :]).then_inc(s["ss_out"] if h < 2 else k.stored, 16)
            if h < 2:
                sp.wait_ge(s["ss_out"], 16 * (h + 1))
                sp.dma_start(SS[h][:, :, :], i_["state_gla"][0, :, h + 2].rearrange("b k v -> k b v")).then_inc(ss_in[h], 16)
        sp.wait_ge(s["s_ready"], SC3)
        sp.dma_start(o_["sg_p"][0, 0].rearrange("h k v -> k h v"), S[:, :, :]).then_inc(k.stored, 16)

    @block.gpsimd
    def _(pl):
        pl.wait_ge(k.stored, STORED_DELTA)
        segment_mask(nc, pl, MT, s["mt_ready"])
        for c in range(3):
            l = L[c]
            for h in range(HB):
                i = HB * c + h
                p = i % 2
                pl.wait_ge(s["ex_ready"], i + 1)
                if i >= 2:
                    pl.wait_ge(s["pair_done"], i - 1)
                kk = QK[:, 4 + h, T0[c]:T0[c] + l]
                if c < 2:
                    nc.gpsimd.tensor_tensor(KP[p][:, :, :], bc_mid(kk, 4), EX[i % 3][:, 2:6, :], ALU.mult).then_inc(s["kp_ready"], 1)
                else:
                    nc.gpsimd.tensor_tensor(KP[p][:, 3, 0:l], kk, EX[i % 3][:, 5, 0:l], ALU.mult).then_inc(s["kp_ready"], 1)
                    pl.wait_ge(s["q_ready"], i + 1)
                    if h >= 2:
                        pl.wait_ge(s["o_done"], i - 1)
                    nc.gpsimd.tensor_tensor(QS[p][:, :, :], bc_mid(QP[i % 3][:, 0, 0:l], 9), MT[:, :, :], ALU.mult).then_inc(s["qs_ready"], 1)
                    pl.wait_ge(s["kd_ready"], 3)
                    if h >= 2:
                        pl.wait_ge(s["su_done"], 4 * (h - 1))
                    nc.gpsimd.tensor_tensor(KM[p][0:l, :, :], bc_mid(Kd[0:l, 2, 128 * h:128 * h + 128], 9), bc_last(seg[0:l, :], 128),
                                            ALU.mult).then_inc(s["km_ready"], 1)

    def out(act, i):
        c, h = divmod(i, HB)
        if c < 2:
            act.wait_ge(s["o_done"], i + 1)
        else:
            act.wait_ge(s["otok_done"], h + 1)
        nc.scalar.activation(QK[:, h::4, T0[c]:T0[c] + L[c]], bank4(4 * (i % 2) + 3)[:, 0:2, 0:L[c]], ACT.Copy).then_inc(s["oT_ready"], 1)

    @block.scalar
    def _(act):
        link = Chain(act, s["act_c"])
        base = units(N_QB)
        for n in range(N_QB, N_QB + 3):
            k.high_part(act, n, HI)
        for b in range(8):
            act.wait_ge(unit_done, base + b + 1)
            nc.scalar.activation(QK[:, b, :], psum[b % 4][:, 0:NT], ACT.Copy, scale=128 ** -0.5 if b < 4 else 1.0).then_inc(s["qk_ready"], 1)
            if b % 2:
                k.high_part(act, N_QB + b // 2 + 3, HI)
        act.preload_act_table_set(LN_EXP)
        for c in range(3):
            l = L[c]
            act.wait_ge(s["lg_done"], c + 1)
            t = TL[c % 2][0:l, :]
            if c == 2:
                act.wait_ge(s["lg_ready"], 1)
            link(nc.scalar.activation(t, psum[4 + c][0:l, :], ACT.Abs))
            link(nc.scalar.activation(t, t, ACT.Exp, scale=-1.0))
            nc.scalar.activation(t, t, ACT.Ln, bias=1.0).then_inc(s["soft_ready"], 1)
        for u in range(12):
            q, c = divmod(u, 3)
            act.wait_ge(unit_done, base + 8 + u + 1)
            nc.scalar.activation(V[0:L[c], c, 256 * q:256 * q + 256], psum[u % 4][0:L[c], 0:256], ACT.Copy).then_inc(s["v_ready"], 1)
            if u == 2:
                k.high_part(act, N_Z - 1, HI)
        for c in range(3):
            l = L[c]
            act.wait_ge(s["kd_done"], c + 1)
            if c == 2:
                act.wait_ge(s["kd_ready"], 1)
            nc.scalar.activation(TL[c % 2][0:l, :], psum[4 + c % 2][0:l, :], ACT.Exp, scale=1 / TAU).then_inc(s["kdec_ready"], 1)

        def by_token(i):
            act.wait_ge(s["o_done"], i + 1)
            nc.scalar.activation(OT[i % 2][0:l3, :], psum[4 * (i % 2) + 3][0:l3, 0:256], ACT.Copy).then_inc(s["otok_ready"], 1)
        for c in range(3):
            l = L[c]
            for h in range(HB):
                i = HB * c + h
                p = i % 2
                act.wait_ge(s["ex_done"], i + 1)
                if i == 2:
                    act.wait_ge(s["kd_ready"], 3)
                if i >= 3:
                    act.wait_ge(s["q_ready"], i - 2)
                    act.wait_ge(s["kp_ready"], i - 2)
                    act.wait_ge(s["s_ready"], i - 2)
                if c == 2 and h >= 3:
                    act.wait_ge(s["su_ready"], 8 * (h - 2))
                a, b = bank4(4 * p), bank4(4 * p + 1)
                if c < 2:
                    nc.scalar.activation(EX[i % 3][:, 0:4, :], a, ACT.Exp, scale=1 / TAU)
                    nc.scalar.activation(EX[i % 3][:, 4, :], b[:, 0, :], ACT.Exp, scale=1 / TAU)
                    nc.scalar.activation(EX[i % 3][:, 5, :], a[:, 1, :], ACT.Exp, scale=-1 / TAU).then_inc(s["ex_ready"], 1)
                else:
                    nc.scalar.activation(EX[i % 3][:, 0:2, 0:l], a[:, 0:2, 0:l], ACT.Exp, scale=1 / TAU)
                    nc.scalar.activation(EX[i % 3][:, 5, 0:l], a[:, 1, 0:l], ACT.Exp, scale=-1 / TAU).then_inc(s["ex_ready"], 1)
                if i >= 2:
                    out(act, i - 2)
                if i > 2 * HB:
                    by_token(i - 1)
        out(act, SC3 - 2)
        by_token(SC3 - 1)
        out(act, SC3 - 1)

    @block.vector
    def _(dve):
        link = Chain(dve, s["dve_c"])
        for n in range(N_QB, N_Z - 1):
            k.low_part(dve, nc.vector, n, HI)
        for c in range(3):
            l = L[c]
            dve.wait_ge(s["soft_ready"], c + 1)
            nc.vector.scalar_tensor_tensor(LG[0:l, c, :], psum[4 + c][0:l, :], 0.0, TL[c % 2][0:l, :], ALU.min, ALU.subtract).then_inc(s["lg_ready"], 1)
        k.low_part(dve, nc.vector, N_Z - 1, HI)
        for c in range(3):
            l = L[c]
            dve.wait_ge(s["kb_done"], c + 1)
            dve.wait_ge(s["kdec_ready"], c + 1)
            nc.vector.tensor_tensor(Kd[0:l, c, :], psum[6 + c % 2][0:l, :], TL[c % 2][0:l, :], ALU.mult).then_inc(s["kd_ready"], 1)

        def state(i):
            c, h = divmod(i, HB)
            p = i % 2
            e = EX[i % 3][:, 0, (TAIL if c == 2 else 128) - 1:][:, 0:1]
            dve.wait_ge(s["ds_done"], i + 1)
            d = psum[4 * p + 2][:, 0:256]
            if c == 0:
                nc.vector.tensor_copy(S[:, h, :], d).then_inc(s["s_ready"], 1)
            else:
                nc.vector.scalar_tensor_tensor(S[:, h, :], S[:, h, :], e, d, ALU.mult, ALU.add).then_inc(s["s_ready"], 1)
            if c == 2:
                for b in range(8):
                    dve.wait_ge(s["su_done"], 4 * h + b // 2 + 1)
                    x = TAIL + TS * b + TS - 1
                    nc.vector.scalar_tensor_tensor(SS[h % 2][:, b, :], SS[h % 2][:, b, :], EX[i % 3][:, 0, x:x + 1],
                                                   psum[4 * p + b // 2 % 2][:, 256 * (b % 2):256 * (b % 2) + 256], ALU.mult, ALU.add).then_inc(s["su_ready"], 1)

        def queries(i):
            c, h = divmod(i, HB)
            l, p = L[c], i % 2
            q = QK[:, h, T0[c]:T0[c] + l]
            dve.wait_ge(s["ex_ready"], i + 1)
            if i >= 3:
                dve.wait_ge(s["o_done"], i - 2)
            if c < 2:
                nc.vector.tensor_tensor(QP[i % 3][:, :, :], bc_mid(q, 5), EX[i % 3][:, 0:5, :], ALU.mult).then_inc(s["q_ready"], 1)
            else:
                nc.vector.tensor_tensor(QP[i % 3][:, 0:2, 0:l], bc_mid(q, 2), EX[i % 3][:, 0:2, 0:l], ALU.mult).then_inc(s["q_ready"], 1)

        def pairs(i):
            c, h = divmod(i, HB)
            l, p = L[c], i % 2
            dve.wait_ge(s["pair_done"], i + 1)
            if i >= 2:
                dve.wait_ge(s["o_done"], i - 1)
            if c < 2:
                link(nc.vector.tensor_tensor(AM[p][:, :, :], bank4(4 * p + 2), GM[:, :, :], ALU.mult))
                nc.vector.tensor_reduce(AT[p][:, :], AM[p][:, :, :].rearrange("p a t -> p t a"), AX.X, ALU.add).then_inc(s["at_ready"], 1)
            else:
                nc.vector.tensor_tensor(AT[p][0:l, 0:l], bank4(4 * p + 2)[0:l, 0, 0:l], U3[0:l, 0:l], ALU.mult).then_inc(s["at_ready"], 1)
        queries(0)
        for i in range(SC3):
            pairs(i)
            if i + 1 < SC3:
                queries(i + 1)
            if i:
                state(i - 1)
        state(SC3 - 1)

    @block.tensor
    def _(pe):
        mm = nc.tensor.matmul
        for b in range(8):
            if b >= 4:
                pe.wait_ge(s["qk_ready"], b - 3)
            k.block_of_slot(pe, N_QB + b // 2, b % 2, b % 4, HI)
        pe.wait_ge(s["up_in"], 32)
        for c in range(3):
            l = L[c]
            mm(psum[4 + c][0:l, :], lrT[:, T0[c]:T0[c] + l], UP[32:48, :], start=True, stop=False)
            mm(psum[4 + c][0:l, :], ones[32:33, 0:l], GB[32:33, :], start=False, stop=True).then_inc(s["lg_done"], 1)
        for u in range(12):
            q, c = divmod(u, 3)
            n = N_VB + q
            if u < 4:
                pe.wait_ge(s["qk_ready"], 5 + u)
            else:
                pe.wait_ge(s["v_ready"], u - 3)
            pe.wait_ge(k.w_lo, n + 1)
            hi, lo = (w.rearrange("p (j c) -> p j c", j=KB) for w in (HI[n % 3], k.LOW[:, n % SLOTS, :]))
            for j in range(KB):
                x, y = (h[:, j, T0[c]:T0[c] + L[c]] for h in (hH, hL))
                mm(psum[u % 4][0:L[c], 0:256], x, hi[:, j, :], start=(j == 0), stop=False)
                mm(psum[u % 4][0:L[c], 0:256], x, lo[:, j, :], start=False, stop=False)
                ins = mm(psum[u % 4][0:L[c], 0:256], y, hi[:, j, :], start=False, stop=(j == KB - 1))
            ins.then_inc(unit_done, 1)
        pe.wait_ge(s["lg_ready"], 3)
        for c in range(3):
            l = L[c]
            if c == 2:
                pe.wait_ge(s["kd_ready"], 1)
            for h in range(HB):
                ins = nc.tensor.transpose(bank4(6 + c % 2)[0:l, h, :], QK[:, 4 + h, T0[c]:T0[c] + l], ident)
            ins.then_inc(s["kb_done"], 1)
            mm(psum[4 + c % 2][0:l, :], (SL if c < 2 else SL3)[0:l, 0:l], LG[0:l, c, :], start=True, stop=True).then_inc(s["kd_done"], 1)

        def exps(i):
            c, h = divmod(i, HB)
            l, p = L[c], i % 2
            lg = LG[0:l, c, 128 * h:128 * h + 128]
            if c < 2:
                mm(psum[4 * p][:, :], lg, GR[:, 0:4, :], start=True, stop=True)
                mm(bank4(4 * p + 1)[:, 0, :], lg, GR[:, 4, :], start=True, stop=True).then_inc(s["ex_done"], 1)
            else:
                mm(bank4(4 * p)[:, 0, 0:l], lg, U3[0:l, 0:l], start=True, stop=True)
                mm(bank4(4 * p)[:, 1, 0:l], lg, R03[0:l, 0:l], start=True, stop=True).then_inc(s["ex_done"], 1)

        pe.wait_ge(s["v_ready"], 12)
        pe.wait_ge(s["kd_ready"], 3)
        pe.wait_ge(s["kdec_ready"], 3)
        def pairs(i):
            c, h = divmod(i, HB)
            l, p = L[c], i % 2
            pe.wait_ge(s["q_ready"], i + 1)
            pe.wait_ge(s["kp_ready"], i + 1)
            if i >= 2:
                pe.wait_ge(s["s_ready"], i - 1)
            if c < 2:
                for r, (kx, qx) in enumerate(((3, 1), (0, 2), (1, 3), (2, 4))):
                    ins = mm(bank4(4 * p + 2)[:, r, :], KP[p][:, kx, :], QP[i % 3][:, qx, :], start=True, stop=True)
            else:
                ins = mm(bank4(4 * p + 2)[0:l, 0, 0:l], KP[p][:, 3, 0:l], QP[i % 3][:, 1, 0:l], start=True, stop=True)
            ins.then_inc(s["pair_done"], 1)

        exps(0)
        exps(1)
        pairs(0)
        for i in range(SC3):
            c, h = divmod(i, HB)
            l, p = L[c], i % 2
            if i + 1 < SC3:
                pairs(i + 1)
            if i + 2 < SC3:
                if c == 2 and h >= 2:
                    pe.wait_ge(s["su_ready"], 8 * (h - 1))
                exps(i + 2)
            if i >= 2:
                pe.wait_ge(s["oT_ready"], i - 1)
            o = bank4(4 * p + 3)
            if c == 2:
                pe.wait_ge(ss_in[h % 2], 16 * (h // 2 + 1))
                pe.wait_ge(s["qs_ready"], h + 1)
                o2 = psum[4 * p + 3][0:l, 0:256]
                for b in range(9):
                    mm(o2, QS[p][:, b, :], S[:, h, :] if b == 0 else SS[h % 2][:, b - 1, :], start=(b == 0), stop=False)
            pe.wait_ge(s["at_ready"], i + 1)
            if c == 2:
                ins = mm(o2, AT[p][0:l, 0:l], V[0:l, c, 256 * h:256 * h + 256], start=False, stop=True)
            for e in range(2 if c < 2 else 0):
                if c == 1:
                    pe.wait_ge(s["s_ready"], i - 3)
                    mm(o[:, e, 0:l], S[:, h, 128 * e:128 * e + 128], QP[i % 3][:, 0, 0:l], start=True, stop=False)
                ins = mm(o[:, e, 0:l], V[0:l, c, 256 * h + 128 * e:256 * h + 128 * e + 128], AT[p][0:l, 0:l],
                         start=(c == 0), stop=True)
            ins.then_inc(s["o_done"], 1)
            if c == 2:
                pe.wait_ge(s["km_ready"], h + 1)
            mm(psum[4 * p + 2][:, 0:256], KM[p][0:l, 0, :] if c == 2 else Kd[0:l, c, 128 * h:128 * h + 128],
               V[0:l, c, 256 * h:256 * h + 256], start=True, stop=True).then_inc(s["ds_done"], 1)
            if c == 2:
                pe.wait_ge(s["ex_ready"], min(i + 3, SC3))
                if h >= 2:
                    pe.wait_ge(s["su_ready"], 8 * (h - 1))
                for b in range(8):
                    if b >= 4 and b % 2 == 0:
                        pe.wait_ge(s["su_ready"], 8 * h + b - 2)
                    ins = mm(psum[4 * p + b // 2 % 2][:, 256 * (b % 2):256 * (b % 2) + 256], KM[p][0:l, 1 + b, :],
                             V[0:l, 2, 256 * h:256 * h + 256], start=True, stop=True)
                    if b % 2:
                        ins.then_inc(s["su_done"], 1)
                pe.wait_ge(s["otok_ready"], h + 1)
                for e in range(2):
                    ins = nc.tensor.transpose(o[:, e, 0:l], OT[p][0:l, 128 * e:128 * e + 128], ident[0:l, 0:l])
                ins.then_inc(s["otok_done"], 1)
    ctx.close()


X_AT = 17696


def merge(k):
    nc, i_, o_ = k.nc, k.i_, k.o_
    oaT, ones, psum, unit_done, epsc, na, nb = k.oaT, k.ones, k.psum, k.unit_done, k.epsc, k.na, k.nb
    obT = k.carve(0, 8 * NT, 8, NT)
    WN = k.carve(3072, D)
    WR = k.carve(4096, 288, KB, 36)
    GA = k.carve(8576, 8 * NT, 8, NT)
    GB = k.carve(11008, 8 * NT, 8, NT)
    MG = k.carve(13440, 8 * NT, 8, NT)
    ZT = k.carve(15872, 2 * NT, 2, NT)
    RS = k.carve(15872 + 2 * NT, 2 * NT, 2, NT)
    assert 15872 + 4 * NT <= X_AT
    HI = [k.carve_r(at, SW) for at in (4384, 4384 + SW, 21984)]
    OAH = [k.carve_r(at, NT) for at in (*(X_AT + 3072 + NT * j for j in range(4)), *(15872 + 2 * NT + NT * j for j in range(4)))]
    OAL = k.rounded("oaT", 0, HA * NT, HA, NT)
    OBH, MGH = k.hH, k.hL
    OBL, MGL = k.carve_r(0, 8 * NT, 8, NT), k.carve_r(13440, 8 * NT, 8, NT)
    X = k.carve(X_AT, 3072, 3, D)
    SQ = [k.carve(X_AT + 3072 + 2 * NT * p, 2 * NT, 2, NT) for p in range(2)]
    s = named(nc, "merge", """x_in par_in sq_ready sum_done rs_ready on_ready silu_ready gated gate_ready ya_ready yb_ready mg_ready
        oah_ready oal_ready obh_ready obl_ready mgh_ready mgl_ready
        x1_ready act_c""")
    ctx = ExitStack()
    block = ctx.enter_context(nc.Block())
    base = units(N_Z)

    def ob(v, j):
        return v[:, j // 2 + 4 * (j % 2), :]

    @block.sync
    def _(sp):
        sp.wait_ge(k.stored, STORED_GLA)
        k.load_x(sp, X, s["x_in"])
        sp.dma_start(WN, i_["norm_final"].partition_broadcast(128)).then_inc(s["par_in"], 16)
        sp.dma_start(WR[:, :, 0:4], i_["router_group_w"][0].rearrange("(p j) g -> p j g", j=KB)).then_inc(s["par_in"], 16)
        sp.dma_start(WR[:, :, 4:36], i_["router_expert_w"][0].rearrange("(p j) e -> p j e", j=KB)).then_inc(s["par_in"], 16)
        for n in range(N_Z + 8, N_PRE):
            k.load_w(sp, n)
        sp.wait_ge(s["par_in"], 48)

    @block.gpsimd
    def _(pl):
        for h in range(12):
            if h >= 2:
                pl.wait_ge(s["sum_done"], h - 1)
            if h < 8:
                nc.gpsimd.tensor_tensor(SQ[h % 2][:, 0, :], oaT[:, h, :], oaT[:, h, :], ALU.mult).then_inc(s["sq_ready"], 1)
            else:
                v = obT[:, h - 8::4, :]
                nc.gpsimd.tensor_tensor(SQ[h % 2][:, :, :], v, v, ALU.mult).then_inc(s["sq_ready"], 1)
        for j in range(8):
            pl.wait_ge(s["oah_ready"], j + 1)
            nc.gpsimd.tensor_tensor(OAL[:, j, :], oaT[:, j, :], OAH[j], ALU.subtract).then_inc(s["oal_ready"], 1)
        for n in range(N_PA, N_PRE):
            k.low_part(pl, nc.gpsimd, n, HI)

    @block.scalar
    def _(act):
        link = Chain(act, s["act_c"])
        act.preload_act_table_set(LN_EXP)
        for n in range(N_Z, N_Z + 3):
            k.high_part(act, n, HI)
        act.wait_ge(k.stored, STORED_GLA)
        for h in range(12):
            act.wait_ge(s["sum_done"], h + 1)
            if h >= 2:
                act.wait_ge(s["on_ready"], h - 1 if h - 1 <= 8 else 8 + 2 * (h - 9))
            link(nc.scalar.activation(RS[:, h % 2, :], psum[4 + h % 4][:, 0:NT], ACT.Ln, scale=1 / 128 if h < 8 else 1 / 256, bias=epsc))
            nc.scalar.activation(RS[:, h % 2, :], RS[:, h % 2, :], ACT.Exp, scale=-0.5).then_inc(s["rs_ready"], 1)
        for u in range(16):
            act.wait_ge(unit_done, base + u + 1)
            if u >= 2:
                act.wait_ge(s["gated"], u - 1)
            nc.scalar.activation(ZT[:, u % 2, :], psum[u % 4][:, 0:NT], ACT.Silu).then_inc(s["silu_ready"], 1)
            if u % 2:
                k.high_part(act, N_Z + u // 2 + 3, HI)
            if 1 <= u <= 8:
                act.wait_ge(s["gated"], u)
                nc.scalar.activation(OAH[u - 1], oaT[:, u - 1, :], ACT.Copy).then_inc(s["oah_ready"], 1)
        for u in range(16, 32):
            act.wait_ge(unit_done, base + u + 1)
            nc.scalar.activation((GA if u < 24 else GB)[:, u % 8, :], psum[u % 4][:, 0:NT], ACT.Sigmoid).then_inc(s["gate_ready"], 1)
            if u % 2:
                k.high_part(act, N_Z + u // 2 + 3, HI)
        act.wait_ge(s["gated"], 16)
        for j in range(8):
            nc.scalar.activation(OBH[:, j, :], ob(obT, j), ACT.Copy).then_inc(s["obh_ready"], 1)
        for n in range(N_PA + 3, N_PA + 7):
            k.high_part(act, n, HI)
        for b in range(8):
            act.wait_ge(s["mg_ready"], b + 1)
            nc.scalar.activation(MGH[:, b, :], MG[:, b, :], ACT.Copy).then_inc(s["mgh_ready"], 1)
            if b % 2:
                k.high_part(act, N_PA + 7 + b // 2, HI)
        k.high_part(act, N_PRE - 1, HI)

    @block.vector
    def _(dve):
        for n in range(N_Z, N_Z + 3):
            k.low_part(dve, nc.vector, n, HI)
        for h in range(12):
            dve.wait_ge(s["rs_ready"], h + 1)
            if h < 8:
                nc.vector.scalar_tensor_tensor(oaT[:, h, :], oaT[:, h, :], na, RS[:, h % 2, :], ALU.mult, ALU.mult).then_inc(s["on_ready"], 1)
            else:
                for e in range(2):
                    v = obT[:, h - 8 + 4 * e, :]
                    nc.vector.scalar_tensor_tensor(v, v, nb[:, e:e + 1], RS[:, h % 2, :], ALU.mult, ALU.mult).then_inc(s["on_ready"], 1)
        dve.wait_ge(s["on_ready"], 16)
        for u in range(16):
            dve.wait_ge(s["silu_ready"], u + 1)
            v = oaT[:, u, :] if u < 8 else ob(obT, u - 8)
            nc.vector.tensor_tensor(v, v, ZT[:, u % 2, :], ALU.mult).then_inc(s["gated"], 1)
            if u % 2:
                k.low_part(dve, nc.vector, N_Z + u // 2 + 3, HI)
        for n in range(N_Z + 11, N_PA):
            k.low_part(dve, nc.vector, n, HI)
        for b in range(8):
            dve.wait_ge(unit_done, base + 32 + b + 1)
            dve.wait_ge(s["gate_ready"], b + 1)
            nc.vector.tensor_tensor(MG[:, b, :], psum[b % 4][:, 0:NT], GA[:, b, :], ALU.mult).then_inc(s["ya_ready"], 1)
            dve.wait_ge(s["obh_ready"], b + 1)
            nc.vector.tensor_tensor(ob(OBL, b), ob(obT, b), OBH[:, b, :], ALU.subtract).then_inc(s["obl_ready"], 1)

        def merged_low(b):
            dve.wait_ge(s["mgh_ready"], b + 1)
            nc.vector.tensor_tensor(MGL[:, b, :], MG[:, b, :], MGH[:, b, :], ALU.subtract).then_inc(s["mgl_ready"], 1)
        for b in range(8):
            dve.wait_ge(unit_done, base + 40 + b + 1)
            dve.wait_ge(s["gate_ready"], 8 + b + 1)
            dve.wait_ge(s["ya_ready"], b + 1)
            nc.vector.tensor_tensor(GB[:, b, :], psum[b % 4][:, 0:NT], GB[:, b, :], ALU.mult).then_inc(s["yb_ready"], 1)
            dve.wait_ge(s["yb_ready"], b + 1)
            nc.vector.tensor_tensor(MG[:, b, :], MG[:, b, :], GB[:, b, :], ALU.add).then_inc(s["mg_ready"], 1)
            if b:
                merged_low(b - 1)
        merged_low(7)
        dve.wait_ge(s["x_in"], 80)
        for u in range(12):
            q, c = divmod(u, 3)
            dve.wait_ge(unit_done, base + 48 + u + 1)
            x = X[0:L[c], c, 256 * q:256 * q + 256]
            nc.vector.tensor_tensor(x, x, psum[4 + u % 4][0:L[c], 0:256], ALU.add).then_inc(s["x1_ready"], 1)

    @block.tensor
    def _(pe):
        mm = nc.tensor.matmul
        for h in range(12):
            pe.wait_ge(s["sq_ready"], h + 1)
            if h >= 4:
                pe.wait_ge(s["rs_ready"], h - 3)
            if h < 8:
                ins = mm(psum[4 + h % 4][:, 0:NT], ones[:, :], SQ[h % 2][:, 0, :], start=True, stop=True)
            else:
                mm(psum[4 + h % 4][:, 0:NT], ones[:, :], SQ[h % 2][:, 0, :], start=True, stop=False)
                ins = mm(psum[4 + h % 4][:, 0:NT], ones[:, :], SQ[h % 2][:, 1, :], start=False, stop=True)
            ins.then_inc(s["sum_done"], 1)
            if h in (3, 5, 7, 9):
                u = (h - 3) // 2
                k.block_of_slot(pe, N_Z + u // 2, u % 2, u, HI)
        for u in range(4, 48):
            if u - 4 < 16:
                pe.wait_ge(s["silu_ready"], u - 3)
            elif u - 4 < 32:
                pe.wait_ge(s["gate_ready"], u - 19)
            elif u - 4 < 40:
                pe.wait_ge(s["ya_ready"], u - 35)
            else:
                pe.wait_ge(s["yb_ready"], u - 43)
            xh = xl = None
            if 32 <= u < 40:
                xh, xl = lambda j: OAH[j], lambda j: OAL[:, j, :]
            elif u >= 40:
                xh, xl = lambda j: OBH[:, j, :], lambda j: ob(OBL, j)
            if u == 32:
                pe.wait_ge(s["oal_ready"], 8)
            if u == 40:
                pe.wait_ge(s["obl_ready"], 8)
            k.block_of_slot(pe, N_Z + u // 2, u % 2, u % 4, HI, xh, xl)
        for u in range(12):
            q, c = divmod(u, 3)
            n = N_WO + q
            pe.wait_ge(k.w_lo, n + 1)
            hi, lo = (w.rearrange("p (j c) -> p j c", j=KB) for w in (HI[n % 3], k.LOW[:, n % SLOTS, :]))
            if u >= 4:
                pe.wait_ge(s["x1_ready"], u - 3)
            tk = slice(T0[c], T0[c] + L[c])
            o = psum[4 + u % 4][0:L[c], 0:256]
            for j in range(KB):
                if u == 0:
                    pe.wait_ge(s["mgl_ready"], j + 1)
                mm(o, MGH[:, j, tk], hi[:, j, :], start=(j == 0), stop=False)
                mm(o, MGH[:, j, tk], lo[:, j, :], start=False, stop=False)
                ins = mm(o, MGL[:, j, tk], hi[:, j, :], start=False, stop=(j == KB - 1))
            ins.then_inc(unit_done, 1)
    ctx.close()


def experts(k):
    nc, i_, o_ = k.nc, k.i_, k.o_
    ident, SU, ones, hT, psum, bank4, epsc, nf, rbias = k.ident, k.SU, k.ones, k.hT, k.psum, k.bank4, k.epsc, k.nf, k.rbias
    X = k.carve(X_AT, 3072, 3, D)
    XN = k.carve(0, 3072, 3, D)
    WN = k.carve(3072, D)
    WR = k.carve(4096, 288, KB, 36)
    XGH = k.carve_r(4384, 1024, KB, 128)
    XGL = k.hL.rearrange("p a b -> p (a b)")[:, 0:1024].rearrange("p (j t) -> p j t", j=KB)
    P = k.carve_r(5408, 384, 3, 128)
    PT = k.carve_r(5792, NT)
    SIL = [k.carve(6096 + 256 * p, 256) for p in range(2)]
    H = [k.carve(6608 + 256 * p, 256) for p in range(2)]
    HXH = [k.carve_r(7120 + 256 * p, 256, 2, 128) for p in range(2)]
    HXL = [k.carve_r(16896 + 256 * p, 256, 2, 128) for p in range(2)]
    OGH = k.carve_r(7632, 1024)
    OGL = k.rounded("masks", 8 * 128, 1024)
    WF = k.carve(7632, 1024)
    HIGU = [k.carve_r(9728, 4096, KB, 512), k.carve_r(20768, 4096, KB, 512)]
    HIDN = [k.carve_r(13824, 2048, 2, 1024), k.rounded("oaT", 0, 2048, 2, 1024)]
    XNH = [k.rounded("hT", 0, 1024), k.rounded("hT", 1024, 1024), k.carve_r(15872, 1024)]
    XNL = k.carve_r(0, 3072, 3, D)
    LOW = k.LOW
    IO = k.carve(8656, 128)
    LT = k.carve(8784, 108, 3, 36)
    TE = k.carve(8892, 96)
    WT = k.carve(8988, 1)
    DESC = k.carve(8989, 8)
    at = [9000]

    def take(n, *dims):
        at[0] += n
        return k.carve(at[0] - n, n, *dims)
    gmax, gkey, gsum, pg, a1, a2, b1, b2, w1, w2, key, ss, rstd, tcount, tmax = (take(3) for _ in range(15))
    eq4, ky4, oh4, ex4 = (take(12, 3, 4) for _ in range(4))
    le, eq8, ky8, oh1, oh2, comb = (take(24, 3, 8) for _ in range(6))
    CMB = take(8)
    IOI = k.carve(9600, 128).bitcast(I32)
    TE4 = TE.rearrange("p (c g e) -> p c g e", g=4, e=8)
    s = named(nc, "experts", """io_ready rstd_ready xn_ready xT_done xT_ready rt_done d4_ready ex4_ready d2_ready w2_ready oh_ready
        rank_done comb_ready cnt_ready p_ready pt_done pt_ready xg_done xgh_ready xgl_ready cmb_ready gu_done sil_ready
        h_ready hx_done hxh_ready hxl_ready wf_in xnh_ready xnl_ready hi_gu lo_gu hi_dn lo_dn lo_dn2
        dn_done ogh_ready og_ready sc_done y_added x2_ready r3_ready key_back fin_ready out_done act_c dve_c pool_c""")
    ctx = ExitStack()
    block = ctx.enter_context(nc.Block())
    PASSES = 3
    assert PASSES * CAP >= NT

    def place(kind, e):
        g, e = divmod(e, EPG)
        if kind < 2:
            m = kind if e == 0 else 3 * e - 1 + kind
        else:
            m = 3 * e + 4 if e < EPG - 1 else PER_GROUP - 1
        return m + PER_GROUP * g
    ORDER = sorted(((place(kind, e), kind, e) for kind in range(3) for e in range(EPG)))

    def expert_load(sp, v, g, p, m):
        _, kind, e = ORDER[m]
        before = m - SLOTS
        if before >= 0:
            _, kb, eb = ORDER[before]
            sp.wait_ge(s["dn_done"] if kb == 2 else s["gu_done"], v * EPG + (eb + 1))
        elif isinstance(v, int) and v == 0:
            sp.wait_ge(k.unit_done, units(N_PRE + before + 1))
        else:
            _, kb, eb = ORDER[before + PER_GROUP]
            sp.wait_ge(s["dn_done"] if kb == 2 else s["gu_done"], (v - 1) * EPG + (eb + 1))
        w = i_[("expert_w_gate", "expert_w_up", "expert_w_down")[kind]][0][g * EPG + e]
        sp.dma_start(k.ring[:, m % SLOTS, :], w.rearrange("(p j) c -> p (j c)", p=128)).then_inc(k.ring_in[m % SLOTS], 16)

    def slot(m):
        return LOW[:, m % SLOTS, :].rearrange("p (j c) -> p j c", j=KB)

    def slot_wait(eng, v, m):
        eng.wait_ge(k.ring_in[m % SLOTS], v * 48 + 16 * (N_PRE // SLOTS + 1 + m // SLOTS))

    def groups(eng, p, body):
        with eng.Fori(0, NG - 1) as g:
            body(g + NG * p, True)
        body(NG * p + NG - 1, False)

    def before(p):
        return (0, 0) if p == 0 else (NG * p - 1, EPG)

    def passes(eng, body):
        body(0)
        eng.wait_ge(s["cnt_ready"], 1)
        count = eng.value_load(k.cnti[0:1, 0:1], min_val=0, max_val=NT)
        for p in range(1, PASSES):
            with eng.If(count > CAP * p):
                body(p)

    @block.sync
    def _(sp):
        sp.dma_start(WF, i_["norm_ffn"][0].partition_broadcast(128)).then_inc(s["wf_in"], 16)

        def one_pass(p):
            for m in range(SLOTS):
                expert_load(sp, NG * p, 0, p, m)
            with sp.Fori(0, NG - 1) as g:
                v = g + NG * p
                for m in range(SLOTS, PER_GROUP):
                    expert_load(sp, v, g, p, m)
                for m in range(SLOTS):
                    expert_load(sp, v + 1, g + 1, p, m)
            for m in range(SLOTS, PER_GROUP):
                expert_load(sp, NG * p + NG - 1, NG - 1, p, m)
        passes(sp, one_pass)
        sp.wait_ge(s["wf_in"], 16)
        yp, ys = o_["y_p"][0], o_["y_s"].rearrange("b t d -> (b t) d")
        for c in range(3):
            sp.wait_ge(s["fin_ready"], c + 1)
            if c == 0:
                sp.dma_start(yp[0:112, :], X[META:128, 0, :]).then_inc(s["out_done"], 16)
            elif c == 1:
                sp.dma_start(yp[112:240, :], X[:, 1, :]).then_inc(s["out_done"], 16)
            else:
                sp.dma_start(yp[240:256, :], X[0:TAIL, 2, :]).then_inc(s["out_done"], 16)
                sp.dma_start(ys, X[TAIL:L[2], 2, :]).then_inc(s["out_done"], 16)
        sp.wait_ge(s["out_done"], 64)

    @block.gpsimd
    def _(pl):
        link = Chain(pl, s["pool_c"])
        link(nc.gpsimd.iota(IOI, [[1, 128]], base=0, channel_multiplier=0))
        for e in range(8):
            nc.gpsimd.memset(DESC[:, e:e + 1], float(8 - e))
        nc.gpsimd.memset(LT[:, :, :], 0.0)
        link(nc.gpsimd.tensor_copy(IO, IOI))
        pl.drain().then_inc(s["io_ready"], 1)
        for c in range(3):
            pl.wait_ge(s["xnh_ready"], c + 1)
            nc.gpsimd.tensor_tensor(XNL[0:L[c], c, :], XN[0:L[c], c, :], XNH[c][0:L[c], :], ALU.subtract).then_inc(s["xnl_ready"], 1)

        def low_down(v, e):
            m = place(2, e)
            pl.wait_ge(s["hi_dn"], v * EPG + (e + 1))
            nc.gpsimd.tensor_tensor(LOW[:, m % SLOTS, 0:1024], k.ring[:, m % SLOTS, 0:1024],
                                    HIDN[e % 2][:, 0, :], ALU.subtract).then_inc(s["lo_dn"], 1)

        def one_pass(p):
            low_down(*before(p))

            def one_group(v, more):
                for e in range(1, EPG + more):
                    low_down(v, e)
            groups(pl, p, one_group)
        passes(pl, one_pass)

    @block.scalar
    def _(act):
        link = Chain(act, s["act_c"])

        def inverse_rms(signal):
            for c in range(3):
                l = L[c]
                link(nc.scalar.activation(XN[0:l, c, :], X[0:l, c, :], ACT.Square, accum_out=ss[0:l, c:c + 1]))
                link(nc.scalar.activation(ss[0:l, c:c + 1], ss[0:l, c:c + 1], ACT.Ln, scale=1 / D, bias=epsc[0:l, :]))
                nc.scalar.activation(rstd[0:l, c:c + 1], ss[0:l, c:c + 1], ACT.Exp, scale=-0.5).then_inc(signal, 1)
        act.preload_act_table_set(LN_EXP)
        inverse_rms(s["rstd_ready"])
        def high_gate_up(v, e):
            for half in range(2):
                m = place(half, e)
                slot_wait(act, v, m)
                nc.scalar.activation(HIGU[e % 2][:, :, 256 * half:256 * half + 256], k.slot8(m), ACT.Copy).then_inc(s["hi_gu"], 1)

        high_gate_up(0, 0)
        act.wait_ge(s["rt_done"], 3)
        for c in range(3):
            nc.scalar.activation(XNH[c][0:L[c], :], XN[0:L[c], c, :], ACT.Copy).then_inc(s["xnh_ready"], 1)

        act.wait_ge(s["d4_ready"], 1)
        nc.scalar.activation(ex4[:, :, :], ex4[:, :, :], ACT.Exp).then_inc(s["ex4_ready"], 1)
        act.wait_ge(s["d2_ready"], 1)
        nc.scalar.activation(w2[:, :], w2[:, :], ACT.Exp).then_inc(s["w2_ready"], 1)

        def high_down(v, e):
            m = place(2, e)
            slot_wait(act, v, m)
            nc.scalar.activation(HIDN[e % 2].rearrange("p j c -> p (j c)"), k.ring[:, m % SLOTS, :], ACT.Copy).then_inc(s["hi_dn"], 1)

        def tokens(v, last):
            for q in range(2):
                act.wait_ge(s["xg_done"], v * 3 + (q + 1))
                nc.scalar.activation(XGH[:, 4 * q:4 * q + 4, :], bank4(6 + q), ACT.Copy).then_inc(s["xgh_ready"], 1)
            act.wait_ge(s["xg_done"], v * 3 + 3)
            if not (isinstance(v, int) and v == 0):
                act.wait_ge(s["h_ready"], last)
            nc.scalar.activation(CMB[:, :], psum[2][:, 400:408], ACT.Copy).then_inc(s["cmb_ready"], 1)

        def turned_places(v):
            act.wait_ge(s["pt_done"], v + 1)
            nc.scalar.activation(PT[:, :], psum[3][:, 0:NT], ACT.Copy).then_inc(s["pt_ready"], 1)

        def high_hidden(v, e):
            act.wait_ge(s["hx_done"], v * EPG + (e + 1))
            if e >= 2:
                act.wait_ge(s["dn_done"], v * EPG + (e - 1))
            nc.scalar.activation(HXH[e % 2][:, :, :], psum[2 + e % 2][:, 0:256].rearrange("p (j t) -> p j t", j=2),
                                 ACT.Copy).then_inc(s["hxh_ready"], 1)

        def one_pass(p):
            v0, e0 = before(p)
            if p:
                high_gate_up(v0, e0)
            high_down(v0, e0)
            high_gate_up(v0, e0 + 1)
            tokens(NG * p, EPG * NG * p)

            def one_group(v, more):
                for e in range(EPG):
                    if e >= 1:
                        high_hidden(v, e - 1)
                    act.wait_ge(s["gu_done"], v * EPG + (e + 1))
                    nc.scalar.activation(SIL[e % 2][:, :], psum[e % 2][:, 0:256], ACT.Silu).then_inc(s["sil_ready"], 1)
                    if more or e + 2 < EPG:
                        high_gate_up(v, e + 2)
                    if more or e + 1 < EPG:
                        if e:
                            act.wait_ge(s["dn_done"], v * EPG + e)
                        high_down(v, e + 1)
                    if e == 0:
                        turned_places(v)
                high_hidden(v, EPG - 1)
                if more:
                    tokens(v + 1, v * EPG + EPG)
                act.wait_ge(s["dn_done"], v * EPG + EPG)
                for half in range(2):
                    nc.scalar.activation(OGH[:, 512 * half:512 * half + 512], psum[4 + half][:, :], ACT.Copy).then_inc(s["ogh_ready"], 1)
            groups(act, p, one_group)
        passes(act, one_pass)
        act.preload_act_table_set(LN_EXP)
        act.wait_ge(s["x2_ready"], 1)
        inverse_rms(s["r3_ready"])

    @block.vector
    def _(dve):
        V = nc.vector
        link = Chain(dve, s["dve_c"])
        for c in range(3):
            l = L[c]
            dve.wait_ge(s["rstd_ready"], c + 1)
            if c == 0:
                dve.wait_ge(s["wf_in"], 16)
            V.scalar_tensor_tensor(XN[0:l, c, :].rearrange("t (j p) -> t p j", j=KB), X[0:l, c, :].rearrange("t (p j) -> t p j", j=KB),
                                   rstd[0:l, c:c + 1], WF[0:l, :].rearrange("t (p j) -> t p j", j=KB), ALU.mult, ALU.mult).then_inc(s["xn_ready"], 1)
        for j in range(KB):
            dve.wait_ge(s["xT_done"], j + 1)
            V.tensor_copy(hT[:, j, :], psum[j % 4][:, 0:NT]).then_inc(s["xT_ready"], 1)
        def places(v):
            for c in range(3):
                ins = V.tensor_scalar(P[0:L[c], c, :], IO[0:L[c], :], key[0:L[c], c:c + 1], None, ALU.is_equal)
            ins.then_inc(s["p_ready"], 1)
            dve.wait_ge(s["p_ready"], v + 1)
            for c in range(3):
                V.tensor_scalar(key[0:L[c], c:c + 1], key[0:L[c], c:c + 1], -1024.0, None, ALU.add)

        def low_gate_up(v, e):
            for half in range(2):
                m = place(half, e)
                dve.wait_ge(s["hi_gu"], v * 2 * EPG + (2 * e + half + 1))
                V.tensor_tensor(slot(m), k.slot8(m), HIGU[e % 2][:, :, 256 * half:256 * half + 256], ALU.subtract).then_inc(s["lo_gu"], 1)

        low_gate_up(0, 0)
        dve.wait_ge(s["io_ready"], 1)
        for c in range(3):
            dve.wait_ge(s["rt_done"], c + 1)
            link(V.tensor_copy(LT[0:L[c], c, :], psum[4 + c][0:L[c], 0:36]))

        def first_of_max(v, n, out_max, eq, ky, oh, top):
            link(V.tensor_reduce(out_max, v, AX.X, ALU.max))
            link(V.tensor_tensor(eq, v, bc_last(out_max, n), ALU.is_equal))
            link(V.tensor_tensor(ky, eq, bc_mid(DESC[:, 8 - n:8], 3), ALU.mult))
            link(V.tensor_reduce(top, ky, AX.X, ALU.max))
            link(V.tensor_tensor(oh, ky, bc_last(top, n), ALU.is_equal))
        lg = LT[:, :, 0:4]
        first_of_max(lg, 4, gmax, eq4, ky4, oh4, gkey)
        dve.drain().then_inc(s["oh_ready"], 1)
        V.tensor_tensor(ex4, lg, bc_last(gmax, 4), ALU.subtract).then_inc(s["d4_ready"], 1)
        link(V.tensor_tensor(TE4, LT[:, :, 4:36].rearrange("p c (g e) -> p c g e", g=4), bc_last(oh4, 8), ALU.mult))
        link(V.tensor_reduce(le, TE4.rearrange("p c g e -> p c e g"), AX.X, ALU.add))
        dve.wait_ge(s["rank_done"], 4)
        link(V.tensor_scalar(tmax, gkey, -1024.0, 4096.0, ALU.mult, ALU.add))
        for c in range(3):
            l = L[c]
            link(V.tensor_tensor(ky4[0:l, c, :], psum[4 + c][0:l, 0:4], oh4[0:l, c, :], ALU.mult))
            link(V.tensor_reduce(key[0:l, c:c + 1], ky4[0:l, c, :], AX.X, ALU.add))
            link(V.tensor_tensor(key[0:l, c:c + 1], key[0:l, c:c + 1], tmax[0:l, c:c + 1], ALU.add))
        link(V.tensor_reduce(tcount[:, 0:1], psum[7][:, 0:4], AX.X, ALU.max))
        V.tensor_copy(k.cnti[:, :], tcount[:, 0:1]).then_inc(s["cnt_ready"], 1)
        places(0)
        first_of_max(le, 8, a1, eq8, ky8, oh1, b1)
        link(V.scalar_tensor_tensor(le, oh1, -1e30, le, ALU.mult, ALU.add))
        first_of_max(le, 8, a2, eq8, ky8, oh2, b2)
        V.tensor_tensor(w2, a2, a1, ALU.subtract).then_inc(s["d2_ready"], 1)
        dve.wait_ge(s["ex4_ready"], 1)
        link(V.tensor_reduce(gsum, ex4, AX.X, ALU.add))
        link(V.reciprocal(pg, gsum))
        dve.wait_ge(s["w2_ready"], 1)
        link(V.tensor_scalar(w1, w2, 1.0, None, ALU.add))
        link(V.reciprocal(w1, w1))
        link(V.tensor_tensor(w1, w1, pg, ALU.mult))
        link(V.tensor_tensor(w2, w2, w1, ALU.mult))
        link(V.tensor_tensor(comb, oh1, bc_last(w1, 8), ALU.mult))
        link(V.tensor_tensor(oh2, oh2, bc_last(w2, 8), ALU.mult))
        V.tensor_tensor(comb, comb, oh2, ALU.add).then_inc(s["comb_ready"], 1)
        def low_down(v, e):
            m = place(2, e)
            dve.wait_ge(s["hi_dn"], v * EPG + (e + 1))
            V.tensor_tensor(LOW[:, m % SLOTS, 1024:2048], k.ring[:, m % SLOTS, 1024:2048], HIDN[e % 2][:, 1, :],
                            ALU.subtract).then_inc(s["lo_dn2"], 1)

        def tokens(v):
            for q in range(2):
                dve.wait_ge(s["xgh_ready"], v * 2 + (q + 1))
                V.tensor_tensor(XGL[:, 4 * q:4 * q + 4, :], bank4(6 + q), XGH[:, 4 * q:4 * q + 4, :], ALU.subtract).then_inc(s["xgl_ready"], 1)

        def low_hidden(v, e):
            dve.wait_ge(s["hxh_ready"], v * EPG + (e + 1))
            V.tensor_tensor(HXL[e % 2][:, :, :], psum[2 + e % 2][:, 0:256].rearrange("p (j t) -> p j t", j=2),
                            HXH[e % 2][:, :, :], ALU.subtract).then_inc(s["hxl_ready"], 1)

        def one_pass(p):
            if p:
                dve.wait_ge(s["key_back"], p)
                dve.wait_ge(s["pt_done"], NG * p)
                places(NG * p)
            v0, e0 = before(p)
            if p:
                low_gate_up(v0, e0)
            tokens(NG * p)
            low_down(v0, e0)
            low_gate_up(v0, e0 + 1)

            def one_group(v, more):
                dve.wait_ge(s["cmb_ready"], v + 1)
                for e in range(EPG):
                    if e >= 1:
                        low_hidden(v, e - 1)
                    dve.wait_ge(s["sil_ready"], v * EPG + (e + 1))
                    if e >= 2:
                        dve.wait_ge(s["hx_done"], v * EPG + (e - 1))
                    V.scalar_tensor_tensor(H[e % 2].rearrange("t (j p) -> t p j", j=2), SIL[e % 2].rearrange("t (p j) -> t p j", j=2),
                                           CMB[:, e:e + 1], psum[e % 2][:, 256:512].rearrange("t (p j) -> t p j", j=2), ALU.mult, ALU.mult).then_inc(s["h_ready"], 1)
                    if more or e + 2 < EPG:
                        low_gate_up(v, e + 2)
                    if more or e + 1 < EPG:
                        low_down(v, e + 1)
                    if more and e == 1:
                        dve.wait_ge(s["pt_done"], v + 1)
                        places(v + 1)
                low_hidden(v, EPG - 1)
                if more:
                    tokens(v + 1)
                for half in range(2):
                    dve.wait_ge(s["ogh_ready"], v * 2 + (half + 1))
                    o = slice(512 * half, 512 * half + 512)
                    V.tensor_tensor(OGL[:, o], psum[4 + half][:, :], OGH[:, o], ALU.subtract).then_inc(s["og_ready"], 1)
                for q in range(6):
                    c, half = divmod(q, 2)
                    dve.wait_ge(s["sc_done"], v * 6 + (q + 1))
                    x = X[0:L[c], c, 512 * half:512 * half + 512]
                    V.tensor_tensor(x, x, psum[6 + q % 2][0:L[c], :], ALU.add).then_inc(s["y_added"], 1)
                dve.wait_ge(s["y_added"], v * 6 + 6)
            groups(dve, p, one_group)
            if p + 1 < PASSES:
                for c in range(3):
                    ins = V.tensor_scalar(key[0:L[c], c:c + 1], key[0:L[c], c:c + 1], 1024.0 * NG - CAP, None, ALU.add)
                ins.then_inc(s["key_back"], 1)
        passes(dve, one_pass)
        dve.drain().then_inc(s["x2_ready"], 1)
        for c in range(3):
            l = L[c]
            dve.wait_ge(s["r3_ready"], c + 1)
            V.scalar_tensor_tensor(X[0:l, c, :], X[0:l, c, :], rstd[0:l, c:c + 1], WN[0:l, :], ALU.mult, ALU.mult).then_inc(s["fin_ready"], 1)

    @block.tensor
    def _(pe):
        mm, tr = nc.tensor.matmul, nc.tensor.transpose
        for j in range(KB):
            if j >= 4:
                pe.wait_ge(s["xT_ready"], j - 3)
            for c in range(3):
                if j == 0:
                    pe.wait_ge(s["xn_ready"], c + 1)
                ins = tr(psum[j % 4][:, T0[c]:T0[c] + L[c]], XN[0:L[c], c, 128 * j:128 * j + 128], ident[0:L[c], 0:L[c]])
            ins.then_inc(s["xT_done"], 1)
        pe.wait_ge(s["xT_ready"], KB)
        for c in range(3):
            l = L[c]
            for j in range(KB):
                mm(psum[4 + c][0:l, 0:36], hT[:, j, T0[c]:T0[c] + l], WR[:, j, :], start=(j == 0), stop=False)
            mm(psum[4 + c][0:l, 0:36], ones[0:1, 0:l], rbias[0:1, :], start=False, stop=True).then_inc(s["rt_done"], 1)
        pe.wait_ge(s["oh_ready"], 1)
        for c in range(3):
            l = L[c]
            ins = mm(psum[4 + c][0:l, 0:4], SU[0:l, 0:l], oh4[0:l, c, :], start=True, stop=(c == 0))
            for b in range(c):
                ins = mm(psum[4 + c][0:l, 0:4], ones[:, 0:l], oh4[:, b, :], start=False, stop=(b == c - 1))
            ins.then_inc(s["rank_done"], 1)
        for c in range(3):
            ins = mm(psum[7][:, 0:4], ones[0:L[c], :], oh4[0:L[c], c, :], start=(c == 0), stop=(c == 2))
        ins.then_inc(s["rank_done"], 1)
        pe.wait_ge(s["cnt_ready"], 1)

        pe.wait_ge(s["xnl_ready"], 3)

        def gather(v, blocks):
            if 0 in blocks:
                pe.wait_ge(s["p_ready"], v + 1)
            for b in blocks:
                q, j = divmod(b, 4)
                for c in range(3):
                    l, ch = L[c], slice(128 * b, 128 * b + 128)
                    mm(bank4(6 + q)[:, j, :], XNH[c][0:l, ch], P[0:l, c, :], start=(c == 0), stop=False)
                    ins = mm(bank4(6 + q)[:, j, :], XNL[0:l, c, ch], P[0:l, c, :], start=False, stop=(c == 2))
                if j == 3:
                    ins.then_inc(s["xg_done"], 1)

        def gather_weights(v):
            pe.wait_ge(s["comb_ready"], 1)
            for c in range(3):
                ins = mm(psum[2][:, 400:408], P[0:L[c], c, :].bitcast(F32), comb[0:L[c], c, :], start=(c == 0), stop=(c == 2))
            ins.then_inc(s["xg_done"], 1)

        def turn_places(v):
            for c in range(3):
                ins = tr(psum[3][:, T0[c]:T0[c] + L[c]], P[0:L[c], c, :].bitcast(F32), ident[0:L[c], 0:L[c]])
            ins.then_inc(s["pt_done"], 1)

        def gate_up(v, e, part):
            if part == 0:
                pe.wait_ge(s["lo_gu"], v * 2 * EPG + (2 * e + 2))
                if e >= 2 and e < EPG:
                    pe.wait_ge(s["h_ready"], v * EPG + (e - 1))
            b = psum[e % 2]
            for j in range(4 * part, 4 * part + 4):
                mm(b[:, :], XGH[:, j, :], HIGU[e % 2][:, j, :], start=(j == 0), stop=False)
                for half in range(2):
                    mm(b[:, 256 * half:256 * half + 256], XGH[:, j, :], slot(place(half, e))[:, j, :], start=False, stop=False)
                ins = mm(b[:, :], XGL[:, j, :], HIGU[e % 2][:, j, :], start=False, stop=(j == KB - 1))
            if part == 1:
                ins.then_inc(s["gu_done"], 1)

        def turn(v, e):
            pe.wait_ge(s["h_ready"], v * EPG + (e + 1))
            if e == 1:
                pe.wait_ge(s["pt_ready"], v + 1)
            if e >= 2:
                pe.wait_ge(s["hxl_ready"], v * EPG + (e - 1))
            for j in range(2):
                ins = tr(psum[2 + e % 2][:, 128 * j:128 * j + 128], H[e % 2][:, 128 * j:128 * j + 128], ident)
            ins.then_inc(s["hx_done"], 1)

        def down(v, e):
            pe.wait_ge(s["lo_dn"], v * EPG + (e + 1))
            pe.wait_ge(s["hxl_ready"], v * EPG + (e + 1))
            w = k.shaped(LOW[:, place(2, e) % SLOTS, :], (2, 1024))
            for j in range(2):
                if j:
                    pe.wait_ge(s["lo_dn2"], v * EPG + (e + 1))
                for x, y in ((HXH, HIDN[e % 2]), (HXH, w), (HXL, HIDN[e % 2])):
                    for half in range(2):
                        ins = mm(psum[4 + half][:, :], x[e % 2][:, j, :], y[:, j, 512 * half:512 * half + 512],
                                 start=(e == 0 and j == 0 and x is HXH and y is not w), stop=(e == EPG - 1 and j == 1 and x is HXL))
            ins.then_inc(s["dn_done"], 1)

        def scatter(v, q):
            c, half = divmod(q, 2)
            if q < 2:
                pe.wait_ge(s["og_ready"], v * 2 + (half + 1))
            else:
                pe.wait_ge(s["y_added"], v * 6 + (q - 1))
            o = slice(512 * half, 512 * half + 512)
            mm(psum[6 + q % 2][0:L[c], :], PT[:, T0[c]:T0[c] + L[c]], OGH[:, o], start=True, stop=False)
            mm(psum[6 + q % 2][0:L[c], :], PT[:, T0[c]:T0[c] + L[c]], OGL[:, o], start=False, stop=True).then_inc(s["sc_done"], 1)

        def one_pass(p):
            gather(NG * p, range(8))
            gather_weights(NG * p)
            turn_places(NG * p)
            pe.wait_ge(s["xgl_ready"], 2 * NG * p + 2)
            v0, e0 = before(p)
            gate_up(v0, e0, 0)
            gate_up(v0, e0, 1)

            def one_group(v, more):
                for e in range(1, EPG):
                    gate_up(v, e, 0)
                    turn(v, e - 1)
                    gate_up(v, e, 1)
                    down(v, e - 1)
                    if more and e >= 4:
                        gather(v + 1, range(2 * (e - 4), 2 * (e - 4) + 2))
                if more:
                    gather_weights(v + 1)
                turn(v, EPG - 1)
                down(v, EPG - 1)
                if more:
                    pe.wait_ge(s["xgl_ready"], v * 2 + 4)
                    gate_up(v, EPG, 0)
                scatter(v, 0)
                scatter(v, 1)
                if more:
                    gate_up(v, EPG, 1)
                for q in range(2, 6):
                    scatter(v, q)
                if more:
                    turn_places(v + 1)
                    pe.wait_ge(s["y_added"], v * 6 + 6)
            groups(pe, p, one_group)
            pe.wait_ge(s["y_added"], 6 * NG * p + 6 * NG)
        passes(pe, one_pass)
    ctx.close()


def build(nc, i_, o_):
    with ExitStack() as ctx:
        k = Core(nc, ctx, i_, o_)
        front(k)
        delta(k)
        gla(k)
        merge(k)
        experts(k)


_INS = ['x_prompt', 'x_sample', 'state_delta', 'state_conv', 'state_gla', 'meta_tokens', 'norm_mix', 'w_in',
        'conv_w', 'a_log', 'dt_bias', 'norm_a', 'gla_gate_up', 'gla_gate_bias', 'norm_b', 'w_proj_a', 'w_proj_b',
        'w_out', 'norm_ffn', 'router_group_w', 'router_group_b', 'router_expert_w', 'router_expert_b',
        'expert_w_gate', 'expert_w_up', 'expert_w_down', 'norm_final']
_OUTS = {'y_p': (1, SEQ, D), 'y_s': (NB, TS, D), 'sd_p': (1, 1, HA, 128, 128), 'conv_p': (1, 1, CW - 1, CONV),
         'sg_p': (1, 1, HB, 128, 256), 'sd_s': (1, NB, HA, 128, 128), 'conv_s': (1, NB, CW - 1, CONV),
         'sg_s': (1, NB, HB, 128, 256)}


def kernel(**inputs):
    import numpy as _np
    import concourse.bacc as _bacc
    from concourse import mybir as _mybir
    from concourse.bass_utils import run_bass_kernel_spmd as _run

    nc = _bacc.Bacc("TRN2", target_bir_lowering=False, num_devices=1)
    arrays, ins, outs = {}, {}, {}
    for name in _INS:
        a = _np.ascontiguousarray(inputs[name])
        arrays[f"in_{name}"] = a
        ins[name] = nc.dram_tensor(f"in_{name}", a.shape, _mybir.dt.from_np(a.dtype), kind="ExternalInput").ap()
    for name, shape in _OUTS.items():
        outs[name] = nc.dram_tensor(f"out_{name}", shape, _mybir.dt.float32, kind="ExternalOutput").ap()
    build(nc, ins, outs)
    r = _run(nc, [arrays], core_ids=[0])
    return tuple(r.results[0][f"out_{name}"] for name in _OUTS)
```
